# Optimizing a Trainium2 kernel written in Bass

```python
import jax, jax.numpy as jnp
from jax import lax
import numpy as np

D_MODEL = 2048
BATCH = 1
SEQ = 512
DEPTH = 1

NORM_EPS = 1e-6
SSD_D_INNER = D_MODEL
SSD_HEAD_DIM = 64
SSD_N_HEADS = SSD_D_INNER // SSD_HEAD_DIM
SSD_D_STATE = 128
SSD_N_GROUPS = 8
SSD_CONV_WIDTH = 4
SSD_CONV_DIM = SSD_D_INNER + 2 * SSD_N_GROUPS * SSD_D_STATE
SSD_CHUNK = 128
HG_D = D_MODEL
HG_N_HEADS = 16
HG_K_DIM = HG_D // HG_N_HEADS
HG_V_DIM = HG_D // HG_N_HEADS
HG_KEY_TOTAL = HG_N_HEADS * HG_K_DIM
HG_VAL_TOTAL = HG_N_HEADS * HG_V_DIM
HG_CHUNK = 64
PEER_HEADS = 8
PEER_N_KEYS = 128
PEER_N_EXPERTS = PEER_N_KEYS * PEER_N_KEYS
PEER_TOPK = 16
PEER_D_QUERY = 256
PEER_D_HALF = PEER_D_QUERY // 2
PEER_TOKEN_BLOCK = 128
IN_SIZES = (SSD_D_INNER, SSD_CONV_DIM, SSD_N_HEADS, HG_KEY_TOTAL, HG_KEY_TOTAL, HG_VAL_TOTAL, HG_D, D_MODEL, D_MODEL)
IN_DIM = SSD_D_INNER + SSD_CONV_DIM + SSD_N_HEADS + 2 * HG_KEY_TOTAL + HG_VAL_TOTAL + HG_D + 2 * D_MODEL

kernel_name = 'hybrid_ssd_hgrn2_peer_block'

def _rms(x32):
    return x32 * lax.rsqrt(jnp.mean(jnp.square(x32), axis=-1, keepdims=True) + NORM_EPS)

def rmsnorm(x, w):
    return (_rms(x.astype(jnp.float32)) * w.astype(jnp.float32)).astype(x.dtype)

def group_rmsnorm(y32, w, groups):
    shp = y32.shape
    yg = _rms(y32.reshape(shp[:-1] + (groups, shp[-1] // groups)))
    return yg.reshape(shp) * w.astype(jnp.float32)

def causal_dwconv(u, w, b):
    k, ch = w.shape
    out = lax.conv_general_dilated(u, w[:, None, :], window_strides=(1,), padding=[(k - 1, 0)],
                                   dimension_numbers=('NWC', 'WIO', 'NWC'), feature_group_count=ch)
    return out + b

def segsum(a):
    t = a.shape[-1]
    aa = jnp.broadcast_to(a[..., :, None], a.shape + (t,))
    aa = jnp.where(jnp.tril(jnp.ones((t, t), dtype=bool), -1), aa, 0.0)
    cs = jnp.cumsum(aa, axis=-2)
    return jnp.where(jnp.tril(jnp.ones((t, t), dtype=bool), 0), cs, -jnp.inf)

def ssd_chunked(xdt, adt, bmat, cmat):
    b, l, h, p = xdt.shape
    g, n = bmat.shape[2], bmat.shape[3]
    r = h // g
    c, s = l // SSD_CHUNK, SSD_CHUNK
    xc = xdt.astype(jnp.float32).reshape(b, c, s, g, r, p)
    bc = bmat.astype(jnp.float32).reshape(b, c, s, g, n)
    cc = cmat.astype(jnp.float32).reshape(b, c, s, g, n)
    ac = adt.astype(jnp.float32).reshape(b, c, s, g, r).transpose(0, 3, 4, 1, 2)
    a_cum = jnp.cumsum(ac, axis=-1)
    lmat = jnp.exp(segsum(ac))
    cb = jnp.einsum('bclgn,bcsgn->bgcls', cc, bc)
    y_diag = jnp.einsum('bgrcls,bcsgrp->bclgrp', cb[:, :, None] * lmat, xc)
    decay_states = jnp.exp(a_cum[..., -1:] - a_cum)
    states = jnp.einsum('bcsgn,bgrcs,bcsgrp->bcgrpn', bc, decay_states, xc)
    states = jnp.concatenate([jnp.zeros_like(states[:, :1]), states], axis=1)
    chunk_decay = jnp.exp(segsum(jnp.pad(a_cum[..., -1], ((0, 0), (0, 0), (0, 0), (1, 0)))))
    states = jnp.einsum('bgrzc,bcgrpn->bzgrpn', chunk_decay, states)[:, :-1]
    y_off = jnp.einsum('bclgn,bcgrpn,bgrcl->bclgrp', cc, states, jnp.exp(a_cum))
    return (y_diag + y_off).reshape(b, l, h, p)

def hgrn2_chunked(q, k, v, log_f):
    b, l, h, dk = q.shape
    dv = v.shape[-1]
    c = l // HG_CHUNK

    def to_chunks(a):
        return a.astype(jnp.float32).reshape(b, c, HG_CHUNK, h, a.shape[-1]).transpose(1, 0, 3, 2, 4)

    causal = jnp.tril(jnp.ones((HG_CHUNK, HG_CHUNK), dtype=bool))[:, :, None]

    def step(state, inp):
        qc, kc, vc, gc = inp
        bcum = jnp.cumsum(gc, axis=2)
        diff = bcum[:, :, :, None, :] - bcum[:, :, None, :, :]
        decay = jnp.exp(jnp.where(causal, diff, -jnp.inf))
        scores = jnp.einsum('bhtk,bhsk,bhtsk->bhts', qc, kc, decay)
        o = (jnp.einsum('bhts,bhsv->bhtv', scores, vc)
             + jnp.einsum('bhtk,bhkv->bhtv', qc * jnp.exp(bcum), state))
        b_end = bcum[:, :, -1:, :]
        state = (jnp.exp(b_end[:, :, 0, :, None]) * state
                 + jnp.einsum('bhsk,bhsv->bhkv', kc * jnp.exp(b_end - bcum), vc))
        return state, o

    s0 = jnp.zeros((b, h, dk, dv), jnp.float32)
    _, o = lax.scan(step, s0, (to_chunks(q), to_chunks(k), to_chunks(v), to_chunks(log_f)))
    return o.transpose(1, 0, 3, 2, 4).reshape(b, l, h, dv)

def mixing_block(h, w_in, conv_w, conv_b, dt_bias, a_log, d_skip, ssd_norm_w, lb, hg_norm_w,
                 w_ssd_br, w_hg_br, w_out):
    bsz, seq, _ = h.shape
    f32 = jnp.float32
    split_at = [int(v) for v in np.cumsum(IN_SIZES)[:-1]]
    z, xbc, dt_raw, hq, hf, hi, hg, gate_s, gate_h = jnp.split(h @ w_in, split_at, axis=-1)
    xbc = jax.nn.silu(causal_dwconv(xbc, conv_w, conv_b))
    xs, bm, cm = jnp.split(xbc, [SSD_D_INNER, SSD_D_INNER + SSD_N_GROUPS * SSD_D_STATE], axis=-1)
    xs = xs.astype(f32).reshape(bsz, seq, SSD_N_HEADS, SSD_HEAD_DIM)
    bm = bm.reshape(bsz, seq, SSD_N_GROUPS, SSD_D_STATE)
    cm = cm.reshape(bsz, seq, SSD_N_GROUPS, SSD_D_STATE)
    dt = jax.nn.softplus(dt_raw.astype(f32) + dt_bias.astype(f32))
    a = -jnp.exp(a_log.astype(f32))
    y = ssd_chunked(xs * dt[..., None], a * dt, bm, cm) + d_skip.astype(f32)[:, None] * xs
    y = y.reshape(bsz, seq, SSD_D_INNER) * jax.nn.silu(z.astype(f32))
    y_ssd = group_rmsnorm(y, ssd_norm_w, SSD_N_GROUPS).astype(h.dtype)
    qh = jax.nn.silu(hq.astype(f32)).reshape(bsz, seq, HG_N_HEADS, HG_K_DIM)
    f = lb + (1.0 - lb) * jax.nn.sigmoid(hf.astype(f32))
    kh = (1.0 - f).reshape(bsz, seq, HG_N_HEADS, HG_K_DIM)
    log_f = jnp.log(f).reshape(bsz, seq, HG_N_HEADS, HG_K_DIM)
    vh = hi.reshape(bsz, seq, HG_N_HEADS, HG_V_DIM)
    o = hgrn2_chunked(qh, kh, vh, log_f)
    o = _rms(o) * hg_norm_w.astype(f32) * jax.nn.silu(hg.astype(f32).reshape(bsz, seq, HG_N_HEADS, HG_V_DIM))
    y_hg = o.reshape(bsz, seq, HG_D).astype(h.dtype)
    mix = jax.nn.sigmoid(gate_s) * (y_ssd @ w_ssd_br) + jax.nn.sigmoid(gate_h) * (y_hg @ w_hg_br)
    return mix @ w_out

def peer_ffn(h, w_q, sub_keys, u, v):
    bsz, seq, d = h.shape
    t = bsz * seq
    hf = h.reshape(t, d)
    q = (hf @ w_q).reshape(t, PEER_HEADS, 2, PEER_D_HALF)
    s = jnp.einsum('thpd,hpkd->thpk', q, sub_keys).astype(jnp.float32)
    s1, i1 = lax.top_k(s[:, :, 0], PEER_TOPK)
    s2, i2 = lax.top_k(s[:, :, 1], PEER_TOPK)
    kk = PEER_TOPK * PEER_TOPK
    cand_s = (s1[..., :, None] + s2[..., None, :]).reshape(t, PEER_HEADS, kk)
    cand_i = (i1[..., :, None] * PEER_N_KEYS + i2[..., None, :]).reshape(t, PEER_HEADS, kk)
    top_s, pos = lax.top_k(cand_s, PEER_TOPK)
    idx = jnp.take_along_axis(cand_i, pos, axis=-1)
    gate = jax.nn.softmax(top_s, axis=-1).astype(h.dtype)
    nb = t // PEER_TOKEN_BLOCK
    hk = PEER_HEADS * PEER_TOPK
    xb = hf.reshape(nb, PEER_TOKEN_BLOCK, d)
    ib = idx.reshape(nb, PEER_TOKEN_BLOCK, hk)
    gb = gate.reshape(nb, PEER_TOKEN_BLOCK, hk)

    def expert_block(args):
        xt, it, gt = args
        act = jax.nn.gelu(jnp.einsum('td,tkd->tk', xt, jnp.take(u, it, axis=0)), approximate=False)
        return jnp.einsum('tk,tkd->td', gt * act, jnp.take(v, it, axis=0))

    out = lax.map(expert_block, (xb, ib, gb))
    return out.reshape(bsz, seq, d)

def setup_inputs(seed: int = 0) -> dict:
    key = jax.random.key(seed)
    ks = jax.random.split(key, 24)
    f32 = jnp.float32
    nrm = lambda k, shp, sc: jax.random.normal(k, shp, f32) * sc
    dt0 = jnp.exp(jax.random.uniform(ks[5], (DEPTH, SSD_N_HEADS), f32, np.log(1e-3), np.log(1e-1)))
    return {
        'x': jax.random.normal(ks[0], (BATCH, SEQ, D_MODEL), f32),
        'norm_mix_w': 1.0 + nrm(ks[1], (DEPTH, D_MODEL), 0.02),
        'w_in': nrm(ks[2], (DEPTH, D_MODEL, IN_DIM), D_MODEL ** -0.5),
        'ssd_conv_w': nrm(ks[3], (DEPTH, SSD_CONV_WIDTH, SSD_CONV_DIM), SSD_CONV_WIDTH ** -0.5),
        'ssd_conv_b': nrm(ks[4], (DEPTH, SSD_CONV_DIM), 0.02),
        'ssd_dt_bias': dt0 + jnp.log(-jnp.expm1(-dt0)),
        'ssd_a_log': jnp.log(jax.random.uniform(ks[6], (DEPTH, SSD_N_HEADS), f32, 1.0, 16.0)),
        'ssd_d': 1.0 + nrm(ks[7], (DEPTH, SSD_N_HEADS), 0.1),
        'ssd_norm_w': 1.0 + nrm(ks[8], (DEPTH, SSD_D_INNER), 0.02),
        'hg_lb': nrm(ks[9], (DEPTH + 1, HG_KEY_TOTAL), 0.1),
        'hg_norm_w': 1.0 + nrm(ks[10], (DEPTH, HG_V_DIM), 0.02),
        'w_ssd_br': nrm(ks[11], (DEPTH, SSD_D_INNER, D_MODEL), SSD_D_INNER ** -0.5),
        'w_hg_br': nrm(ks[12], (DEPTH, HG_D, D_MODEL), HG_D ** -0.5),
        'w_out': nrm(ks[13], (DEPTH, D_MODEL, D_MODEL), D_MODEL ** -0.5),
        'norm_ffn_w': 1.0 + nrm(ks[14], (DEPTH, D_MODEL), 0.02),
        'peer_w_q': nrm(ks[15], (DEPTH, D_MODEL, PEER_HEADS * PEER_D_QUERY), D_MODEL ** -0.5),
        'peer_sub_keys': nrm(ks[16], (DEPTH, PEER_HEADS, 2, PEER_N_KEYS, PEER_D_HALF), PEER_D_HALF ** -0.5),
        'peer_u': nrm(ks[17], (DEPTH, PEER_N_EXPERTS, D_MODEL), D_MODEL ** -0.5),
        'peer_v': nrm(ks[18], (DEPTH, PEER_N_EXPERTS, D_MODEL), PEER_HEADS ** -0.5),
        'final_norm_w': 1.0 + nrm(ks[19], (D_MODEL,), 0.02),
    }

def reference(x, norm_mix_w, w_in, ssd_conv_w, ssd_conv_b, ssd_dt_bias, ssd_a_log, ssd_d, ssd_norm_w,
              hg_lb, hg_norm_w, w_ssd_br, w_hg_br, w_out, norm_ffn_w, peer_w_q, peer_sub_keys,
              peer_u, peer_v, final_norm_w):
    lb_all = jnp.cumsum(jax.nn.softmax(hg_lb.astype(jnp.float32), axis=0), axis=0)
    for layer in range(DEPTH):
        h = rmsnorm(x, norm_mix_w[layer])
        x = x + mixing_block(h, w_in[layer], ssd_conv_w[layer], ssd_conv_b[layer], ssd_dt_bias[layer],
                             ssd_a_log[layer], ssd_d[layer], ssd_norm_w[layer], lb_all[layer],
                             hg_norm_w[layer], w_ssd_br[layer], w_hg_br[layer], w_out[layer])
        h = rmsnorm(x, norm_ffn_w[layer])
        x = x + peer_ffn(h, peer_w_q[layer], peer_sub_keys[layer], peer_u[layer], peer_v[layer])
    return rmsnorm(x, final_norm_w)


_drawn_inputs = setup_inputs


def setup_inputs(seed=0):
    import zlib

    import numpy as np

    out = dict(_drawn_inputs(seed))
    spreads = {}
    factors = {'ssd_norm_w': 31.002,
     'hg_lb': 5.271,
     'hg_norm_w': 44.831,
     'final_norm_w': 24.684,
     'norm_ffn_w': 16.513}
    for name, (base, spread) in spreads.items():
        noise = np.random.default_rng([zlib.crc32(name.encode()), seed]).standard_normal(out[name].shape)
        drawn = base * np.exp(spread * noise) if base else spread * noise
        out[name] = __import__('jax').numpy.asarray(drawn.astype(out[name].dtype))
    for name, factor in factors.items():
        out[name] = (out[name] * factor).astype(out[name].dtype)
    return out
```

```python
from collections import namedtuple
from contextlib import ExitStack, contextmanager

import numpy as np

import concourse.bass as bass
from concourse import mybir

F32 = mybir.dt.float32
F32R = mybir.dt.float32r
U32 = mybir.dt.uint32
ALU = mybir.AluOpType
ACT = mybir.ActivationFunctionType
AX_X = mybir.AxisListType.X
EXP_LN_SET = "natural_log_exp_and_others"

P = 128
T = 512
D = 2048
KT = D // P
CH = 128
NC = T // CH
EPS = 1e-6

SSD_GROUPS = 8
SSD_HEADS = 32
HPG = SSD_HEADS // SSD_GROUPS
HD = 64
SSD_TILES = 6
CONV = 4

HG_HEADS = 16
HG_TILES = 4
LEVELS = 7
HALVES = [CH >> (l + 1) for l in range(LEVELS)]

PEER_HEADS = 8
KEYS = 128
TOPK = 16
HK = PEER_HEADS * TOPK
GT = 128
NEG = -3.0e38

ts = bass.ts
ds = bass.ds


def one(ap):
    return ap.rearrange("a p n -> (a p) n")


class Chain:

    def __init__(self, engine, done):
        self.engine, self.done = engine, done
        self.start, self.at, self.per, self.turn = 0, 0, 0, 0

    def after(self, ins):
        self.at += 1
        ins.then_inc(self.done, 1)
        self.engine.wait_ge(self.done, self.turn * self.per + (self.start + self.at))

    def enter(self, turn, per):
        self.start, self.at, self.per, self.turn = self.start + self.at, 0, per, turn

    def leave(self, turns):
        assert self.at == self.per, (self.at, self.per)
        self.start, self.at, self.per, self.turn = self.start + turns * self.per, 0, 0, 0


Ring = namedtuple("Ring", "raw high low landed high_ready low_ready used")


@contextmanager
def semaphores(nc, stage):
    with ExitStack() as ctx:
        made = []

        def sem(name):
            made.append(ctx.enter_context(nc.semaphore(f"{stage}_{name}")))
            return made[-1]

        yield sem
        with nc.Block() as block:
            @block.sync
            def _(sp):
                for s in made:
                    sp.sem_clear(s)


def make_ring(nc, ctx, name, sem):
    sb = lambda n, dt: ctx.enter_context(nc.sbuf_tensor(f"{name}_{n}", [P, 2, D], dt))
    return Ring(sb("raw", F32), sb("high", F32R), sb("low", F32R), [sem("landed0"), sem("landed1")],
                sem("high_ready"), sem("low_ready"), sem("used"))


def load_tile(sp, ring, slot, tile, n):
    if n is not None:
        sp.wait_ge(ring.low_ready, n - 1)
    sp.dma_start(ring.raw[:, slot], tile).then_inc(ring.landed[slot], 16)


def split_high(nc, act, ring, slot, n, pair):
    act.wait_ge(ring.landed[slot], 16 * pair + 16)
    act.wait_ge(ring.used, n + 1)
    nc.scalar.activation(ring.high[:, slot], ring.raw[:, slot], ACT.Copy).then_inc(ring.high_ready, 1)


def split_low_all(nc, pool, ring, tiles):
    with pool.Fori(0, tiles // 2) as i:
        for slot in range(2):
            pool.wait_ge(ring.high_ready, 2 * i + (slot + 1))
            nc.gpsimd.tensor_tensor(ring.low[:, slot], ring.raw[:, slot], ring.high[:, slot].bitcast(F32),
                                    ALU.subtract).then_inc(ring.low_ready, 1)


def product(nc, out, high, low, x_high, x_low, steps=range(KT)):
    for k in steps:
        m = slice(k * P, (k + 1) * P)
        nc.tensor.matmul(out, high[:, m], x_high[:, k], start=(k == 0), stop=False, skip_group_check=True)
        nc.tensor.matmul(out, high[:, m], x_low[:, k], start=False, stop=False, skip_group_check=True)
        last = nc.tensor.matmul(out, low[:, m], x_high[:, k], start=False, stop=(k == KT - 1),
                                skip_group_check=True)
    return last



def norm_stage(nc, name, src, weight, work, ones, eps, load=None, split=None, store=None):
    with ExitStack() as ctx:
        sem = ctx.enter_context(semaphores(nc, name))
        mean = ctx.enter_context(nc.psum_tensor(f"{name}_mean", [P, T], F32))
        rstd = ctx.enter_context(nc.sbuf_tensor(f"{name}_rstd", [P, T], F32))
        landed, squared, summed, rooted, normed, high_done, low_done, stored, act_done = (
            sem(n) for n in ("landed", "squared", "summed", "rooted", "normed", "high_done", "low_done",
                             "stored", "act_done"))
        QUARTER = KT // 4
        block = ctx.enter_context(nc.Block())

        @block.sync
        def _(sp):
            if load is not None:
                for q in range(4):
                    sl = slice(q * QUARTER, (q + 1) * QUARTER)
                    sp.dma_start(src[:, sl], load[:, sl]).then_inc(landed, 16)
            if store is not None:
                for k in range(KT):
                    sp.wait_ge(normed, k + 1)
                    sp.dma_start(store[:, k], work[:, k]).then_inc(stored, 16)
                sp.wait_ge(stored, 16 * KT)

        @block.scalar
        def _(act):
            nc.scalar.preload_act_table_set(EXP_LN_SET)
            if load is not None:
                act.wait_ge(landed, 64)
            for q in range(4):
                sl = slice(q * QUARTER, (q + 1) * QUARTER)
                nc.scalar.activation(work[:, sl], src[:, sl], ACT.Square).then_inc(squared, 1)
            act.wait_ge(summed, 1)
            nc.scalar.activation(rstd[:], mean[:], ACT.Ln, bias=eps, scale=1.0 / D).then_inc(act_done, 1)
            act.wait_ge(act_done, 1)
            nc.scalar.activation(rstd[:], rstd[:], ACT.Exp, scale=-0.5).then_inc(rooted, 1)
            if split is not None:
                for k in range(KT):
                    act.wait_ge(normed, k + 1)
                    nc.scalar.activation(split[0][:, k], work[:, k], ACT.Copy).then_inc(high_done, 1)

        @block.tensor
        def _(pe):
            for k in range(KT):
                pe.wait_ge(squared, k // QUARTER + 1)
                last = nc.tensor.matmul(mean[:], ones, work[:, k], start=(k == 0), stop=(k == KT - 1))
            last.then_inc(summed, 1)

        @block.vector
        def _(dve):
            dve.wait_ge(rooted, 1)
            for k in range(KT):
                nc.vector.scalar_tensor_tensor(work[:, k], src[:, k], weight[:, k:k + 1], rstd[:],
                                               ALU.mult, ALU.mult).then_inc(normed, 1)

        @block.gpsimd
        def _(pool):
            if split is not None:
                for k in range(KT):
                    pool.wait_ge(high_done, k + 1)
                    nc.gpsimd.tensor_tensor(split[1][:, k], work[:, k], split[0][:, k].bitcast(F32),
                                            ALU.subtract).then_inc(low_done, 1)



def ssd_stage(nc, dram, h, const, y_out):
    G = SSD_GROUPS
    with ExitStack() as ctx:
        sb = lambda n, s, dt=F32: ctx.enter_context(nc.sbuf_tensor(f"sb_ssd_{n}", s, dt))
        ps = lambda n, s: ctx.enter_context(nc.psum_tensor(f"ssd_{n}", s, F32))
        sem = ctx.enter_context(semaphores(nc, "ssd"))
        ring = make_ring(nc, ctx, "ssd", sem)
        W4 = HPG * CH
        conv = sb("conv", [P, SSD_TILES, T])
        sig = sb("sig", [P, SSD_TILES, T])
        act_in = sb("act_in", [P, SSD_TILES, T])
        expo = sb("expo", [P, 2, T])
        xdt = sb("xdt", [P, NC, HPG * HD])
        b_tok = sb("b_tok", [P, NC, P])
        steps = sb("steps", [P, HPG, CH])
        decay = sb("decay", [P, HPG, CH])
        decay0 = sb("decay0", [P, HPG, CH])
        scores = sb("scores", [P, CH])
        mixed = sb("mixed", [P, HPG, CH])
        c_dec = sb("c_dec", [P, HPG, CH])
        x_dec = sb("x_dec", [P, HPG, HD])
        chunk_dec = sb("chunk_dec", [P, HPG])
        state = sb("state", [P, HPG, HD])
        y = sb("y", [P, 2, T])
        y_sq = sb("y_sq", [P, 2, T])
        rstd = sb("rstd", [P, T])
        y_norm = sb("y_norm", [P, 2, T])
        wdt = sb("wdt", [P, KT, SSD_HEADS])
        wdt_high = sb("wdt_high", [P, KT, SSD_HEADS], F32R)
        wdt_low = sb("wdt_low", [P, KT, SSD_HEADS], F32R)
        dt_bias = sb("dt_bias", [P, SSD_HEADS])
        a_log = sb("a_log", [P, SSD_HEADS])
        dt = sb("dt", [P, NC, SSD_HEADS])
        adt = sb("adt", [P, NC, SSD_HEADS])
        dtx = sb("dtx", [P, NC, SSD_HEADS])
        dte = sb("dte", [P, NC, SSD_HEADS])
        dtw = sb("dtw", [P, NC, SSD_HEADS])
        dtl = sb("dtl", [P, NC, SSD_HEADS])
        conv_w = sb("conv_w", [P, G * 4 * (CONV + 1)])
        d_col = sb("d_col", [P, KT])
        norm_w = sb("norm_w", [P, KT])

        acc = [ps(f"acc{i}", [P, T]) for i in range(2)]
        ps_decay = ps("ps_decay", [P, W4])
        ps_decay0 = ps("ps_decay0", [P, W4])
        ps_turn = ps("ps_turn", [P, T])
        ps_state = ps("ps_state", [P, HPG * HD])
        ps_y = [ps(f"ps_y{i}", [P, T]) for i in range(2)]

        consts = sem("consts")
        dt_split, dt_low, dt_sum, dt_exp, dt_ln = (sem(n) for n in ("dt_split", "dt_low", "dt_sum", "dt_exp", "dt_ln"))
        acc_read = sem("acc_read")
        exp_done = sem("exp_done")
        sig_done = sem("sig_done")
        in_ready = sem("in_ready")
        turned = sem("turned")
        turned_read = sem("turned_read")
        steps_ready = sem("steps_ready")
        a_done = sem("a_done")
        decayed = sem("decayed")
        mixed_ready = sem("mixed_ready")
        b_done = sem("b_done")
        state_ready = sem("state_ready")
        y_read = sem("y_read")
        gated = sem("gated")
        squared = sem("squared")
        summed = sem("summed")
        rooted = sem("rooted")
        y_ready = sem("y_ready")
        y_stored = sem("y_stored")
        act_done = sem("act_done")
        vec_done = sem("vec_done")
        block = ctx.enter_context(nc.Block())

        LAST = G + 2
        @block.sync
        def _(sp):
            for dst, src in ((wdt, dram["w_dt"]), (dt_bias, dram["dt_bias"]), (a_log, dram["a_log"]),
                             (conv_w, dram["conv_w"])):
                sp.dma_start(dst[:], src).then_inc(consts, 16)
            for dst, src in ((d_col, dram["ssd_d"]), (norm_w, dram["ssd_norm_w"])):
                sp.dma_start(dst[:], src).then_inc(y_stored, 16)

            def store(f):
                sp.wait_ge(y_ready, f + 1)
                for t in range(2):
                    sp.dma_start(one(y_out[ds(2 * f + t, 1)]), y_norm[:, t]).then_inc(y_stored, 16)

            for s in range(2):
                load_tile(sp, ring, s, dram["w_ssd"][s], None)
            for s in range(2, SSD_TILES):
                load_tile(sp, ring, s % 2, dram["w_ssd"][s], s)
            for s in range(SSD_TILES):
                load_tile(sp, ring, s % 2, dram["w_ssd"][SSD_TILES + s], SSD_TILES + s)
            with sp.Fori(2, G) as u:
                for s in range(SSD_TILES):
                    n = SSD_TILES * u + s
                    load_tile(sp, ring, s % 2, one(dram["w_ssd"][ds(n, 1)]), n)
                store(u - 2)
            store(G - 2)
            store(G - 1)
            sp.wait_ge(y_stored, 32 + 32 * G)

        @block.gpsimd
        def _(pool):
            split_low_all(nc, pool, ring, G * SSD_TILES)

        @block.scalar
        def _(act):
            chain = Chain(act, act_done)
            nc.scalar.preload_act_table_set(EXP_LN_SET)
            act.wait_ge(consts, 64)
            nc.scalar.activation(wdt_high[:], wdt[:], ACT.Copy).then_inc(dt_split, 1)
            split_high(nc, act, ring, 0, 0, 0)
            chain.after(nc.scalar.activation(a_log[:], a_log[:], ACT.Exp))
            act.wait_ge(dt_sum, 1)
            nc.scalar.activation(dte[:], dte[:], ACT.Exp, scale=-1.0).then_inc(dt_exp, 1)
            act.wait_ge(dt_ln, 1)
            nc.scalar.activation(dtl[:], dtw[:], ACT.Ln).then_inc(dt_exp, 1)

            def body(u, proj, comp, fin, ahead=True):
                p, f = u - 1, u - 2
                for s in range(SSD_TILES):
                    if proj and (ahead or s < SSD_TILES - 1):
                        split_high(nc, act, ring, (s + 1) % 2, SSD_TILES * u + s + 1, 3 * u + (s + 1) // 2)
                    if s == 0 and fin:
                        act.wait_ge(gated, f + 1)
                        nc.scalar.activation(y_sq[:], y[:], ACT.Square).then_inc(squared, 1)
                    if proj:
                        if s < 4:
                            act.wait_ge(acc_read, SSD_TILES * u + s + 3)
                        else:
                            act.wait_ge(ring.used, SSD_TILES * u + s + 3)
                        act.wait_ge(sig_done, SSD_TILES * u + s + 1)
                        nc.scalar.activation(expo[:, s % 2], conv[:, s] if s < 4 else acc[s % 2][:],
                                             ACT.Exp, scale=-1.0).then_inc(exp_done, 1)
                    if s == 1 and fin:
                        act.wait_ge(summed, f + 1)
                        chain.after(nc.scalar.activation(rstd[:], ps_decay[:], ACT.Ln, bias=const["eps"],
                                                         scale=1.0 / (2 * P)))
                        nc.scalar.activation(rstd[:], rstd[:], ACT.Exp, scale=-0.5).then_inc(rooted, 1)
                    if s >= 2 and comp:
                        act.wait_ge(a_done, NC * p + s - 1)
                        nc.scalar.activation(decay[:].rearrange("p h l -> p (h l)"), ps_decay[:], ACT.Exp)
                        nc.scalar.activation(decay0[:].rearrange("p h l -> p (h l)"), ps_decay0[:],
                                             ACT.Exp).then_inc(decayed, 1)

            body(0, True, False, False)
            body(1, True, True, False)
            with act.Fori(2, G - 1) as u:
                chain.enter(u - 2, 1)
                body(u, True, True, True)
            chain.leave(G - 3)
            body(G - 1, True, True, True, ahead=False)
            body(G, False, True, True)
            body(G + 1, False, False, True)

        @block.tensor
        def _(pe):
            nc.tensor.nop().then_inc(ring.used, 2)
            pe.wait_ge(dt_low, 1)
            for c in range(NC):
                for k in range(KT):
                    tok = slice(c * CH, (c + 1) * CH)
                    o = ps_turn[:, c * SSD_HEADS:(c + 1) * SSD_HEADS]
                    nc.tensor.matmul(o, h[0][:, k, tok], wdt_high[:, k], start=(k == 0), stop=False,
                                     skip_group_check=True)
                    nc.tensor.matmul(o, h[1][:, k, tok], wdt_high[:, k], start=False, stop=False,
                                     skip_group_check=True)
                    last = nc.tensor.matmul(o, h[0][:, k, tok], wdt_low[:, k], start=False,
                                            stop=(k == KT - 1), skip_group_check=True)
            last.then_inc(dt_low, 1)

            def turn(dst, src, done):
                for c in range(NC):
                    last = nc.tensor.transpose(dst[:, c * P:(c + 1) * P], src[:, c * CH:(c + 1) * CH],
                                               const["ident"])
                last.then_inc(done, 1)

            def part_a(p, c):
                pe.wait_ge(steps_ready, NC * p + c + 1)
                pe.wait_ge(decayed, NC * p + c + 1)
                rhs = steps[:].rearrange("p h l -> p (h l)")
                nc.tensor.matmul(ps_decay[:], const["later"], rhs, start=True, stop=True)
                nc.tensor.matmul(ps_decay0[:], const["ones"], rhs, start=True, stop=True)
                tok = slice(c * CH, (c + 1) * CH)
                nc.tensor.matmul(ps_turn[:, 0:CH], act_in[:, 2, tok], act_in[:, 3, tok],
                                 start=True, stop=True).then_inc(a_done, 1)

            def part_b(p, c):
                pe.wait_ge(mixed_ready, NC * p + c + 1)
                if c == 0:
                    pe.wait_ge(y_read, p + 1)
                else:
                    pe.wait_ge(state_ready, (NC - 1) * p + c)
                for head in range(HPG):
                    part = slice(HD * (head % 2), HD * (head % 2) + HD)
                    o = ps_y[head // 2][part, c * CH:(c + 1) * CH]
                    last = nc.tensor.matmul(o, xdt[:, c, head * HD:(head + 1) * HD], mixed[:, head],
                                            start=True, stop=(c == 0), skip_group_check=True)
                    if c > 0:
                        last = nc.tensor.matmul(o, state[:, head], c_dec[:, head], start=False, stop=True,
                                                skip_group_check=True)
                if c < NC - 1:
                    last = nc.tensor.matmul(ps_state[:], b_tok[:, c], x_dec[:].rearrange("p h d -> p (h d)"),
                                            start=True, stop=True)
                last.then_inc(b_done, 1)

            def body(u, proj, comp, fin):
                p, f = u - 1, u - 2
                for s in range(SSD_TILES):
                    n = SSD_TILES * u + s
                    if proj:
                        pe.wait_ge(ring.low_ready, n + 1)
                        pe.wait_ge(acc_read, n + 1)
                        product(nc, acc[s % 2][:], ring.high[:, s % 2], ring.low[:, s % 2],
                                h[0], h[1]).then_inc(ring.used, 1)
                    if s == 0:
                        if fin:
                            part_b(f, NC - 1)
                        if comp:
                            pe.wait_ge(in_ready, p + 1)
                            turn(ps_turn, act_in[:, 0], turned)
                    if s == 1:
                        if fin:
                            pe.wait_ge(squared, f + 1)
                            pe.wait_ge(decayed, NC * f + NC + 1)
                            for t in range(2):
                                last = nc.tensor.matmul(ps_decay[:], const["ones"], y_sq[:, t],
                                                        start=(t == 0), stop=(t == 1))
                            last.then_inc(summed, 1)
                        if comp:
                            pe.wait_ge(turned_read, 3 * p + 1)
                            turn(ps_turn, act_in[:, 1], turned)
                    if comp:
                        if s == 2:
                            pe.wait_ge(turned_read, 3 * p + 2)
                            turn(ps_turn, act_in[:, 2], turned)
                            pe.wait_ge(turned_read, 3 * p + 3)
                            pe.wait_ge(rooted, p + 1)
                            part_a(p, 0)
                        if s > 2:
                            part_b(p, s - 3)
                            part_a(p, s - 2)

            body(0, True, False, False)
            body(1, True, True, False)
            with pe.Fori(2, G) as u:
                body(u, True, True, True)
            body(G, False, True, True)
            body(G + 1, False, False, True)

        @block.vector
        def _(dve):
            chain = Chain(dve, vec_done)
            v = nc.vector
            v.nop().then_inc(acc_read, 2)
            v.nop().then_inc(sig_done, 2)
            v.nop().then_inc(decayed, 1)
            v.nop().then_inc(y_read, 1)
            v.nop().then_inc(rooted, 1)
            dve.wait_ge(dt_split, 1)
            v.tensor_tensor(wdt_low[:], wdt[:], wdt_high[:].bitcast(F32), ALU.subtract).then_inc(dt_low, 1)
            dve.wait_ge(dt_low, 2)
            dve.wait_ge(consts, 64)
            chain.after(v.tensor_tensor(dtx[:], ps_turn[:, 0:NC * SSD_HEADS].rearrange("p (c h) -> p c h", c=NC),
                                        dt_bias[:].unsqueeze(1).to_broadcast([P, NC, SSD_HEADS]), ALU.add))
            chain.after(v.tensor_scalar(dte[:], dtx[:], -1.0, None, ALU.mult))
            v.tensor_tensor(dte[:], dte[:], dtx[:], ALU.max).then_inc(dt_sum, 1)
            dve.wait_ge(dt_exp, 1)
            v.tensor_scalar(dtw[:], dte[:], 1.0, None, ALU.add).then_inc(dt_ln, 1)
            dve.wait_ge(dt_ln, 1)
            chain.after(v.tensor_scalar(dt[:], dtw[:], -1.0, None, ALU.add))
            chain.after(v.tensor_tensor(dte[:], dte[:], dt[:], ALU.subtract))
            dve.wait_ge(dt_exp, 2)
            chain.after(v.reciprocal(dtw[:], dtw[:]))
            chain.after(v.tensor_tensor(dte[:], dte[:], dtw[:], ALU.mult))
            chain.after(v.tensor_tensor(dtl[:], dtl[:], dte[:], ALU.add))
            chain.after(v.scalar_tensor_tensor(dt[:], dtx[:], 0.0, dtl[:], ALU.max, ALU.add))
            chain.after(v.scalar_tensor_tensor(adt[:], dt[:], -1.0,
                                               a_log[:].unsqueeze(1).to_broadcast([P, NC, SSD_HEADS]),
                                               ALU.mult, ALU.mult))
            dve.wait_ge(y_stored, 32)

            def convolve(u, s):
                src, dst = acc[s % 2], conv[:, s]
                w = lambda j: conv_w[:, ds(u * 4 * (CONV + 1) + s * (CONV + 1) + j, 1)]
                dve.wait_ge(ring.used, SSD_TILES * u + s + 3)
                chain.after(v.tensor_scalar(dst, src[:], w(CONV - 1), w(CONV), ALU.mult, ALU.add))
                for back in range(1, CONV):
                    ins = v.scalar_tensor_tensor(dst[:, back:], src[:, :T - back], w(CONV - 1 - back),
                                                 dst[:, back:], ALU.mult, ALU.add)
                    if back < CONV - 1:
                        chain.after(ins)
                ins.then_inc(acc_read, 1)

            def sigmoid(u, s):
                dve.wait_ge(exp_done, SSD_TILES * u + s + 1)
                chain.after(v.tensor_scalar(sig[:, s], expo[:, s % 2], 1.0, None, ALU.add))
                v.reciprocal(sig[:, s], sig[:, s]).then_inc(sig_done, 1)

            def take_z(u, s):
                dve.wait_ge(exp_done, SSD_TILES * u + s + 1)
                v.tensor_copy(conv[:, s], acc[s % 2][:]).then_inc(acc_read, 1)

            def take_x(p, t):
                dve.wait_ge(turned, 3 * p + t + 1)
                v.tensor_tensor(xdt[:, :, t * P:(t + 1) * P].rearrange("p c (h d) -> p c h d", h=2),
                                ps_turn[:].rearrange("p (c h d) -> p c h d", c=NC, h=2),
                                dt[:, :, ds(HPG * p + 2 * t, 2)].unsqueeze(3).to_broadcast([P, NC, 2, HD]),
                                ALU.mult).then_inc(turned_read, 1)

            def make_steps(p, c):
                v.tensor_tensor(steps[:], const["upto"].unsqueeze(1).to_broadcast([P, HPG, CH]),
                                adt[:, c, ds(HPG * p, HPG)].unsqueeze(2).to_broadcast([P, HPG, CH]),
                                ALU.mult).then_inc(steps_ready, 1)

            def next_state(p, c):
                dve.wait_ge(b_done, NC * p + c + 1)
                new = ps_state[:].rearrange("p (h d) -> p h d", h=HPG)
                if c == 0:
                    v.tensor_copy(state[:], new).then_inc(state_ready, 1)
                else:
                    chain.after(v.tensor_tensor(state[:], state[:],
                                                chunk_dec[:].unsqueeze(2).to_broadcast([P, HPG, HD]), ALU.mult))
                    v.tensor_tensor(state[:], state[:], new, ALU.add).then_inc(state_ready, 1)

            def mix(p, c):
                dve.wait_ge(decayed, NC * p + c + 2)
                if c > 0:
                    dve.wait_ge(mixed_ready, NC * p + c)
                chain.after(v.tensor_tensor(scores[:], ps_turn[:, 0:CH], const["upto"], ALU.mult))
                v.tensor_tensor(mixed[:], decay[:], scores[:].unsqueeze(1).to_broadcast([P, HPG, CH]), ALU.mult)
                if c < NC - 1:
                    v.tensor_tensor(x_dec[:], xdt[:, c].rearrange("p (h d) -> p h d", h=HPG),
                                    decay[:, :, CH - 1:CH].to_broadcast([P, HPG, HD]), ALU.mult)
                    v.tensor_copy(chunk_dec[:], decay0[:, :, CH - 1])
                v.tensor_tensor(c_dec[:], decay0[:],
                                act_in[:, 3, c * CH:(c + 1) * CH].unsqueeze(1).to_broadcast([P, HPG, CH]),
                                ALU.mult).then_inc(mixed_ready, 1)

            def body(u, proj, comp, fin):
                p, f = u - 1, u - 2
                for s in range(SSD_TILES):
                    if s == 0:
                        if fin:
                            dve.wait_ge(b_done, NC * f + NC)
                            for t in range(2):
                                ins = v.scalar_tensor_tensor(y[:, t], act_in[:, t], d_col[:, ds(2 * f + t, 1)],
                                                             ps_y[t][:], ALU.mult, ALU.add)
                            ins.then_inc(y_read, 1)
                            dve.wait_ge(y_read, f + 2)
                            v.tensor_tensor(y[:], y[:], act_in[:, 4:6], ALU.mult).then_inc(gated, 1)
                        if comp:
                            dve.wait_ge(sig_done, SSD_TILES * p + SSD_TILES + 2)
                            if fin:
                                dve.wait_ge(gated, f + 1)
                            v.tensor_tensor(act_in[:], conv[:], sig[:], ALU.mult).then_inc(in_ready, 1)
                            dve.wait_ge(in_ready, p + 1)
                        if proj:
                            convolve(u, 0)
                        if comp:
                            take_x(p, 0)
                            make_steps(p, 0)
                    if s == 1:
                        if proj:
                            convolve(u, 1)
                            sigmoid(u, 0)
                        if comp:
                            take_x(p, 1)
                        if fin:
                            dve.wait_ge(rooted, f + 2)
                            dve.wait_ge(y_stored, 32 * f + 32)
                            for t in range(2):
                                ins = v.scalar_tensor_tensor(y_norm[:, t], y[:, t], norm_w[:, ds(2 * f + t, 1)],
                                                             rstd[:], ALU.mult, ALU.mult)
                            ins.then_inc(y_ready, 1)
                    if s == 2:
                        if proj:
                            convolve(u, 2)
                            sigmoid(u, 1)
                        if comp:
                            dve.wait_ge(turned, 3 * p + 3)
                            v.tensor_copy(b_tok[:].rearrange("p c n -> p (c n)"), ps_turn[:]).then_inc(turned_read, 1)
                            mix(p, 0)
                            make_steps(p, 1)
                    if s >= 3:
                        if proj:
                            sigmoid(u, s - 1)
                            if s == 3:
                                convolve(u, s)
                            else:
                                take_z(u, s)
                        if comp:
                            next_state(p, s - 3)
                            mix(p, s - 2)
                            if s < SSD_TILES - 1:
                                make_steps(p, s - 1)
                if proj:
                    sigmoid(u, SSD_TILES - 1)

            body(0, True, False, False)
            body(1, True, True, False)
            with dve.Fori(2, G) as u:
                chain.enter(u - 2, 4 * 3 + 6 + 4 + 2)
                body(u, True, True, True)
            chain.leave(G - 2)
            body(G, False, True, True)
            body(G + 1, False, False, True)



def hg_stage(nc, dram, h, const, y_out):
    H = HG_HEADS
    L7, L8, LK, LQ = LEVELS, LEVELS + 1, LEVELS + 2, LEVELS + 3
    with ExitStack() as ctx:
        sb = lambda n, s, dt=F32: ctx.enter_context(nc.sbuf_tensor(f"sb_hg_{n}", s, dt))
        ps = lambda n, s: ctx.enter_context(nc.psum_tensor(f"hg_{n}", s, F32))
        sem = ctx.enter_context(semaphores(nc, "hg"))
        ring = make_ring(nc, ctx, "hg", sem)
        mask = sb("mask", [P, LEVELS + 1, CH])
        lb = sb("lb", [P, 2, KT])
        lb_in = sb("lb_in", [P, 2, KT])
        lb_max = sb("lb_max", [P, KT])
        norm_w = sb("norm_w", [P, 1])
        f = sb("f", [P, T])
        k = sb("k", [P, T])
        q = sb("q", [P, T])
        v = sb("v", [P, T])
        og = sb("og", [P, T])
        sg = sb("sg", [P, T])
        b = sb("b", [P, T])
        lev = sb("lev", [P, LEVELS + 4, T])
        qe = sb("qe", [P, T])
        k_end = sb("k_end", [P, NC])
        v_tok = sb("v_tok", [P, NC, P])
        k_tok = sb("k_tok", [P, NC, P])
        masked = sb("masked", [P, LEVELS + 1, CH])
        probs = sb("probs", [P, 2, CH])
        state = sb("state", [P, P])
        o_sq = sb("o_sq", [P, T])
        rstd = sb("rstd", [P, T])
        o_norm = sb("o_norm", [P, T])

        acc = [ps(f"acc{i}", [P, T]) for i in range(2)]
        ps_lev = ps("ps_lev", [P, LEVELS + 1, CH])
        ps_o = ps("ps_o", [P, T])
        ps_state = ps("ps_state", [P, P])
        ps_v = ps("ps_v", [P, T])
        ps_k = ps("ps_k", [P, T])

        consts = sem("consts")
        lb_step = sem("lb_step")
        acc_read = sem("acc_read")
        f_exp, q_exp, g_exp, f_ready, f_log, b_ready = (
            sem(n) for n in ("f_exp", "q_exp", "g_exp", "f_ready", "f_log", "b_ready"))
        turned = sem("turned")
        turned_read = sem("turned_read")
        lev_diff = sem("lev_diff")
        lev_exp = sem("lev_exp")
        lev_ready = sem("lev_ready")
        a_done = sem("a_done")
        a_read = sem("a_read")
        probs_ready = sem("probs_ready")
        b_done = sem("b_done")
        state_ready = sem("state_ready")
        squared, summed, rooted = sem("squared"), sem("summed"), sem("rooted")
        o_ready = sem("o_ready")
        o_stored = sem("o_stored")
        act_done, vec_done = sem("act_done"), sem("vec_done")
        block = ctx.enter_context(nc.Block())

        @block.sync
        def _(sp):
            sp.dma_start(mask[:], dram["level_mask"]).then_inc(consts, 16)
            sp.dma_start(lb_in[:], dram["hg_lb"]).then_inc(consts, 16)
            sp.dma_start(norm_w[:], dram["hg_norm_w"]).then_inc(o_stored, 16)
            for s in range(2):
                load_tile(sp, ring, s, dram["w_hg"][s], None)
            for s in range(2, HG_TILES):
                load_tile(sp, ring, s % 2, dram["w_hg"][s], s)

            def store(p):
                sp.wait_ge(o_ready, p + 2)
                sp.dma_start(one(y_out[ds(p, 1)]), o_norm[:]).then_inc(o_stored, 16)

            for s in range(HG_TILES):
                load_tile(sp, ring, s % 2, dram["w_hg"][HG_TILES + s], HG_TILES + s)
            with sp.Fori(2, H) as u:
                for s in range(HG_TILES):
                    n = HG_TILES * u + s
                    load_tile(sp, ring, s % 2, one(dram["w_hg"][ds(n, 1)]), n)
                store(u - 2)
            store(H - 2)
            store(H - 1)
            sp.wait_ge(o_stored, 16 + 16 * H)

        @block.gpsimd
        def _(pool):
            split_low_all(nc, pool, ring, H * HG_TILES)

        @block.scalar
        def _(act):
            chain = Chain(act, act_done)
            nc.scalar.preload_act_table_set(EXP_LN_SET)
            act.wait_ge(lb_step, 1)
            nc.scalar.activation(lb_in[:], lb_in[:], ACT.Exp).then_inc(lb_step, 1)
            split_high(nc, act, ring, 0, 0, 0)

            def body(u, proj, comp, ahead=True):
                p = u - 1
                for s in range(HG_TILES):
                    n = HG_TILES * u + s
                    if proj and (ahead or s < HG_TILES - 1):
                        split_high(nc, act, ring, (s + 1) % 2, n + 1, 2 * u + (s + 1) // 2)
                    if s == 0 and proj:
                        act.wait_ge(ring.used, n + 3)
                        act.wait_ge(lev_ready, u + 1)
                        nc.scalar.activation(f[:], acc[0][:], ACT.Exp, scale=-1.0).then_inc(f_exp, 1)
                        act.wait_ge(f_ready, u + 1)
                        nc.scalar.activation(b[:], f[:], ACT.Ln).then_inc(f_log, 1)
                    if s == 1 and proj:
                        act.wait_ge(ring.used, n + 3)
                        nc.scalar.activation(sg[:], acc[1][:], ACT.Exp, scale=-1.0).then_inc(q_exp, 1)
                    if s == 2:
                        if proj:
                            act.wait_ge(lev_diff, u + 1)
                            nc.scalar.activation(lev[:, 0:LK], lev[:, 0:LK], ACT.Exp).then_inc(lev_exp, 1)
                        if comp:
                            act.wait_ge(b_done, NC * p + NC)
                            nc.scalar.activation(o_sq[:], ps_o[:], ACT.Square).then_inc(squared, 1)
                    if s == 3:
                        if comp:
                            act.wait_ge(summed, p + 1)
                            chain.after(nc.scalar.activation(rstd[:], ps_k[:], ACT.Ln, bias=const["eps"],
                                                             scale=1.0 / P))
                            nc.scalar.activation(rstd[:], rstd[:], ACT.Exp, scale=-0.5).then_inc(rooted, 1)
                        if proj:
                            act.wait_ge(ring.used, n + 3)
                            act.wait_ge(acc_read, HG_TILES * u + 4)
                            nc.scalar.activation(sg[:], acc[1][:], ACT.Exp, scale=-1.0).then_inc(g_exp, 1)

            body(0, True, False)
            with act.Fori(1, H - 1) as u:
                chain.enter(u - 1, 1)
                body(u, True, True)
            chain.leave(H - 2)
            body(H - 1, True, True, ahead=False)
            body(H, False, True)

        @block.tensor
        def _(pe):
            nc.tensor.nop().then_inc(ring.used, 2)

            def turn(dst, src):
                for c in range(NC):
                    last = nc.tensor.transpose(dst[:, c * P:(c + 1) * P], src[:, c * CH:(c + 1) * CH],
                                               const["ident"])
                last.then_inc(turned, 1)

            def part_a(p, c):
                pe.wait_ge(a_read, NC * p + c + 1)
                tok = slice(c * CH, (c + 1) * CH)
                for l in range(LEVELS):
                    nc.tensor.matmul(ps_lev[:, l], lev[:, l, tok], lev[:, l, tok], start=True, stop=True)
                nc.tensor.matmul(ps_lev[:, LEVELS], lev[:, LK, tok], lev[:, LQ, tok],
                                 start=True, stop=True).then_inc(a_done, 1)

            def part_b(p, c):
                tok = slice(c * CH, (c + 1) * CH)
                pe.wait_ge(probs_ready, NC * p + c + 1)
                if c == 0:
                    pe.wait_ge(o_ready, p + 1)
                    pe.wait_ge(turned_read, 2 * p + 2)
                last = nc.tensor.matmul(ps_o[:, tok], v_tok[:, c], probs[:, c % 2], start=True, stop=(c == 0))
                if c > 0:
                    pe.wait_ge(state_ready, (NC - 1) * p + c)
                    last = nc.tensor.matmul(ps_o[:, tok], state[:], qe[:, tok], start=False, stop=True)
                if c < NC - 1:
                    last = nc.tensor.matmul(ps_state[:], k_tok[:, c], v_tok[:, c], start=True, stop=True)
                last.then_inc(b_done, 1)

            def body(u, proj, comp):
                p = u - 1
                for s in range(HG_TILES):
                    n = HG_TILES * u + s

                    def half(i):
                        if not proj:
                            return
                        if i == 0:
                            pe.wait_ge(ring.low_ready, n + 1)
                            pe.wait_ge(acc_read, n + 1)
                        last = product(nc, acc[s % 2][:], ring.high[:, s % 2], ring.low[:, s % 2], h[0], h[1],
                                       range(i * KT // 2, (i + 1) * KT // 2))
                        if i == 1:
                            last.then_inc(ring.used, 1)

                    half(0)
                    if comp:
                        if s == 0:
                            pe.wait_ge(lev_ready, p + 2)
                            turn(ps_v, v)
                            pe.wait_ge(rooted, p + 1)
                            turn(ps_k, lev[:, L8])
                            part_a(p, 0)
                        if s == 1:
                            part_b(p, 0)
                            part_a(p, 2)
                        if s == 2:
                            part_b(p, 2)
                        if s == 3:
                            pe.wait_ge(squared, p + 1)
                            nc.tensor.matmul(ps_k[:], const["ones"], o_sq[:], start=True, stop=True).then_inc(summed, 1)
                    half(1)
                    if comp:
                        if s == 0:
                            part_a(p, 1)
                        if s == 1:
                            part_b(p, 1)
                            part_a(p, 3)
                        if s == 2:
                            part_b(p, 3)

            body(0, True, False)
            with pe.Fori(1, H) as u:
                body(u, True, True)
            body(H, False, True)

        @block.vector
        def _(dve):
            chain = Chain(dve, vec_done)
            vec = nc.vector
            vec.nop().then_inc(acc_read, 2)
            vec.nop().then_inc(a_read, 1)
            vec.nop().then_inc(o_ready, 1)
            vec.nop().then_inc(rooted, 1)
            vec.nop().then_inc(lev_ready, 1)
            dve.wait_ge(consts, 32)
            dve.wait_ge(o_stored, 16)
            chain.after(vec.tensor_tensor(lb_max[:], lb_in[:, 0], lb_in[:, 1], ALU.max))
            vec.tensor_tensor(lb_in[:], lb_in[:], lb_max[:].unsqueeze(1).to_broadcast([P, 2, KT]),
                              ALU.subtract).then_inc(lb_step, 1)
            dve.wait_ge(lb_step, 2)
            chain.after(vec.tensor_tensor(lb_max[:], lb_in[:, 0], lb_in[:, 1], ALU.add))
            chain.after(vec.reciprocal(lb_max[:], lb_max[:]))
            chain.after(vec.tensor_tensor(lb[:, 0], lb_in[:, 0], lb_max[:], ALU.mult))
            chain.after(vec.tensor_scalar(lb[:, 1], lb[:, 0], -1.0, 1.0, ALU.mult, ALU.add))

            def take_f(u):
                dve.wait_ge(f_exp, u + 1)
                ins = vec.tensor_scalar(sg[:], f[:], 1.0, None, ALU.add)
                ins.then_inc(acc_read, 1)
                dve.wait_ge(acc_read, HG_TILES * u + 3)
                chain.after(vec.reciprocal(sg[:], sg[:]))
                vec.tensor_scalar(f[:], sg[:], lb[:, 1, ds(u, 1)], lb[:, 0, ds(u, 1)],
                                  ALU.mult, ALU.add).then_inc(f_ready, 1)
                dve.wait_ge(f_ready, u + 1)
                chain.after(vec.tensor_scalar(k[:], f[:], -1.0, 1.0, ALU.mult, ALU.add))
                dve.wait_ge(f_log, u + 1)
                for c in range(NC):
                    tok = slice(c * CH, (c + 1) * CH)
                    ins = vec.tensor_tensor_scan(b[:, tok], const["ones"][:, 0:CH], b[:, tok], 0.0,
                                                 ALU.mult, ALU.add)
                ins.then_inc(b_ready, 1)

            def swish(dst, src, exp_done, value, taken):
                dve.wait_ge(exp_done, value)
                chain.after(vec.tensor_scalar(sg[:], sg[:], 1.0, None, ALU.add))
                chain.after(vec.reciprocal(sg[:], sg[:]))
                vec.tensor_tensor(dst[:], src[:], sg[:], ALU.mult).then_inc(acc_read, 1)
                dve.wait_ge(acc_read, taken)

            def take_probs(p, c):
                dve.wait_ge(a_done, NC * p + c + 1)
                if c > 0:
                    dve.wait_ge(probs_ready, NC * p + c)
                vec.tensor_tensor(masked[:], ps_lev[:], mask[:], ALU.mult).then_inc(a_read, 1)
                dve.wait_ge(a_read, NC * p + c + 2)
                vec.tensor_reduce(probs[:, c % 2], masked[:].rearrange("p l t -> p t l"), AX_X,
                                  ALU.add).then_inc(probs_ready, 1)

            def next_state(p, c):
                dve.wait_ge(b_done, NC * p + c + 1)
                if c == 0:
                    vec.tensor_copy(state[:], ps_state[:]).then_inc(state_ready, 1)
                else:
                    vec.scalar_tensor_tensor(state[:], state[:], k_end[:, c:c + 1], ps_state[:],
                                             ALU.mult, ALU.add).then_inc(state_ready, 1)

            def exponents(u):
                dve.wait_ge(b_ready, u + 1)
                for l, w in enumerate(HALVES):
                    halves = lambda x: x.rearrange("p (n a w) -> p n a w", a=2, w=w)
                    src, dst = halves(b[:]), halves(lev[:, l])
                    n = T // (2 * w)
                    ref = src[:, :, 0, w - 1:w].to_broadcast([P, n, w])
                    vec.tensor_tensor(dst[:, :, 1, :], src[:, :, 1, :], ref, ALU.subtract)
                    vec.tensor_tensor(dst[:, :, 0, :], ref, src[:, :, 0, :], ALU.subtract)
                vec.tensor_copy(lev[:, L7], b[:])
                chunks = lambda x: x.rearrange("p (c t) -> p c t", c=NC)
                vec.tensor_tensor(chunks(lev[:, L8]), chunks(b[:])[:, :, CH - 1:CH].to_broadcast([P, NC, CH]),
                                  chunks(b[:]), ALU.subtract).then_inc(lev_diff, 1)

            def weigh(u, p, comp):
                dve.wait_ge(lev_exp, u + 1)
                for l, w in enumerate(HALVES):
                    halves = lambda x: x.rearrange("p (n a w) -> p n a w", a=2, w=w)
                    dst = halves(lev[:, l])
                    vec.tensor_tensor(dst[:, :, 1, :], dst[:, :, 1, :], halves(q[:])[:, :, 1, :], ALU.mult)
                    vec.tensor_tensor(dst[:, :, 0, :], dst[:, :, 0, :], halves(k[:])[:, :, 0, :], ALU.mult)
                vec.tensor_copy(lev[:, LK], k[:])
                vec.tensor_copy(lev[:, LQ], q[:])
                if comp:
                    dve.wait_ge(b_done, NC * p + NC)
                vec.tensor_tensor(qe[:], lev[:, L7], q[:], ALU.mult)
                vec.tensor_copy(k_end[:], lev[:, L7].rearrange("p (c t) -> p c t", c=NC)[:, :, CH - 1])
                vec.tensor_tensor(lev[:, L8], lev[:, L8], k[:], ALU.mult).then_inc(lev_ready, 1)
                dve.wait_ge(lev_ready, u + 2)

            def body(u, proj, comp):
                p = u - 1
                n = HG_TILES * u
                if comp:
                    dve.wait_ge(turned, 2 * p + 1)
                    vec.tensor_copy(v_tok[:].rearrange("p c v -> p (c v)"), ps_v[:]).then_inc(turned_read, 1)
                    dve.wait_ge(turned, 2 * p + 2)
                    vec.tensor_copy(k_tok[:].rearrange("p c v -> p (c v)"), ps_k[:]).then_inc(turned_read, 1)
                    take_probs(p, 0)
                    take_probs(p, 1)
                if proj:
                    take_f(u)
                if comp:
                    next_state(p, 0)
                    take_probs(p, 2)
                    next_state(p, 1)
                    take_probs(p, 3)
                if proj:
                    swish(q, acc[1], q_exp, u + 1, n + 4)
                    exponents(u)
                    dve.wait_ge(ring.used, n + 5)
                    vec.tensor_copy(v[:], acc[0][:]).then_inc(acc_read, 1)
                if comp:
                    next_state(p, 2)
                if proj:
                    weigh(u, p, comp)
                if comp:
                    dve.wait_ge(rooted, p + 2)
                    dve.wait_ge(o_stored, 16 * p + 16)
                    chain.after(vec.scalar_tensor_tensor(o_norm[:], ps_o[:], norm_w[:, 0:1], rstd[:],
                                                         ALU.mult, ALU.mult))
                    vec.tensor_tensor(o_norm[:], o_norm[:], og[:], ALU.mult).then_inc(o_ready, 1)
                    dve.wait_ge(o_ready, p + 2)
                if proj:
                    swish(og, acc[1], g_exp, u + 1, n + 6)

            body(0, True, False)
            with dve.Fori(1, H) as u:
                chain.enter(u - 1, 2 + 2 + 1 + 2)
                body(u, True, True)
            chain.leave(H - 1)
            body(H, False, True)



def mix_stage(nc, name, w, h, y_src, prior, dst):
    with ExitStack() as ctx:
        sb = lambda n, s, dt=F32: ctx.enter_context(nc.sbuf_tensor(f"sb_{name}_{n}", s, dt))
        ps = lambda n, s: ctx.enter_context(nc.psum_tensor(f"{name}_{n}", s, F32))
        sem = ctx.enter_context(semaphores(nc, name))
        ring = make_ring(nc, ctx, name, sem)
        PIECE = 4
        y_raw = sb("y_raw", [P, 2, PIECE, T])
        y_high = sb("y_high", [P, KT, T], F32R)
        y_low = sb("y_low", [P, KT, T], F32R)
        expo = sb("expo", [P, T])
        gate = sb("gate", [P, T])
        mixed = sb("mixed", [P, T])
        before = sb("before", [P, T])
        acc = [ps(f"acc{i}", [P, T]) for i in range(2)]
        y_landed = [sem("y_landed0"), sem("y_landed1")]
        y_high_ready, y_low_ready = sem("y_high_ready"), sem("y_low_ready")
        gate_exp, gate_ready = sem("gate_exp"), sem("gate_ready")
        mixed_ready, stored, before_landed, vec_done = (
            sem("mixed_ready"), sem("stored"), sem("before_landed"), sem("vec_done"))
        block = ctx.enter_context(nc.Block())

        @block.sync
        def _(sp):
            for s in range(2):
                load_tile(sp, ring, s, w[s], None)
            for i in range(KT // PIECE):
                if i >= 2:
                    sp.wait_ge(y_low_ready, i - 1)
                sp.dma_start(y_raw[:, i % 2], y_src[i * PIECE:(i + 1) * PIECE].rearrange("k p t -> p k t")
                             ).then_inc(y_landed[i % 2], 16)

            def rest(n, load):
                if load:
                    for s in range(2):
                        load_tile(sp, ring, s, one(w[ds(2 * n + 2 + s, 1)]), 2 * n + 2 + s)
                if prior is not None:
                    sp.dma_start(before[:], one(prior[ds(n, 1)])).then_inc(before_landed, 16)
                sp.wait_ge(mixed_ready, n + 1)
                sp.dma_start(one(dst[ds(n, 1)]), mixed[:]).then_inc(stored, 16)

            with sp.Fori(0, KT - 1) as n:
                rest(n, True)
            rest(KT - 1, False)
            sp.wait_ge(stored, 16 * KT)

        @block.gpsimd
        def _(pool):
            split_low_all(nc, pool, ring, 2 * KT)

        @block.scalar
        def _(act):
            split_high(nc, act, ring, 0, 0, 0)
            for i in range(KT // PIECE):
                act.wait_ge(y_landed[i % 2], 16 * (i // 2) + 16)
                nc.scalar.activation(y_high[:, i * PIECE:(i + 1) * PIECE], y_raw[:, i % 2],
                                     ACT.Copy).then_inc(y_high_ready, 1)

            def body(n, ahead):
                split_high(nc, act, ring, 1, 2 * n + 1, n)
                act.wait_ge(ring.used, 2 * n + 3)
                act.wait_ge(gate_ready, n + 1)
                nc.scalar.activation(expo[:], acc[0][:], ACT.Exp, scale=-1.0).then_inc(gate_exp, 1)
                if ahead:
                    split_high(nc, act, ring, 0, 2 * n + 2, n + 1)

            with act.Fori(0, KT - 1) as n:
                body(n, True)
            body(KT - 1, False)

        @block.tensor
        def _(pe):
            nc.tensor.nop().then_inc(ring.used, 2)

            def body(n, first):
                pe.wait_ge(ring.low_ready, 2 * n + 1)
                if not first:
                    pe.wait_ge(gate_exp, n)
                product(nc, acc[0][:], ring.high[:, 0], ring.low[:, 0], h[0], h[1]).then_inc(ring.used, 1)
                pe.wait_ge(ring.low_ready, 2 * n + 2)
                if first:
                    pe.wait_ge(y_low_ready, KT // PIECE)
                else:
                    pe.wait_ge(mixed_ready, n)
                product(nc, acc[1][:], ring.high[:, 1], ring.low[:, 1], y_high, y_low).then_inc(ring.used, 1)

            body(0, True)
            with pe.Fori(1, KT) as n:
                body(n, False)

        @block.vector
        def _(dve):
            chain = Chain(dve, vec_done)
            nc.vector.nop().then_inc(gate_ready, 1)
            for i in range(KT // PIECE):
                dve.wait_ge(y_high_ready, i + 1)
                piece = slice(i * PIECE, (i + 1) * PIECE)
                nc.vector.tensor_tensor(y_low[:, piece], y_raw[:, i % 2], y_high[:, piece].bitcast(F32),
                                        ALU.subtract).then_inc(y_low_ready, 1)

            def body(n, first):
                dve.wait_ge(gate_exp, n + 1)
                if not first:
                    dve.wait_ge(mixed_ready, n)
                nc.vector.tensor_scalar(gate[:], expo[:], 1.0, None, ALU.add).then_inc(gate_ready, 1)
                dve.wait_ge(gate_ready, n + 2)
                chain.after(nc.vector.reciprocal(gate[:], gate[:]))
                dve.wait_ge(ring.used, 2 * n + 4)
                if not first:
                    dve.wait_ge(stored, 16 * n)
                product_done = nc.vector.tensor_tensor(mixed[:], acc[1][:], gate[:], ALU.mult)
                if prior is None:
                    product_done.then_inc(mixed_ready, 1)
                else:
                    chain.after(product_done)
                    dve.wait_ge(before_landed, 16 * n + 16)
                    nc.vector.tensor_tensor(mixed[:], mixed[:], before[:], ALU.add).then_inc(mixed_ready, 1)

            body(0, True)
            with dve.Fori(1, KT) as n:
                chain.enter(n - 1, 1 if prior is None else 2)
                body(n, False)



def out_stage(nc, dram, mix, x_mid):
    with ExitStack() as ctx:
        sb = lambda n, s, dt=F32: ctx.enter_context(nc.sbuf_tensor(f"sb_out_{n}", s, dt))
        sem = ctx.enter_context(semaphores(nc, "out"))
        ring = make_ring(nc, ctx, "out", sem)
        PIECE = 4
        raw = sb("raw_mix", [P, 2, PIECE, T])
        m_high = sb("m_high", [P, KT, T], F32R)
        m_low = sb("m_low", [P, KT, T], F32R)
        acc = [ctx.enter_context(nc.psum_tensor(f"out_acc{i}", [P, T], F32)) for i in range(2)]
        landed = [sem("mix_landed0"), sem("mix_landed1")]
        x_landed, m_high_ready, m_low_ready, added = (sem("x_landed"), sem("m_high_ready"),
                                                      sem("m_low_ready"), sem("added"))
        w = dram["w_out"]
        block = ctx.enter_context(nc.Block())

        @block.sync
        def _(sp):
            load_tile(sp, ring, 0, w[0], None)
            for i in range(KT // PIECE):
                if i >= 2:
                    sp.wait_ge(m_low_ready, i - 1)
                sp.dma_start(raw[:, i % 2], mix[i * PIECE:(i + 1) * PIECE].rearrange("k p t -> p k t")
                             ).then_inc(landed[i % 2], 16)
            load_tile(sp, ring, 1, w[1], None)
            sp.dma_start(x_mid[:], dram["x_t"]).then_inc(x_landed, 16)
            with sp.Fori(1, KT // 2) as i:
                for s in range(2):
                    load_tile(sp, ring, s, one(w[ds(2 * i + s, 1)]), 2 * i + s)

        @block.gpsimd
        def _(pool):
            split_low_all(nc, pool, ring, KT)

        @block.scalar
        def _(act):
            for i in range(KT // PIECE):
                act.wait_ge(landed[i % 2], 16 * (i // 2) + 16)
                nc.scalar.activation(m_high[:, i * PIECE:(i + 1) * PIECE], raw[:, i % 2],
                                     ACT.Copy).then_inc(m_high_ready, 1)
            with act.Fori(0, KT // 2) as i:
                for s in range(2):
                    split_high(nc, act, ring, s, 2 * i + s, i)

        @block.tensor
        def _(pe):
            nc.tensor.nop().then_inc(ring.used, 2)
            pe.wait_ge(m_low_ready, KT // PIECE)
            with pe.Fori(0, KT // 2) as i:
                for s in range(2):
                    pe.wait_ge(ring.low_ready, 2 * i + (s + 1))
                    pe.wait_ge(added, 2 * i + (s + 1))
                    product(nc, acc[s][:], ring.high[:, s], ring.low[:, s], m_high, m_low).then_inc(ring.used, 1)

        @block.vector
        def _(dve):
            nc.vector.nop().then_inc(added, 2)
            for i in range(KT // PIECE):
                dve.wait_ge(m_high_ready, i + 1)
                piece = slice(i * PIECE, (i + 1) * PIECE)
                nc.vector.tensor_tensor(m_low[:, piece], raw[:, i % 2], m_high[:, piece].bitcast(F32),
                                        ALU.subtract).then_inc(m_low_ready, 1)
            dve.wait_ge(x_landed, 16)
            with dve.Fori(0, KT // 2) as i:
                for s in range(2):
                    dve.wait_ge(ring.used, 2 * i + (s + 3))
                    x = x_mid[:, ds(2 * i + s, 1)].rearrange("p a t -> p (a t)")
                    nc.vector.tensor_tensor(x, x, acc[s][:], ALU.add).then_inc(added, 1)



def route_stage(nc, dram, h, const, place, gate_t):
    with ExitStack() as ctx:
        sb = lambda n, s, dt=F32: ctx.enter_context(nc.sbuf_tensor(f"sb_rt_{n}", s, dt))
        ps = lambda n, s: ctx.enter_context(nc.psum_tensor(f"rt_{n}", s, F32))
        sem = ctx.enter_context(semaphores(nc, "rt"))
        ring = make_ring(nc, ctx, "rt", sem)
        w = dram["w_query"]
        keys = sb("keys", [P, KT, KEYS])
        count = sb("count", [P, P])
        query = sb("query", [P, 2, T])
        score = sb("score", [P, 2, NC, KEYS])
        top = sb("top", [P, 2, NC, TOPK])
        top_at = sb("top_at", [P, 2, NC, TOPK], U32)
        top_key = sb("top_key", [P, 2, NC, TOPK])
        pair = sb("pair", [P, NC, TOPK, TOPK])
        best_at = sb("best_at", [P, NC, TOPK], U32)
        half_at = sb("half_at", [P, NC, TOPK], U32)
        half_pos = sb("half_pos", [P, NC, TOPK])
        hit = sb("hit", [P, NC, TOPK, TOPK])
        best = sb("best", [P, NC, PEER_HEADS, TOPK])
        total = sb("total", [P, NC, PEER_HEADS])
        chosen = sb("chosen", [P, 2, NC, PEER_HEADS, TOPK])
        acc = [ps(f"acc{i}", [P, T]) for i in range(2)]
        ps_score = [ps(f"score{i}", [P, NC, KEYS]) for i in range(2)]
        ps_turn = [ps(f"turn{i}", [P, T]) for i in range(3)]
        consts, query_ready, score_done, score_read, exp_in, exp_done, gates_ready, turned, vec_done = (
            sem(n) for n in ("consts", "query_ready", "score_done", "score_read", "exp_in", "exp_done",
                             "gates_ready", "turned", "vec_done"))
        block = ctx.enter_context(nc.Block())

        @block.sync
        def _(sp):
            for s in range(2):
                load_tile(sp, ring, s, w[s], None)
            sp.dma_start(keys[:], dram["sub_keys"]).then_inc(consts, 16)
            sp.dma_start(count[:], dram["count"]).then_inc(consts, 16)
            with sp.Fori(1, KT // 2) as i:
                for s in range(2):
                    load_tile(sp, ring, s, one(w[ds(2 * i + s, 1)]), 2 * i + s)

        @block.gpsimd
        def _(pool):
            split_low_all(nc, pool, ring, KT)

        @block.scalar
        def _(act):
            split_high(nc, act, ring, 0, 0, 0)

            def body(i, ahead):
                for s in range(2):
                    if s == 0 or ahead:
                        split_high(nc, act, ring, 1 - s, 2 * i + s + 1, i + s)
                    act.wait_ge(ring.used, 2 * i + (s + 3))
                    act.wait_ge(score_done, 2 * i + (s + 1))
                    nc.scalar.activation(query[:, s], acc[s][:], ACT.Copy).then_inc(query_ready, 1)

            with act.Fori(0, KT // 2 - 1) as i:
                body(i, True)
            body(KT // 2 - 1, False)
            act.wait_ge(exp_in, 1)
            nc.scalar.activation(best[:], best[:], ACT.Exp).then_inc(exp_done, 1)

        @block.tensor
        def _(pe):
            nc.tensor.nop().then_inc(ring.used, 2)
            nc.tensor.nop().then_inc(score_done, 2)
            pe.wait_ge(consts, 32)

            def project(i, s):
                pe.wait_ge(ring.low_ready, 2 * i + (s + 1))
                pe.wait_ge(query_ready, 2 * i + (s + 1))
                product(nc, acc[s][:], ring.high[:, s], ring.low[:, s], h[0], h[1]).then_inc(ring.used, 1)

            def match(i, s):
                pe.wait_ge(query_ready, 2 * i + (s + 3))
                pe.wait_ge(score_read, 2 * i + (s + 1))
                for c in range(NC):
                    last = nc.tensor.matmul(ps_score[s][:, c], query[:, s, c * P:(c + 1) * P],
                                            keys[:, ds(2 * i + s, 1)].rearrange("p a k -> p (a k)"),
                                            start=True, stop=True)
                last.then_inc(score_done, 1)

            with pe.Fori(0, KT // 2) as i:
                project(i, 0)
                project(i, 1)
                match(i, 0)
                match(i, 1)
            pe.wait_ge(gates_ready, 1)
            for a, src in enumerate((chosen[:, 0], chosen[:, 1], best)):
                for c in range(NC):
                    last = nc.tensor.transpose(ps_turn[a][:, c * P:(c + 1) * P],
                                               src[:, c].rearrange("p h k -> p (h k)"), const["ident"])
            last.then_inc(turned, 1)

        @block.vector
        def _(dve):
            vec = nc.vector
            chain = Chain(dve, vec_done)
            vec.nop().then_inc(query_ready, 2)
            vec.nop().then_inc(score_read, 2)
            dve.wait_ge(consts, 32)

            def top_of(dst, dst_at, src, row):
                for j in range(0, TOPK, 8):
                    for c in range(NC):
                        ins = vec.max(dst(c)[:, j:j + 8], src(c))
                    chain.after(ins)
                    for c in range(NC):
                        ins = vec.max_index(dst_at(c)[:, j:j + 8], dst(c)[:, j:j + 8], src(c))
                    chain.after(ins)
                    if j + 8 < TOPK:
                        for c in range(NC):
                            ins = vec.match_replace(src(c), dst(c)[:, j:j + 8], src(c), NEG)
                        chain.after(ins)

            def body(head):
                for s in range(2):
                    dve.wait_ge(score_done, 2 * head + s + 3)
                    vec.tensor_copy(score[:, s], ps_score[s][:]).then_inc(score_read, 1)
                    dve.wait_ge(score_read, 2 * head + s + 3)
                    top_of(lambda c: top[:, s, c], lambda c: top_at[:, s, c], lambda c: score[:, s, c], KEYS)
                chain.after(vec.tensor_copy(top_key[:], top_at[:]))
                full = [P, NC, TOPK, TOPK]
                chain.after(vec.tensor_tensor(pair[:], top[:, 0].unsqueeze(3).to_broadcast(full),
                                              top[:, 1].unsqueeze(2).to_broadcast(full), ALU.add))
                best_h = best[:, :, head]
                top_of(lambda c: best_h[:, c], lambda c: best_at[:, c],
                       lambda c: pair[:, c].rearrange("p a b -> p (a b)"), TOPK * TOPK)
                for half, (op, by) in enumerate(((ALU.logical_shift_right, 4), (ALU.bitwise_and, TOPK - 1))):
                    chain.after(vec.tensor_scalar(half_at[:], best_at[:], by, None, op))
                    chain.after(vec.tensor_copy(half_pos[:], half_at[:]))
                    chain.after(vec.tensor_tensor(
                        hit[:], half_pos[:].unsqueeze(3).to_broadcast(full),
                        count[:, 0:TOPK].unsqueeze(1).unsqueeze(1).to_broadcast(full), ALU.is_equal))
                    chain.after(vec.tensor_tensor(hit[:], hit[:], top_key[:, half].unsqueeze(2).to_broadcast(full),
                                                  ALU.mult))
                    chain.after(vec.tensor_reduce(chosen[:, half, :, head], hit[:], AX_X, ALU.add))

            for head in range(PEER_HEADS):
                body(head)
            wide = [P, NC, PEER_HEADS, TOPK]
            flat = lambda x: x[:].rearrange("p c h k -> p (c h) k")
            chain.after(vec.tensor_copy(total[:], best[:, :, :, 0]))
            vec.tensor_tensor(flat(best), flat(best),
                              total[:].rearrange("p c h -> p (c h)").unsqueeze(2).to_broadcast(
                                  [P, NC * PEER_HEADS, TOPK]), ALU.subtract).then_inc(exp_in, 1)
            dve.wait_ge(exp_done, 1)
            chain.after(vec.tensor_reduce(total[:], best[:], AX_X, ALU.add))
            chain.after(vec.reciprocal(total[:], total[:]))
            vec.tensor_tensor(flat(best), flat(best),
                              total[:].rearrange("p c h -> p (c h)").unsqueeze(2).to_broadcast(
                                  [P, NC * PEER_HEADS, TOPK]), ALU.mult).then_inc(gates_ready, 1)
            dve.wait_ge(turned, 1)
            vec.tensor_copy(place[:, 0], ps_turn[0][:])
            vec.tensor_copy(place[:, 1], ps_turn[1][:])
            vec.tensor_copy(gate_t[:], ps_turn[2][:])


def gate_stage(nc, dram, place, gate_t, gates):
    with ExitStack() as ctx:
        sb = lambda n, s, dt=F32: ctx.enter_context(nc.sbuf_tensor(f"sb_gt_{n}", s, dt))
        sem = ctx.enter_context(semaphores(nc, "gt"))
        GROUP = 4
        BANKS = 4
        count = sb("count", [P, P])
        hot1 = sb("hot1", [P, BANKS, GROUP, KEYS])
        hot2 = sb("hot2", [P, BANKS, GROUP, KEYS])
        table = sb("table", [P, KEYS, GT])
        ps_gate = [ctx.enter_context(nc.psum_tensor(f"gt_ps{i}", [P, GROUP, KEYS], F32)) for i in range(BANKS)]
        consts, hot_ready, made, taken, stored = (
            sem(n) for n in ("consts", "hot_ready", "made", "taken", "stored"))
        TURNS = GT // GROUP // BANKS
        block = ctx.enter_context(nc.Block())

        @block.sync
        def _(sp):
            sp.dma_start(count[:], dram["count"]).then_inc(consts, 16)
            for blk in range(T // GT):
                sp.wait_ge(taken, (blk + 1) * GT // GROUP + BANKS)
                sp.dma_start(gates[:, :, blk * GT:(blk + 1) * GT].rearrange("j i t -> i j t"), table[:]
                             ).then_inc(stored, 16)
            sp.wait_ge(stored, 16 * (T // GT))

        @block.vector
        def _(dve):
            nc.vector.nop().then_inc(made, BANKS)
            nc.vector.nop().then_inc(taken, BANKS)
            dve.wait_ge(consts, 16)
            with dve.Fori(0, T // GROUP // BANKS) as i:
                for b in range(BANKS):
                    dve.wait_ge(made, BANKS * i + (b + 1))
                    for g in range(GROUP):
                        t = (i * BANKS + b) * GROUP + g
                        nc.vector.tensor_scalar(hot1[:, b, g], count[:], place[:, 0, ds(t, 1)],
                                                      gate_t[:, ds(t, 1)], ALU.is_equal, ALU.mult)
                        ins = nc.vector.tensor_scalar(hot2[:, b, g], count[:], place[:, 1, ds(t, 1)], None,
                                                      ALU.is_equal)
                    ins.then_inc(hot_ready, 1)

        @block.tensor
        def _(pe):
            with pe.Fori(0, T // GROUP // BANKS) as i:
                for b in range(BANKS):
                    pe.wait_ge(hot_ready, BANKS * i + (b + 1))
                    pe.wait_ge(taken, BANKS * i + (b + 1))
                    for g in range(GROUP):
                        last = nc.tensor.matmul(ps_gate[b][:, g], hot1[:, b, g], hot2[:, b, g],
                                                start=True, stop=True)
                    last.then_inc(made, 1)

        @block.scalar
        def _(act):
            for blk in range(T // GT):
                if blk:
                    act.wait_ge(stored, 16 * blk)
                with act.Fori(blk * TURNS, (blk + 1) * TURNS) as i:
                    for b in range(BANKS):
                        act.wait_ge(made, BANKS * i + (b + 1 + BANKS))
                        t = (i * BANKS + b - blk * TURNS * BANKS) * GROUP
                        nc.scalar.activation(table[:, :, ds(t, GROUP)].rearrange("p j g -> p g j"),
                                             ps_gate[b][:], ACT.Copy).then_inc(taken, 1)



def expert_stage(nc, dram, h, x_mid, gates):
    with ExitStack() as ctx:
        sb = lambda n, s, dt=F32: ctx.enter_context(nc.sbuf_tensor(f"sb_ex_{n}", s, dt))
        ps = lambda n, s: ctx.enter_context(nc.psum_tensor(f"ex_{n}", s, F32))
        sem = ctx.enter_context(semaphores(nc, "ex"))
        N = KEYS // 2
        raw = sb("raw", [P, 2, D])
        u_high, u_low = sb("u_high", [P, 2, D], F32R), sb("u_low", [P, 2, D], F32R)
        v_high, v_low = sb("v_high", [P, 2, D], F32R), sb("v_low", [P, 2, D], F32R)
        gelu = sb("gelu", [P, 2, T])
        gate = sb("gate", [P, 2, T])
        w_high, w_low = sb("w_high", [P, 2, T], F32R), sb("w_low", [P, 2, T], F32R)
        OUTS = 4
        acc = [ps(f"acc{i}", [P, T]) for i in range(2)]
        ps_out = [ps(f"out{i}", [P, T]) for i in range(OUTS)]
        landed = [sem("landed0"), sem("landed1")]
        high_ready, low_ready = sem("high_ready"), sem("low_ready")
        acts_done = sem("acts_done")
        gelu_done = sem("gelu_done")
        gate_landed = sem("gate_landed")
        gated = sem("gated")
        w_high_done = sem("w_high_done")
        w_ready = sem("w_ready")
        out_done = sem("out_done")
        out_added = sem("out_added")
        block = ctx.enter_context(nc.Block())

        def load(sp, slot, tile, n):
            if n is not None:
                sp.wait_ge(low_ready, n - 1)
            sp.dma_start(raw[:, slot], tile).then_inc(landed[slot], 16)

        @block.sync
        def _(sp):
            def gate_load(g, wait=True):
                if wait:
                    sp.wait_ge(gated, g)
                sp.dma_start(gate[:], gates[ds(2 * g, 2)].rearrange("a p t -> p a t")).then_inc(gate_landed, 16)

            for s in range(2):
                load(sp, s, dram["u_tiles"][s], None)
            gate_load(0, False)
            for s in range(2):
                load(sp, s, dram["u_tiles"][2 + s], 2 + s)

            def body(g, more_u, more_gate, first=4):
                for s in range(2):
                    load(sp, s, one(dram["v_tiles"][ds(2 * g + s, 1)]), 4 * g + (first + s))
                if more_gate:
                    gate_load(g + 1)
                if more_u:
                    for s in range(2):
                        load(sp, s, one(dram["u_tiles"][ds(2 * g + 4 + s, 1)]), 4 * g + (6 + s))

            with sp.Fori(0, N - 2) as g:
                body(g, True, True)
            body(N - 2, False, True)
            body(N - 1, False, False, first=2)

        @block.gpsimd
        def _(pool):
            def low(slot, n, high, dst):
                pool.wait_ge(high_ready, n + 1)
                nc.gpsimd.tensor_tensor(dst[:, slot], raw[:, slot], high[:, slot].bitcast(F32),
                                        ALU.subtract).then_inc(low_ready, 1)

            for n in range(4):
                low(n % 2, n, u_high, u_low)

            def body(g, more_u, first=4):
                for s in range(2):
                    low(s, 4 * g + (first + s), v_high, v_low)
                if more_u:
                    for s in range(2):
                        low(s, 4 * g + (6 + s), u_high, u_low)

            with pool.Fori(0, N - 2) as g:
                body(g, True)
            body(N - 2, False)
            body(N - 1, False, first=2)

        @block.scalar
        def _(act):
            def high(slot, pair, dst, free, value):
                act.wait_ge(landed[slot], 16 * pair + 16)
                if value is not None:
                    act.wait_ge(free, value)
                nc.scalar.activation(dst[:, slot], raw[:, slot], ACT.Copy).then_inc(high_ready, 1)

            def gelus(g):
                for s in range(2):
                    act.wait_ge(acts_done, 2 * g + (s + 3))
                    act.wait_ge(w_ready, g + 1)
                    nc.scalar.activation(gelu[:, s], acc[s][:], ACT.Gelu).then_inc(gelu_done, 1)

            for s in range(2):
                high(s, 0, u_high, acts_done, None)
            gelus(0)
            for s in range(2):
                high(s, 1, u_high, acts_done, 3 + s)

            def body(g, first, more_u, more_acts):
                for s in range(2):
                    high(s, 2 * g + (2 if more_acts else 1), v_high, out_done, None if first else 16 * g)
                if more_acts:
                    gelus(g + 1)
                if more_u:
                    for s in range(2):
                        high(s, 2 * g + 3, u_high, acts_done, 2 * g + (5 + s))

            body(0, True, True, True)
            with act.Fori(1, N - 2) as g:
                body(g, False, True, True)
            body(N - 2, False, False, True)
            body(N - 1, False, False, False)

        @block.tensor
        def _(pe):
            nc.tensor.nop().then_inc(acts_done, 2)

            def activations(g, n):
                for s in range(2):
                    pe.wait_ge(low_ready, n + (s + 1))
                    pe.wait_ge(gelu_done, 2 * g + (s + 1))
                    product(nc, acc[s][:], u_high[:, s], u_low[:, s], h[0], h[1]).then_inc(acts_done, 1)

            def outputs(g, last_v=6):
                pe.wait_ge(low_ready, 4 * g + last_v)
                pe.wait_ge(w_ready, g + 2)
                for d in range(KT):
                    pe.wait_ge(out_added, KT * g + (d + 1))
                    o, m = ps_out[d % OUTS][:], slice(d * P, (d + 1) * P)
                    for s in range(2):
                        nc.tensor.matmul(o, v_high[:, s, m], w_high[:, s], start=(s == 0), stop=False)
                        nc.tensor.matmul(o, v_high[:, s, m], w_low[:, s], start=False, stop=False)
                        last = nc.tensor.matmul(o, v_low[:, s, m], w_high[:, s], start=False, stop=(s == 1))
                    last.then_inc(out_done, 1)

            activations(0, 0)
            activations(1, 2)
            outputs(0)
            with pe.Fori(1, N - 1) as g:
                activations(g + 1, 4 * g + 2)
                outputs(g)
            outputs(N - 1, last_v=4)

        @block.vector
        def _(dve):
            vec = nc.vector
            vec.nop().then_inc(gelu_done, 2)
            vec.nop().then_inc(w_ready, 1)
            vec.nop().then_inc(out_added, OUTS)

            def weights(g):
                dve.wait_ge(gelu_done, 2 * g + 4)
                dve.wait_ge(gate_landed, 16 * g + 16)
                vec.tensor_tensor(gelu[:], gelu[:], gate[:], ALU.mult).then_inc(gated, 1)
                dve.wait_ge(gated, g + 1)
                vec.tensor_copy(w_high[:], gelu[:]).then_inc(w_high_done, 1)
                dve.wait_ge(w_high_done, g + 1)
                vec.tensor_tensor(w_low[:], gelu[:], w_high[:].bitcast(F32), ALU.subtract).then_inc(w_ready, 1)

            def add_outputs(g):
                for d in range(KT):
                    dve.wait_ge(out_done, KT * g + (d + 1))
                    vec.tensor_tensor(x_mid[:, d], x_mid[:, d], ps_out[d % OUTS][:], ALU.add).then_inc(out_added, 1)

            weights(0)
            with dve.Fori(0, N - 1) as g:
                add_outputs(g)
                weights(g + 1)
            add_outputs(N - 1)


def peer(nc, dram, const, vecs, mix, gates, out):
    with ExitStack() as ctx:
        x_mid = ctx.enter_context(nc.sbuf_tensor("x_mid", [P, KT, T], F32))
        out_stage(nc, dram, mix, x_mid)
        with ExitStack() as ffn:
            h = [ffn.enter_context(nc.sbuf_tensor(f"h2_{n}", [P, KT, T], F32R)) for n in ("high", "low")]
            with ExitStack() as tmp:
                work = tmp.enter_context(nc.sbuf_tensor("ffn_work", [P, KT, T], F32))
                norm_stage(nc, "ffn", x_mid, vecs["norm_ffn_w"], work, const["ones"], const["eps"], split=h)
            with ExitStack() as routing:
                place = routing.enter_context(nc.sbuf_tensor("place", [P, 2, T], F32))
                gate_t = routing.enter_context(nc.sbuf_tensor("gate_t", [P, T], F32))
                route_stage(nc, dram, h, const, place, gate_t)
                gate_stage(nc, dram, place, gate_t, gates)
            expert_stage(nc, dram, h, x_mid, gates)
        work = ctx.enter_context(nc.sbuf_tensor("final_work", [P, KT, T], F32))
        norm_stage(nc, "final", x_mid, vecs["final_norm_w"], work, const["ones"], const["eps"], store=out)



SHAPES = {
    "x_t": [P, KT, T], "norm_mix_w": [P, KT], "norm_ffn_w": [P, KT], "final_norm_w": [P, KT],
    "w_ssd": [SSD_GROUPS * SSD_TILES, P, D], "w_dt": [P, KT, SSD_HEADS],
    "w_hg": [HG_HEADS * HG_TILES, P, D],
    "w_mix_s": [2 * KT, P, D], "w_mix_h": [2 * KT, P, D], "w_out": [KT, P, D], "w_query": [KT, P, D],
    "u_tiles": [KEYS, P, D], "v_tiles": [KEYS, P, D],
    "conv_w": [P, SSD_GROUPS * 4 * (CONV + 1)], "dt_bias": [P, SSD_HEADS], "a_log": [P, SSD_HEADS],
    "ssd_d": [P, KT], "ssd_norm_w": [P, KT], "hg_lb": [P, 2, KT], "hg_norm_w": [P, 1],
    "sub_keys": [P, KT, KEYS],
    "ident": [P, P], "ones": [P, P], "later": [P, P], "upto": [P, P], "level_mask": [P, LEVELS + 1, P],
    "count": [P, P],
}


def program(nc):
    dram = {n: nc.dram_tensor(n, s, F32, kind="ExternalInput").ap() for n, s in SHAPES.items()}
    out = nc.dram_tensor("out_t", [P, KT, T], F32, kind="ExternalOutput").ap()
    y_ssd = nc.dram_tensor("y_ssd", [KT, P, T], F32).ap()
    y_hg = nc.dram_tensor("y_hg", [KT, P, T], F32).ap()
    mix_s = nc.dram_tensor("mix_s", [KT, P, T], F32).ap()
    mix = nc.dram_tensor("mix", [KT, P, T], F32).ap()
    gates = nc.dram_tensor("gates", [KEYS, P, T], F32).ap()
    with ExitStack() as ctx:
        sb = lambda n, s, dt=F32: ctx.enter_context(nc.sbuf_tensor(n, s, dt))
        const, eps, vecs = load_constants(nc, ctx, dram)
        with ExitStack() as mixers:
            h = [mixers.enter_context(nc.sbuf_tensor(f"h_{n}", [P, KT, T], F32R)) for n in ("high", "low")]
            with ExitStack() as tmp:
                x = tmp.enter_context(nc.sbuf_tensor("x", [P, KT, T], F32))
                work = tmp.enter_context(nc.sbuf_tensor("x_work", [P, KT, T], F32))
                norm_stage(nc, "in", x, vecs["norm_mix_w"], work, const["ones"], const["eps"],
                           load=dram["x_t"], split=h)
            ssd_stage(nc, dram, h, const, y_ssd)
            hg_stage(nc, dram, h, const, y_hg)
            mix_stage(nc, "mix_s", dram["w_mix_s"], h, y_ssd, None, mix_s)
            mix_stage(nc, "mix_h", dram["w_mix_h"], h, y_hg, mix_s, mix)
        peer(nc, dram, const, vecs, mix, gates, out)


def load_constants(nc, ctx, dram):
    sb = lambda n, s: ctx.enter_context(nc.sbuf_tensor(n, s, F32))
    shared = {n: sb(f"c_{n}", SHAPES[n]) for n in ("ident", "ones", "later", "upto", "norm_mix_w",
                                                   "norm_ffn_w", "final_norm_w")}
    eps = sb("c_eps", [P, 1])
    landed = ctx.enter_context(nc.semaphore("c_landed"))
    with nc.Block() as block:
        @block.sync
        def _(sp):
            for n, t in shared.items():
                sp.dma_start(t[:], dram[n]).then_inc(landed, 16)
            sp.wait_ge(landed, 16 * len(shared))

        @block.vector
        def _(dve):
            nc.vector.memset(eps[:], EPS)
    const = {n: shared[n][:] for n in ("ident", "ones", "later", "upto")}
    const["eps"] = eps[:]
    return const, eps, {n: shared[n] for n in ("norm_mix_w", "norm_ffn_w", "final_norm_w")}


def tiles_of(w):
    n = w.shape[1] // P
    return w.reshape(KT, P, n, P).transpose(2, 1, 0, 3).reshape(n, P, D)


def columns(v):
    return v.reshape(KT, P).T


def laid_out(inp):
    a = {k: np.asarray(v) for k, v in inp.items()}
    r = {}
    r["x_t"] = a["x"][0].T.reshape(KT, P, T).transpose(1, 0, 2)
    for n in ("norm_mix_w", "norm_ffn_w", "ssd_norm_w"):
        r[n] = columns(a[n][0])
    r["final_norm_w"] = columns(a["final_norm_w"])
    w = a["w_in"][0]
    sizes = (D, D + 2 * SSD_GROUPS * P, SSD_HEADS, D, D, D, D, D, D)
    z, xbc, wdt, hq, hf, hi, hg, gs, gh = np.split(w, np.cumsum(sizes)[:-1], axis=1)
    z, xbc, hq, hf, hi, hg, gs, gh = (tiles_of(m) for m in (z, xbc, hq, hf, hi, hg, gs, gh))
    order = [i for g in range(SSD_GROUPS) for i in (2 * g, 2 * g + 1, KT + g, KT + SSD_GROUPS + g)]
    per_group = xbc[order].reshape(SSD_GROUPS, 4, P, D)
    r["w_ssd"] = np.concatenate([per_group, z.reshape(SSD_GROUPS, 2, P, D)], 1).reshape(-1, P, D)
    r["w_dt"] = wdt.reshape(KT, P, SSD_HEADS).transpose(1, 0, 2)
    r["w_hg"] = np.stack([hf, hq, hi, hg], 1).reshape(-1, P, D)
    r["w_mix_s"] = np.stack([gs, tiles_of(a["w_ssd_br"][0])], 1).reshape(-1, P, D)
    r["w_mix_h"] = np.stack([gh, tiles_of(a["w_hg_br"][0])], 1).reshape(-1, P, D)
    r["w_out"] = tiles_of(a["w_out"][0])
    r["w_query"] = tiles_of(a["peer_w_q"][0])
    r["u_tiles"] = a["peer_u"][0].reshape(KEYS, KEYS, KT, P).transpose(1, 3, 2, 0).reshape(KEYS, P, D)
    r["v_tiles"] = a["peer_v"][0].reshape(KEYS, KEYS, D).transpose(1, 0, 2)
    cw = np.concatenate([a["ssd_conv_w"][0], a["ssd_conv_b"][0][None]], 0)
    r["conv_w"] = cw.reshape(CONV + 1, -1, P)[:, order].transpose(2, 1, 0).reshape(P, -1)
    r["dt_bias"] = np.broadcast_to(a["ssd_dt_bias"][0], (P, SSD_HEADS))
    r["a_log"] = np.broadcast_to(a["ssd_a_log"][0], (P, SSD_HEADS))
    r["ssd_d"] = columns(np.repeat(a["ssd_d"][0], HD))
    r["hg_lb"] = a["hg_lb"].reshape(2, KT, P).transpose(2, 0, 1)
    r["hg_norm_w"] = a["hg_norm_w"][0][:, None]
    r["sub_keys"] = a["peer_sub_keys"][0].reshape(KT, KEYS, P).transpose(2, 0, 1)
    i = np.arange(P)
    r["ident"] = np.eye(P, dtype=np.float32)
    r["ones"] = np.ones((P, P), np.float32)
    r["later"] = (i[:, None] > i[None]).astype(np.float32)
    r["upto"] = (i[:, None] <= i[None]).astype(np.float32)
    s, t = i[:, None], i[None]
    levels = [(s // (2 * w) == t // (2 * w)) & (s // w % 2 == 0) & (t // w % 2 == 1) for w in HALVES]
    r["level_mask"] = np.stack(levels + [s == t], 1).astype(np.float32)
    r["count"] = np.broadcast_to(i.astype(np.float32), (P, P))
    return {n: np.ascontiguousarray(r[n]) for n in SHAPES}


def kernel(**inputs):
    import concourse.bacc as bacc
    from concourse.bass_utils import run_bass_kernel_spmd

    nc = bacc.Bacc("TRN2", target_bir_lowering=False, num_devices=1)
    program(nc)
    got = run_bass_kernel_spmd(nc, [laid_out(inputs)], core_ids=[0]).results[0]["out_t"]
    return np.ascontiguousarray(got.transpose(1, 0, 2).reshape(D, T).T)[None]
```

```python
from contextlib import ExitStack, contextmanager

import numpy as np

import concourse.bass as bass
from concourse import mybir

F32 = mybir.dt.float32
F32R = mybir.dt.float32r
U32 = mybir.dt.uint32
ALU = mybir.AluOpType
ACT = mybir.ActivationFunctionType
AX_X = mybir.AxisListType.X
EXP_LN_SET = "natural_log_exp_and_others"

P = 128
T = 512
D = 2048
KT = D // P
CH = 128
NC = T // CH
EPS = 1e-6

SSD_GROUPS = 8
SSD_HEADS = 32
HPG = SSD_HEADS // SSD_GROUPS
HD = 64
SSD_TILES = 6
CONV = 4

HG_HEADS = 16
HG_TILES = 4
LEVELS = 7
HALVES = [CH >> (l + 1) for l in range(LEVELS)]

PEER_HEADS = 8
KEYS = 128
TOPK = 16
GT = 64
NEG = -3.0e38

ts = bass.ts
ds = bass.ds


def one(ap):
    return ap.rearrange("a p n -> (a p) n")


class Chain:

    def __init__(self, engine, done):
        self.engine, self.done = engine, done
        self.start, self.at, self.per, self.turn = 0, 0, 0, 0

    def after(self, ins):
        self.at += 1
        ins.then_inc(self.done, 1)
        self.engine.wait_ge(self.done, self.turn * self.per + (self.start + self.at))

    def enter(self, turn, per):
        self.start, self.at, self.per, self.turn = self.start + self.at, 0, per, turn

    def leave(self, turns):
        assert self.at == self.per, (self.at, self.per)
        self.start, self.at, self.per, self.turn = self.start + turns * self.per, 0, 0, 0


@contextmanager
def semaphores(nc, stage):
    with ExitStack() as ctx:
        made = []

        def sem(name):
            made.append(ctx.enter_context(nc.semaphore(f"{stage}_{name}")))
            return made[-1]

        yield sem
        with nc.Block() as block:
            @block.sync
            def _(sp):
                for s in made:
                    sp.sem_clear(s)


class Ring:

    def __init__(self, nc, ctx):
        sb = lambda n, dt: ctx.enter_context(nc.sbuf_tensor(f"ring_{n}", [P, 2, D], dt))
        sem = lambda n: ctx.enter_context(nc.semaphore(f"ring_{n}"))
        self.raw, self.high, self.low = sb("raw", F32), sb("high", F32R), sb("low", F32R)
        self.landed = [sem("landed0"), sem("landed1")]
        self.high_ready, self.low_ready, self.used = sem("high_ready"), sem("low_ready"), sem("used")
        self.base = 0


def load_tile(sp, ring, slot, tile, n):
    sp.wait_ge(ring.low_ready, ring.base + n - 1)
    sp.dma_start(ring.raw[:, slot], tile).then_inc(ring.landed[slot], 16)


def load_ahead(sp, ring, tiles, following):
    if following is not None:
        for s in range(2):
            load_tile(sp, ring, s, following[s], tiles + s)


def split_high(nc, act, ring, slot, n, pair):
    act.wait_ge(ring.landed[slot], 16 * pair + (8 * ring.base + 16))
    act.wait_ge(ring.used, ring.base + n + 1)
    nc.scalar.activation(ring.high[:, slot], ring.raw[:, slot], ACT.Copy).then_inc(ring.high_ready, 1)


def split_low(nc, pool, ring, slot, n):
    pool.wait_ge(ring.high_ready, ring.base + n + 1)
    nc.gpsimd.tensor_tensor(ring.low[:, slot], ring.raw[:, slot], ring.high[:, slot].bitcast(F32),
                            ALU.subtract).then_inc(ring.low_ready, 1)


def split_low_all(nc, pool, ring, tiles):
    with pool.Fori(0, tiles // 2) as i:
        for n in (1, 2):
            split_low(nc, pool, ring, n % 2, 2 * i + n)


def product(nc, out, high, low, x_high, x_low, steps=range(KT)):
    for k in steps:
        m = slice(k * P, (k + 1) * P)
        nc.tensor.matmul(out, high[:, m], x_high[:, k], start=(k == 0), stop=False, skip_group_check=True)
        nc.tensor.matmul(out, high[:, m], x_low[:, k], start=False, stop=False, skip_group_check=True)
        last = nc.tensor.matmul(out, low[:, m], x_high[:, k], start=False, stop=(k == KT - 1),
                                skip_group_check=True)
    return last



def norm_stage(nc, name, src, weight, work, ones, eps, load=None, split=None, store=None, ring=None,
               first_tiles=None, keep=None):
    with ExitStack() as ctx:
        sem = ctx.enter_context(semaphores(nc, name))
        mean = ctx.enter_context(nc.psum_tensor(f"{name}_mean", [P, T], F32))
        rstd = ctx.enter_context(nc.sbuf_tensor(f"{name}_rstd", [P, T], F32))
        landed, squared, summed, rooted, normed, high_done, low_done, stored, act_done = (
            sem(n) for n in ("landed", "squared", "summed", "rooted", "normed", "high_done", "low_done",
                             "stored", "act_done"))
        QUARTER = KT // 4
        block = ctx.enter_context(nc.Block())

        @block.sync
        def _(sp):
            if load is not None:
                for q in range(4):
                    sl = slice(q * QUARTER, (q + 1) * QUARTER)
                    sp.dma_start(src[:, sl], load[:, sl]).then_inc(landed, 16)
            if ring is not None:
                for s in range(2):
                    sp.dma_start(ring.raw[:, s], first_tiles[s]).then_inc(ring.landed[s], 16)
            if keep is not None:
                sp.dma_start(keep, src[:]).then_inc(stored, 16)
                sp.wait_ge(stored, 16)
            if store is not None:
                for k in range(KT):
                    sp.wait_ge(normed, k + 1)
                    sp.dma_start(store[:, k], work[:, k]).then_inc(stored, 16)
                sp.wait_ge(stored, 16 * KT)

        @block.scalar
        def _(act):
            nc.scalar.preload_act_table_set(EXP_LN_SET)
            if load is not None:
                act.wait_ge(landed, 64)
            for q in range(4):
                sl = slice(q * QUARTER, (q + 1) * QUARTER)
                nc.scalar.activation(work[:, sl], src[:, sl], ACT.Square).then_inc(squared, 1)
            act.wait_ge(summed, 1)
            nc.scalar.activation(rstd[:], mean[:], ACT.Ln, bias=eps, scale=1.0 / D).then_inc(act_done, 1)
            act.wait_ge(act_done, 1)
            nc.scalar.activation(rstd[:], rstd[:], ACT.Exp, scale=-0.5).then_inc(rooted, 1)
            if split is not None:
                for k in range(KT):
                    act.wait_ge(normed, k + 1)
                    nc.scalar.activation(split[0][:, k], work[:, k], ACT.Copy).then_inc(high_done, 1)
            if ring is not None:
                split_high(nc, act, ring, 0, 0, 0)

        @block.tensor
        def _(pe):
            if ring is not None:
                nc.tensor.nop().then_inc(ring.used, 2)
            for k in range(KT):
                pe.wait_ge(squared, k // QUARTER + 1)
                last = nc.tensor.matmul(mean[:], ones, work[:, k], start=(k == 0), stop=(k == KT - 1))
            last.then_inc(summed, 1)

        @block.vector
        def _(dve):
            dve.wait_ge(rooted, 1)
            for k in range(KT):
                nc.vector.scalar_tensor_tensor(work[:, k], src[:, k], weight[:, k:k + 1], rstd[:],
                                               ALU.mult, ALU.mult).then_inc(normed, 1)

        @block.gpsimd
        def _(pool):
            if split is not None:
                for k in range(KT):
                    pool.wait_ge(high_done, k + 1)
                    nc.gpsimd.tensor_tensor(split[1][:, k], work[:, k], split[0][:, k].bitcast(F32),
                                            ALU.subtract).then_inc(low_done, 1)
            if ring is not None:
                split_low(nc, pool, ring, 0, 0)



def ssd_stage(nc, dram, ring, h, const, y_out, following):
    G = SSD_GROUPS
    with ExitStack() as ctx:
        sb = lambda n, s, dt=F32: ctx.enter_context(nc.sbuf_tensor(f"sb_ssd_{n}", s, dt))
        ps = lambda n, s: ctx.enter_context(nc.psum_tensor(f"ssd_{n}", s, F32))
        sem = ctx.enter_context(semaphores(nc, "ssd"))
        W4 = HPG * CH
        conv = sb("conv", [P, SSD_TILES, T])
        sig = sb("sig", [P, SSD_TILES, T])
        act_in = sb("act_in", [P, SSD_TILES, T])
        half_tanh = sb("half_tanh", [P, 2, T])
        xdt = sb("xdt", [P, NC, HPG * HD])
        b_tok = sb("b_tok", [P, NC, P])
        steps = sb("steps", [P, HPG, CH])
        decay = sb("decay", [P, HPG, CH])
        decay0 = sb("decay0", [P, HPG, CH])
        scores = sb("scores", [P, CH])
        mixed = sb("mixed", [P, HPG, CH])
        c_dec = sb("c_dec", [P, HPG, CH])
        x_dec = sb("x_dec", [P, HPG, HD])
        chunk_dec = sb("chunk_dec", [P, HPG])
        state = sb("state", [P, HPG, HD])
        y = sb("y", [P, 2, T])
        y_sq = sb("y_sq", [P, 2, T])
        rstd = sb("rstd", [P, T])
        y_norm = sb("y_norm", [P, 2, T])
        wdt = sb("wdt", [P, KT, SSD_HEADS])
        wdt_high = sb("wdt_high", [P, KT, SSD_HEADS], F32R)
        wdt_low = sb("wdt_low", [P, KT, SSD_HEADS], F32R)
        dt_bias = sb("dt_bias", [P, SSD_HEADS])
        a_log = sb("a_log", [P, SSD_HEADS])
        dt = sb("dt", [P, NC, SSD_HEADS])
        adt = sb("adt", [P, NC, SSD_HEADS])
        dtx = sb("dtx", [P, NC, SSD_HEADS])
        dte = sb("dte", [P, NC, SSD_HEADS])
        dtw = sb("dtw", [P, NC, SSD_HEADS])
        dtl = sb("dtl", [P, NC, SSD_HEADS])
        conv_w = sb("conv_w", [P, G * 4 * (CONV + 1)])
        d_col = sb("d_col", [P, KT])
        norm_w = sb("norm_w", [P, KT])

        acc = [ps(f"acc{i}", [P, T]) for i in range(2)]
        ps_decay = ps("ps_decay", [P, W4])
        ps_decay0 = ps("ps_decay0", [P, W4])
        ps_turn = ps("ps_turn", [P, T])
        ps_state = ps("ps_state", [P, HPG * HD])
        ps_y = [ps(f"ps_y{i}", [P, T]) for i in range(2)]

        consts = sem("consts")
        dt_split, dt_low, dt_sum, dt_exp, dt_ln = (sem(n) for n in ("dt_split", "dt_low", "dt_sum", "dt_exp", "dt_ln"))
        acc_read = sem("acc_read")
        tanh_done = sem("tanh_done")
        sig_done = sem("sig_done")
        in_ready = sem("in_ready")
        turned = sem("turned")
        turned_read = sem("turned_read")
        steps_ready = sem("steps_ready")
        a_done = sem("a_done")
        decayed = sem("decayed")
        mixed_ready = sem("mixed_ready")
        b_done = sem("b_done")
        state_ready = sem("state_ready")
        y_read = sem("y_read")
        gated = sem("gated")
        squared = sem("squared")
        summed = sem("summed")
        rooted = sem("rooted")
        y_ready = sem("y_ready")
        y_stored = sem("y_stored")
        act_done = sem("act_done")
        vec_done = sem("vec_done")
        block = ctx.enter_context(nc.Block())

        LAST = G + 2
        @block.sync
        def _(sp):
            for dst, src in ((wdt, dram["w_dt"]), (dt_bias, dram["dt_bias"]), (a_log, dram["a_log"]),
                             (conv_w, dram["conv_w"])):
                sp.dma_start(dst[:], src).then_inc(consts, 16)
            for dst, src in ((d_col, dram["ssd_d"]), (norm_w, dram["ssd_norm_w"])):
                sp.dma_start(dst[:], src).then_inc(y_stored, 16)

            def store(f):
                sp.wait_ge(y_ready, f + 1)
                for t in range(2):
                    sp.dma_start(one(y_out[ds(2 * f + t, 1)]), y_norm[:, t]).then_inc(y_stored, 16)

            for s in range(2, SSD_TILES):
                load_tile(sp, ring, s % 2, dram["w_ssd"][s], s)
            for s in range(SSD_TILES):
                load_tile(sp, ring, s % 2, dram["w_ssd"][SSD_TILES + s], SSD_TILES + s)
            with sp.Fori(2, G) as u:
                for s in range(SSD_TILES):
                    n = SSD_TILES * u + s
                    load_tile(sp, ring, s % 2, one(dram["w_ssd"][ds(n, 1)]), n)
                store(u - 2)
            load_ahead(sp, ring, G * SSD_TILES, following)
            store(G - 2)
            store(G - 1)
            sp.wait_ge(y_stored, 32 + 32 * G)

        @block.gpsimd
        def _(pool):
            split_low_all(nc, pool, ring, G * SSD_TILES)

        @block.scalar
        def _(act):
            chain = Chain(act, act_done)
            act.wait_ge(consts, 64)
            nc.scalar.activation(wdt_high[:], wdt[:], ACT.Copy).then_inc(dt_split, 1)
            chain.after(nc.scalar.activation(a_log[:], a_log[:], ACT.Exp))
            act.wait_ge(dt_sum, 1)
            nc.scalar.activation(dte[:], dte[:], ACT.Exp, scale=-1.0).then_inc(dt_exp, 1)
            act.wait_ge(dt_ln, 1)
            nc.scalar.activation(dtl[:], dtw[:], ACT.Ln).then_inc(dt_exp, 1)

            def body(u, proj, comp, fin):
                p, f = u - 1, u - 2
                for s in range(SSD_TILES):
                    if proj:
                        split_high(nc, act, ring, (s + 1) % 2, SSD_TILES * u + s + 1, 3 * u + (s + 1) // 2)
                    if s == 0 and fin:
                        act.wait_ge(gated, f + 1)
                        nc.scalar.activation(y_sq[:], y[:], ACT.Square).then_inc(squared, 1)
                    if proj:
                        if s < 4:
                            act.wait_ge(acc_read, SSD_TILES * u + s + 3)
                        else:
                            act.wait_ge(ring.used, ring.base + SSD_TILES * u + s + 3)
                        act.wait_ge(sig_done, SSD_TILES * u + s + 1)
                        nc.scalar.activation(half_tanh[:, s % 2], conv[:, s] if s < 4 else acc[s % 2][:],
                                             ACT.Tanh, scale=0.5).then_inc(tanh_done, 1)
                    if s == 1 and fin:
                        act.wait_ge(summed, f + 1)
                        chain.after(nc.scalar.activation(rstd[:], ps_decay[:], ACT.Ln, bias=const["eps"],
                                                         scale=1.0 / (2 * P)))
                        nc.scalar.activation(rstd[:], rstd[:], ACT.Exp, scale=-0.5).then_inc(rooted, 1)
                    if s >= 2 and comp:
                        act.wait_ge(a_done, NC * p + s - 1)
                        nc.scalar.activation(decay[:].rearrange("p h l -> p (h l)"), ps_decay[:], ACT.Exp)
                        nc.scalar.activation(decay0[:].rearrange("p h l -> p (h l)"), ps_decay0[:],
                                             ACT.Exp).then_inc(decayed, 1)

            body(0, True, False, False)
            body(1, True, True, False)
            with act.Fori(2, G) as u:
                chain.enter(u - 2, 1)
                body(u, True, True, True)
            chain.leave(G - 2)
            body(G, False, True, True)
            body(G + 1, False, False, True)

        @block.tensor
        def _(pe):
            pe.wait_ge(dt_low, 1)
            for c in range(NC):
                for k in range(KT):
                    tok = slice(c * CH, (c + 1) * CH)
                    o = ps_turn[:, c * SSD_HEADS:(c + 1) * SSD_HEADS]
                    nc.tensor.matmul(o, h[0][:, k, tok], wdt_high[:, k], start=(k == 0), stop=False,
                                     skip_group_check=True)
                    nc.tensor.matmul(o, h[1][:, k, tok], wdt_high[:, k], start=False, stop=False,
                                     skip_group_check=True)
                    last = nc.tensor.matmul(o, h[0][:, k, tok], wdt_low[:, k], start=False,
                                            stop=(k == KT - 1), skip_group_check=True)
            last.then_inc(dt_low, 1)

            def turn(dst, src, done):
                for c in range(NC):
                    last = nc.tensor.transpose(dst[:, c * P:(c + 1) * P], src[:, c * CH:(c + 1) * CH],
                                               const["ident"])
                last.then_inc(done, 1)

            def part_a(p, c):
                pe.wait_ge(steps_ready, NC * p + c + 1)
                pe.wait_ge(decayed, NC * p + c + 1)
                rhs = steps[:].rearrange("p h l -> p (h l)")
                nc.tensor.matmul(ps_decay[:], const["later"], rhs, start=True, stop=True)
                nc.tensor.matmul(ps_decay0[:], const["ones"], rhs, start=True, stop=True)
                tok = slice(c * CH, (c + 1) * CH)
                nc.tensor.matmul(ps_turn[:, 0:CH], act_in[:, 2, tok], act_in[:, 3, tok],
                                 start=True, stop=True).then_inc(a_done, 1)

            def part_b(p, c):
                pe.wait_ge(mixed_ready, NC * p + c + 1)
                if c == 0:
                    pe.wait_ge(y_read, p + 1)
                else:
                    pe.wait_ge(state_ready, (NC - 1) * p + c)
                for head in range(HPG):
                    part = slice(HD * (head % 2), HD * (head % 2) + HD)
                    o = ps_y[head // 2][part, c * CH:(c + 1) * CH]
                    last = nc.tensor.matmul(o, xdt[:, c, head * HD:(head + 1) * HD], mixed[:, head],
                                            start=True, stop=(c == 0), skip_group_check=True)
                    if c > 0:
                        last = nc.tensor.matmul(o, state[:, head], c_dec[:, head], start=False, stop=True,
                                                skip_group_check=True)
                if c < NC - 1:
                    last = nc.tensor.matmul(ps_state[:], b_tok[:, c], x_dec[:].rearrange("p h d -> p (h d)"),
                                            start=True, stop=True)
                last.then_inc(b_done, 1)

            def body(u, proj, comp, fin):
                p, f = u - 1, u - 2
                for s in range(SSD_TILES):
                    n = SSD_TILES * u + s
                    if proj:
                        pe.wait_ge(ring.low_ready, ring.base + n + 1)
                        pe.wait_ge(acc_read, n + 1)
                        product(nc, acc[s % 2][:], ring.high[:, s % 2], ring.low[:, s % 2],
                                h[0], h[1]).then_inc(ring.used, 1)
                    if s == 0:
                        if fin:
                            part_b(f, NC - 1)
                        if comp:
                            pe.wait_ge(in_ready, p + 1)
                            turn(ps_turn, act_in[:, 0], turned)
                    if s == 1:
                        if fin:
                            pe.wait_ge(squared, f + 1)
                            pe.wait_ge(decayed, NC * f + NC + 1)
                            for t in range(2):
                                last = nc.tensor.matmul(ps_decay[:], const["ones"], y_sq[:, t],
                                                        start=(t == 0), stop=(t == 1))
                            last.then_inc(summed, 1)
                        if comp:
                            pe.wait_ge(turned_read, 3 * p + 1)
                            turn(ps_turn, act_in[:, 1], turned)
                    if comp:
                        if s == 2:
                            pe.wait_ge(turned_read, 3 * p + 2)
                            turn(ps_turn, act_in[:, 2], turned)
                            pe.wait_ge(turned_read, 3 * p + 3)
                            pe.wait_ge(rooted, p + 1)
                            part_a(p, 0)
                        if s > 2:
                            part_b(p, s - 3)
                            part_a(p, s - 2)

            body(0, True, False, False)
            body(1, True, True, False)
            with pe.Fori(2, G) as u:
                body(u, True, True, True)
            body(G, False, True, True)
            body(G + 1, False, False, True)

        @block.vector
        def _(dve):
            chain = Chain(dve, vec_done)
            v = nc.vector
            v.nop().then_inc(acc_read, 2)
            v.nop().then_inc(sig_done, 2)
            v.nop().then_inc(decayed, 1)
            v.nop().then_inc(y_read, 1)
            v.nop().then_inc(rooted, 1)
            dve.wait_ge(dt_split, 1)
            v.tensor_tensor(wdt_low[:], wdt[:], wdt_high[:].bitcast(F32), ALU.subtract).then_inc(dt_low, 1)
            dve.wait_ge(dt_low, 2)
            dve.wait_ge(consts, 64)
            chain.after(v.tensor_tensor(dtx[:], ps_turn[:, 0:NC * SSD_HEADS].rearrange("p (c h) -> p c h", c=NC),
                                        dt_bias[:].unsqueeze(1).to_broadcast([P, NC, SSD_HEADS]), ALU.add))
            chain.after(v.tensor_scalar(dte[:], dtx[:], -1.0, None, ALU.mult))
            v.tensor_tensor(dte[:], dte[:], dtx[:], ALU.max).then_inc(dt_sum, 1)
            dve.wait_ge(dt_exp, 1)
            v.tensor_scalar(dtw[:], dte[:], 1.0, None, ALU.add).then_inc(dt_ln, 1)
            dve.wait_ge(dt_ln, 1)
            chain.after(v.tensor_scalar(dt[:], dtw[:], -1.0, None, ALU.add))
            chain.after(v.tensor_tensor(dte[:], dte[:], dt[:], ALU.subtract))
            dve.wait_ge(dt_exp, 2)
            chain.after(v.reciprocal(dtw[:], dtw[:]))
            chain.after(v.tensor_tensor(dte[:], dte[:], dtw[:], ALU.mult))
            chain.after(v.tensor_tensor(dtl[:], dtl[:], dte[:], ALU.add))
            chain.after(v.scalar_tensor_tensor(dt[:], dtx[:], 0.0, dtl[:], ALU.max, ALU.add))
            chain.after(v.scalar_tensor_tensor(adt[:], dt[:], -1.0,
                                               a_log[:].unsqueeze(1).to_broadcast([P, NC, SSD_HEADS]),
                                               ALU.mult, ALU.mult))
            dve.wait_ge(y_stored, 32)

            def convolve(u, s):
                src, dst = acc[s % 2], conv[:, s]
                w = lambda j: conv_w[:, ds(u * 4 * (CONV + 1) + s * (CONV + 1) + j, 1)]
                dve.wait_ge(ring.used, ring.base + SSD_TILES * u + s + 3)
                chain.after(v.tensor_scalar(dst, src[:], w(CONV - 1), w(CONV), ALU.mult, ALU.add))
                for back in range(1, CONV):
                    ins = v.scalar_tensor_tensor(dst[:, back:], src[:, :T - back], w(CONV - 1 - back),
                                                 dst[:, back:], ALU.mult, ALU.add)
                    if back < CONV - 1:
                        chain.after(ins)
                ins.then_inc(acc_read, 1)

            def sigmoid(u, s):
                dve.wait_ge(tanh_done, SSD_TILES * u + s + 1)
                v.tensor_scalar(sig[:, s], half_tanh[:, s % 2], 1.0, 0.5, ALU.add, ALU.mult).then_inc(sig_done, 1)

            def take_z(u, s):
                dve.wait_ge(tanh_done, SSD_TILES * u + s + 1)
                v.tensor_copy(conv[:, s], acc[s % 2][:]).then_inc(acc_read, 1)

            def take_x(p, t):
                dve.wait_ge(turned, 3 * p + t + 1)
                v.tensor_tensor(xdt[:, :, t * P:(t + 1) * P].rearrange("p c (h d) -> p c h d", h=2),
                                ps_turn[:].rearrange("p (c h d) -> p c h d", c=NC, h=2),
                                dt[:, :, ds(HPG * p + 2 * t, 2)].unsqueeze(3).to_broadcast([P, NC, 2, HD]),
                                ALU.mult).then_inc(turned_read, 1)

            def make_steps(p, c):
                v.tensor_tensor(steps[:], const["upto"].unsqueeze(1).to_broadcast([P, HPG, CH]),
                                adt[:, c, ds(HPG * p, HPG)].unsqueeze(2).to_broadcast([P, HPG, CH]),
                                ALU.mult).then_inc(steps_ready, 1)

            def next_state(p, c):
                dve.wait_ge(b_done, NC * p + c + 1)
                new = ps_state[:].rearrange("p (h d) -> p h d", h=HPG)
                if c == 0:
                    v.tensor_copy(state[:], new).then_inc(state_ready, 1)
                else:
                    chain.after(v.tensor_tensor(state[:], state[:],
                                                chunk_dec[:].unsqueeze(2).to_broadcast([P, HPG, HD]), ALU.mult))
                    v.tensor_tensor(state[:], state[:], new, ALU.add).then_inc(state_ready, 1)

            def mix(p, c):
                dve.wait_ge(decayed, NC * p + c + 2)
                if c > 0:
                    dve.wait_ge(mixed_ready, NC * p + c)
                chain.after(v.tensor_tensor(scores[:], ps_turn[:, 0:CH], const["upto"], ALU.mult))
                v.tensor_tensor(mixed[:], decay[:], scores[:].unsqueeze(1).to_broadcast([P, HPG, CH]), ALU.mult)
                if c < NC - 1:
                    v.tensor_tensor(x_dec[:], xdt[:, c].rearrange("p (h d) -> p h d", h=HPG),
                                    decay[:, :, CH - 1:CH].to_broadcast([P, HPG, HD]), ALU.mult)
                    v.tensor_copy(chunk_dec[:], decay0[:, :, CH - 1])
                v.tensor_tensor(c_dec[:], decay0[:],
                                act_in[:, 3, c * CH:(c + 1) * CH].unsqueeze(1).to_broadcast([P, HPG, CH]),
                                ALU.mult).then_inc(mixed_ready, 1)

            def body(u, proj, comp, fin):
                p, f = u - 1, u - 2
                for s in range(SSD_TILES):
                    if s == 0:
                        if fin:
                            dve.wait_ge(b_done, NC * f + NC)
                            for t in range(2):
                                ins = v.scalar_tensor_tensor(y[:, t], act_in[:, t], d_col[:, ds(2 * f + t, 1)],
                                                             ps_y[t][:], ALU.mult, ALU.add)
                            ins.then_inc(y_read, 1)
                            dve.wait_ge(y_read, f + 2)
                            v.tensor_tensor(y[:], y[:], act_in[:, 4:6], ALU.mult).then_inc(gated, 1)
                        if comp:
                            dve.wait_ge(sig_done, SSD_TILES * p + SSD_TILES + 2)
                            if fin:
                                dve.wait_ge(gated, f + 1)
                            v.tensor_tensor(act_in[:], conv[:], sig[:], ALU.mult).then_inc(in_ready, 1)
                            dve.wait_ge(in_ready, p + 1)
                        if proj:
                            convolve(u, 0)
                        if comp:
                            take_x(p, 0)
                            make_steps(p, 0)
                    if s == 1:
                        if proj:
                            convolve(u, 1)
                            sigmoid(u, 0)
                        if comp:
                            take_x(p, 1)
                        if fin:
                            dve.wait_ge(rooted, f + 2)
                            dve.wait_ge(y_stored, 32 * f + 32)
                            for t in range(2):
                                ins = v.scalar_tensor_tensor(y_norm[:, t], y[:, t], norm_w[:, ds(2 * f + t, 1)],
                                                             rstd[:], ALU.mult, ALU.mult)
                            ins.then_inc(y_ready, 1)
                    if s == 2:
                        if proj:
                            convolve(u, 2)
                            sigmoid(u, 1)
                        if comp:
                            dve.wait_ge(turned, 3 * p + 3)
                            v.tensor_copy(b_tok[:].rearrange("p c n -> p (c n)"), ps_turn[:]).then_inc(turned_read, 1)
                            mix(p, 0)
                            make_steps(p, 1)
                    if s >= 3:
                        if proj:
                            sigmoid(u, s - 1)
                            if s == 3:
                                convolve(u, s)
                            else:
                                take_z(u, s)
                        if comp:
                            next_state(p, s - 3)
                            mix(p, s - 2)
                            if s < SSD_TILES - 1:
                                make_steps(p, s - 1)
                if proj:
                    sigmoid(u, SSD_TILES - 1)

            body(0, True, False, False)
            body(1, True, True, False)
            with dve.Fori(2, G) as u:
                chain.enter(u - 2, 4 * 3 + 4 + 2)
                body(u, True, True, True)
            chain.leave(G - 2)
            body(G, False, True, True)
            body(G + 1, False, False, True)
    ring.base += G * SSD_TILES



def hg_stage(nc, dram, ring, h, const, y_out, following):
    H = HG_HEADS
    L7, L8, LK, LQ = LEVELS, LEVELS + 1, LEVELS + 2, LEVELS + 3
    with ExitStack() as ctx:
        sb = lambda n, s, dt=F32: ctx.enter_context(nc.sbuf_tensor(f"sb_hg_{n}", s, dt))
        ps = lambda n, s: ctx.enter_context(nc.psum_tensor(f"hg_{n}", s, F32))
        sem = ctx.enter_context(semaphores(nc, "hg"))
        mask = sb("mask", [P, LEVELS + 1, CH])
        lb = sb("lb", [P, 2, KT])
        lb_in = sb("lb_in", [P, 2, KT])
        lb_max = sb("lb_max", [P, KT])
        norm_w = sb("norm_w", [P, 1])
        f = sb("f", [P, T])
        k = sb("k", [P, T])
        q = sb("q", [P, T])
        v = sb("v", [P, T])
        og = sb("og", [P, T])
        sg = sb("sg", [P, T])
        b = sb("b", [P, T])
        lev = sb("lev", [P, LEVELS + 4, T])
        qe = sb("qe", [P, T])
        k_end = sb("k_end", [P, NC])
        v_tok = sb("v_tok", [P, NC, P])
        k_tok = sb("k_tok", [P, NC, P])
        masked = sb("masked", [P, LEVELS + 1, CH])
        probs = sb("probs", [P, 2, CH])
        state = sb("state", [P, P])
        o_sq = sb("o_sq", [P, T])
        rstd = sb("rstd", [P, T])
        o_norm = sb("o_norm", [P, T])

        acc = [ps(f"acc{i}", [P, T]) for i in range(2)]
        ps_lev = ps("ps_lev", [P, LEVELS + 1, CH])
        ps_o = ps("ps_o", [P, T])
        ps_state = ps("ps_state", [P, P])
        ps_v = ps("ps_v", [P, T])
        ps_k = ps("ps_k", [P, T])

        consts = sem("consts")
        lb_step = sem("lb_step")
        acc_read = sem("acc_read")
        f_exp, q_exp, g_exp, f_ready, f_log, b_ready = (
            sem(n) for n in ("f_exp", "q_exp", "g_exp", "f_ready", "f_log", "b_ready"))
        turned = sem("turned")
        turned_read = sem("turned_read")
        lev_diff = sem("lev_diff")
        lev_exp = sem("lev_exp")
        lev_ready = sem("lev_ready")
        a_done = sem("a_done")
        a_read = sem("a_read")
        probs_ready = sem("probs_ready")
        b_done = sem("b_done")
        state_ready = sem("state_ready")
        squared, summed, rooted = sem("squared"), sem("summed"), sem("rooted")
        o_ready = sem("o_ready")
        o_stored = sem("o_stored")
        act_done, vec_done = sem("act_done"), sem("vec_done")
        block = ctx.enter_context(nc.Block())

        @block.sync
        def _(sp):
            sp.dma_start(mask[:], dram["level_mask"]).then_inc(consts, 16)
            sp.dma_start(lb_in[:], dram["hg_lb"]).then_inc(consts, 16)
            sp.dma_start(norm_w[:], dram["hg_norm_w"]).then_inc(o_stored, 16)
            for s in range(2, HG_TILES):
                load_tile(sp, ring, s % 2, dram["w_hg"][s], s)

            def store(p):
                sp.wait_ge(o_ready, p + 2)
                sp.dma_start(one(y_out[ds(p, 1)]), o_norm[:]).then_inc(o_stored, 16)

            for s in range(HG_TILES):
                load_tile(sp, ring, s % 2, dram["w_hg"][HG_TILES + s], HG_TILES + s)
            with sp.Fori(2, H) as u:
                for s in range(HG_TILES):
                    n = HG_TILES * u + s
                    load_tile(sp, ring, s % 2, one(dram["w_hg"][ds(n, 1)]), n)
                store(u - 2)
            load_ahead(sp, ring, H * HG_TILES, following)
            store(H - 2)
            store(H - 1)
            sp.wait_ge(o_stored, 16 + 16 * H)

        @block.gpsimd
        def _(pool):
            split_low_all(nc, pool, ring, H * HG_TILES)

        @block.scalar
        def _(act):
            chain = Chain(act, act_done)
            nc.scalar.preload_act_table_set(EXP_LN_SET)
            act.wait_ge(lb_step, 1)
            nc.scalar.activation(lb_in[:], lb_in[:], ACT.Exp).then_inc(lb_step, 1)

            def body(u, proj, comp):
                p = u - 1
                for s in range(HG_TILES):
                    n = HG_TILES * u + s
                    if proj:
                        split_high(nc, act, ring, (s + 1) % 2, n + 1, 2 * u + (s + 1) // 2)
                    if s == 0 and proj:
                        act.wait_ge(ring.used, ring.base + n + 3)
                        act.wait_ge(lev_ready, u + 1)
                        nc.scalar.activation(f[:], acc[0][:], ACT.Exp, scale=-1.0).then_inc(f_exp, 1)
                        act.wait_ge(f_ready, u + 1)
                        nc.scalar.activation(b[:], f[:], ACT.Ln).then_inc(f_log, 1)
                    if s == 1 and proj:
                        act.wait_ge(ring.used, ring.base + n + 3)
                        nc.scalar.activation(sg[:], acc[1][:], ACT.Exp, scale=-1.0).then_inc(q_exp, 1)
                    if s == 2:
                        if proj:
                            act.wait_ge(lev_diff, u + 1)
                            nc.scalar.activation(lev[:, 0:LK], lev[:, 0:LK], ACT.Exp).then_inc(lev_exp, 1)
                        if comp:
                            act.wait_ge(b_done, NC * p + NC)
                            nc.scalar.activation(o_sq[:], ps_o[:], ACT.Square).then_inc(squared, 1)
                    if s == 3:
                        if comp:
                            act.wait_ge(summed, p + 1)
                            chain.after(nc.scalar.activation(rstd[:], ps_k[:], ACT.Ln, bias=const["eps"],
                                                             scale=1.0 / P))
                            nc.scalar.activation(rstd[:], rstd[:], ACT.Exp, scale=-0.5).then_inc(rooted, 1)
                        if proj:
                            act.wait_ge(ring.used, ring.base + n + 3)
                            act.wait_ge(acc_read, HG_TILES * u + 4)
                            nc.scalar.activation(sg[:], acc[1][:], ACT.Exp, scale=-1.0).then_inc(g_exp, 1)

            body(0, True, False)
            with act.Fori(1, H) as u:
                chain.enter(u - 1, 1)
                body(u, True, True)
            chain.leave(H - 1)
            body(H, False, True)

        @block.tensor
        def _(pe):

            def turn(dst, src):
                for c in range(NC):
                    last = nc.tensor.transpose(dst[:, c * P:(c + 1) * P], src[:, c * CH:(c + 1) * CH],
                                               const["ident"])
                last.then_inc(turned, 1)

            def part_a(p, c):
                pe.wait_ge(a_read, NC * p + c + 1)
                tok = slice(c * CH, (c + 1) * CH)
                for l in range(LEVELS):
                    nc.tensor.matmul(ps_lev[:, l], lev[:, l, tok], lev[:, l, tok], start=True, stop=True)
                nc.tensor.matmul(ps_lev[:, LEVELS], lev[:, LK, tok], lev[:, LQ, tok],
                                 start=True, stop=True).then_inc(a_done, 1)

            def part_b(p, c):
                tok = slice(c * CH, (c + 1) * CH)
                pe.wait_ge(probs_ready, NC * p + c + 1)
                if c == 0:
                    pe.wait_ge(o_ready, p + 1)
                    pe.wait_ge(turned_read, 2 * p + 2)
                last = nc.tensor.matmul(ps_o[:, tok], v_tok[:, c], probs[:, c % 2], start=True, stop=(c == 0))
                if c > 0:
                    pe.wait_ge(state_ready, (NC - 1) * p + c)
                    last = nc.tensor.matmul(ps_o[:, tok], state[:], qe[:, tok], start=False, stop=True)
                if c < NC - 1:
                    last = nc.tensor.matmul(ps_state[:], k_tok[:, c], v_tok[:, c], start=True, stop=True)
                last.then_inc(b_done, 1)

            def body(u, proj, comp):
                p = u - 1
                for s in range(HG_TILES):
                    n = HG_TILES * u + s

                    def half(i):
                        if not proj:
                            return
                        if i == 0:
                            pe.wait_ge(ring.low_ready, ring.base + n + 1)
                            pe.wait_ge(acc_read, n + 1)
                        last = product(nc, acc[s % 2][:], ring.high[:, s % 2], ring.low[:, s % 2], h[0], h[1],
                                       range(i * KT // 2, (i + 1) * KT // 2))
                        if i == 1:
                            last.then_inc(ring.used, 1)

                    half(0)
                    if comp:
                        if s == 0:
                            pe.wait_ge(lev_ready, p + 2)
                            turn(ps_v, v)
                            pe.wait_ge(rooted, p + 1)
                            turn(ps_k, lev[:, L8])
                            part_a(p, 0)
                        if s == 1:
                            part_b(p, 0)
                            part_a(p, 2)
                        if s == 2:
                            part_b(p, 2)
                        if s == 3:
                            pe.wait_ge(squared, p + 1)
                            nc.tensor.matmul(ps_k[:], const["ones"], o_sq[:], start=True, stop=True).then_inc(summed, 1)
                    half(1)
                    if comp:
                        if s == 0:
                            part_a(p, 1)
                        if s == 1:
                            part_b(p, 1)
                            part_a(p, 3)
                        if s == 2:
                            part_b(p, 3)

            body(0, True, False)
            with pe.Fori(1, H) as u:
                body(u, True, True)
            body(H, False, True)

        @block.vector
        def _(dve):
            chain = Chain(dve, vec_done)
            vec = nc.vector
            vec.nop().then_inc(acc_read, 2)
            vec.nop().then_inc(a_read, 1)
            vec.nop().then_inc(o_ready, 1)
            vec.nop().then_inc(rooted, 1)
            vec.nop().then_inc(lev_ready, 1)
            dve.wait_ge(consts, 32)
            dve.wait_ge(o_stored, 16)
            chain.after(vec.tensor_tensor(lb_max[:], lb_in[:, 0], lb_in[:, 1], ALU.max))
            vec.tensor_tensor(lb_in[:], lb_in[:], lb_max[:].unsqueeze(1).to_broadcast([P, 2, KT]),
                              ALU.subtract).then_inc(lb_step, 1)
            dve.wait_ge(lb_step, 2)
            chain.after(vec.tensor_tensor(lb_max[:], lb_in[:, 0], lb_in[:, 1], ALU.add))
            chain.after(vec.reciprocal(lb_max[:], lb_max[:]))
            chain.after(vec.tensor_tensor(lb[:, 0], lb_in[:, 0], lb_max[:], ALU.mult))
            chain.after(vec.tensor_scalar(lb[:, 1], lb[:, 0], -1.0, 1.0, ALU.mult, ALU.add))

            def take_f(u):
                dve.wait_ge(f_exp, u + 1)
                ins = vec.tensor_scalar(sg[:], f[:], 1.0, None, ALU.add)
                ins.then_inc(acc_read, 1)
                dve.wait_ge(acc_read, HG_TILES * u + 3)
                chain.after(vec.reciprocal(sg[:], sg[:]))
                vec.tensor_scalar(f[:], sg[:], lb[:, 1, ds(u, 1)], lb[:, 0, ds(u, 1)],
                                  ALU.mult, ALU.add).then_inc(f_ready, 1)
                dve.wait_ge(f_ready, u + 1)
                chain.after(vec.tensor_scalar(k[:], f[:], -1.0, 1.0, ALU.mult, ALU.add))
                dve.wait_ge(f_log, u + 1)
                for c in range(NC):
                    tok = slice(c * CH, (c + 1) * CH)
                    ins = vec.tensor_tensor_scan(b[:, tok], const["ones"][:, 0:CH], b[:, tok], 0.0,
                                                 ALU.mult, ALU.add)
                ins.then_inc(b_ready, 1)

            def swish(dst, src, exp_done, value, taken):
                dve.wait_ge(exp_done, value)
                chain.after(vec.tensor_scalar(sg[:], sg[:], 1.0, None, ALU.add))
                chain.after(vec.reciprocal(sg[:], sg[:]))
                vec.tensor_tensor(dst[:], src[:], sg[:], ALU.mult).then_inc(acc_read, 1)
                dve.wait_ge(acc_read, taken)

            def take_probs(p, c):
                dve.wait_ge(a_done, NC * p + c + 1)
                if c > 0:
                    dve.wait_ge(probs_ready, NC * p + c)
                vec.tensor_tensor(masked[:], ps_lev[:], mask[:], ALU.mult).then_inc(a_read, 1)
                dve.wait_ge(a_read, NC * p + c + 2)
                vec.tensor_reduce(probs[:, c % 2], masked[:].rearrange("p l t -> p t l"), AX_X,
                                  ALU.add).then_inc(probs_ready, 1)

            def next_state(p, c):
                dve.wait_ge(b_done, NC * p + c + 1)
                if c == 0:
                    vec.tensor_copy(state[:], ps_state[:]).then_inc(state_ready, 1)
                else:
                    vec.scalar_tensor_tensor(state[:], state[:], k_end[:, c:c + 1], ps_state[:],
                                             ALU.mult, ALU.add).then_inc(state_ready, 1)

            def exponents(u):
                dve.wait_ge(b_ready, u + 1)
                for l, w in enumerate(HALVES):
                    halves = lambda x: x.rearrange("p (n a w) -> p n a w", a=2, w=w)
                    src, dst = halves(b[:]), halves(lev[:, l])
                    n = T // (2 * w)
                    ref = src[:, :, 0, w - 1:w].to_broadcast([P, n, w])
                    vec.tensor_tensor(dst[:, :, 1, :], src[:, :, 1, :], ref, ALU.subtract)
                    vec.tensor_tensor(dst[:, :, 0, :], ref, src[:, :, 0, :], ALU.subtract)
                vec.tensor_copy(lev[:, L7], b[:])
                chunks = lambda x: x.rearrange("p (c t) -> p c t", c=NC)
                vec.tensor_tensor(chunks(lev[:, L8]), chunks(b[:])[:, :, CH - 1:CH].to_broadcast([P, NC, CH]),
                                  chunks(b[:]), ALU.subtract).then_inc(lev_diff, 1)

            def weigh(u, p, comp):
                dve.wait_ge(lev_exp, u + 1)
                for l, w in enumerate(HALVES):
                    halves = lambda x: x.rearrange("p (n a w) -> p n a w", a=2, w=w)
                    dst = halves(lev[:, l])
                    vec.tensor_tensor(dst[:, :, 1, :], dst[:, :, 1, :], halves(q[:])[:, :, 1, :], ALU.mult)
                    vec.tensor_tensor(dst[:, :, 0, :], dst[:, :, 0, :], halves(k[:])[:, :, 0, :], ALU.mult)
                vec.tensor_copy(lev[:, LK], k[:])
                vec.tensor_copy(lev[:, LQ], q[:])
                if comp:
                    dve.wait_ge(b_done, NC * p + NC)
                vec.tensor_tensor(qe[:], lev[:, L7], q[:], ALU.mult)
                vec.tensor_copy(k_end[:], lev[:, L7].rearrange("p (c t) -> p c t", c=NC)[:, :, CH - 1])
                vec.tensor_tensor(lev[:, L8], lev[:, L8], k[:], ALU.mult).then_inc(lev_ready, 1)
                dve.wait_ge(lev_ready, u + 2)

            def body(u, proj, comp):
                p = u - 1
                n = HG_TILES * u
                if comp:
                    dve.wait_ge(turned, 2 * p + 1)
                    vec.tensor_copy(v_tok[:].rearrange("p c v -> p (c v)"), ps_v[:]).then_inc(turned_read, 1)
                    dve.wait_ge(turned, 2 * p + 2)
                    vec.tensor_copy(k_tok[:].rearrange("p c v -> p (c v)"), ps_k[:]).then_inc(turned_read, 1)
                    take_probs(p, 0)
                    take_probs(p, 1)
                if proj:
                    take_f(u)
                if comp:
                    next_state(p, 0)
                    take_probs(p, 2)
                    next_state(p, 1)
                    take_probs(p, 3)
                if proj:
                    swish(q, acc[1], q_exp, u + 1, n + 4)
                    exponents(u)
                    dve.wait_ge(ring.used, ring.base + n + 5)
                    vec.tensor_copy(v[:], acc[0][:]).then_inc(acc_read, 1)
                if comp:
                    next_state(p, 2)
                if proj:
                    weigh(u, p, comp)
                if comp:
                    dve.wait_ge(rooted, p + 2)
                    dve.wait_ge(o_stored, 16 * p + 16)
                    chain.after(vec.scalar_tensor_tensor(o_norm[:], ps_o[:], norm_w[:, 0:1], rstd[:],
                                                         ALU.mult, ALU.mult))
                    vec.tensor_tensor(o_norm[:], o_norm[:], og[:], ALU.mult).then_inc(o_ready, 1)
                    dve.wait_ge(o_ready, p + 2)
                if proj:
                    swish(og, acc[1], g_exp, u + 1, n + 6)

            body(0, True, False)
            with dve.Fori(1, H) as u:
                chain.enter(u - 1, 2 + 2 + 1 + 2)
                body(u, True, True)
            chain.leave(H - 1)
            body(H, False, True)
    ring.base += H * HG_TILES



def mix_stage(nc, name, w, ring, h, y_src, prior, dst, following):
    with ExitStack() as ctx:
        sb = lambda n, s, dt=F32: ctx.enter_context(nc.sbuf_tensor(f"sb_{name}_{n}", s, dt))
        ps = lambda n, s: ctx.enter_context(nc.psum_tensor(f"{name}_{n}", s, F32))
        sem = ctx.enter_context(semaphores(nc, name))
        PIECE = 4
        y_raw = sb("y_raw", [P, 2, PIECE, T])
        y_high = sb("y_high", [P, KT, T], F32R)
        y_low = sb("y_low", [P, KT, T], F32R)
        expo = sb("expo", [P, T])
        gate = sb("gate", [P, T])
        mixed = sb("mixed", [P, T])
        before = sb("before", [P, T])
        acc = [ps(f"acc{i}", [P, T]) for i in range(2)]
        y_landed = [sem("y_landed0"), sem("y_landed1")]
        y_high_ready, y_low_ready = sem("y_high_ready"), sem("y_low_ready")
        gate_exp, gate_ready = sem("gate_exp"), sem("gate_ready")
        mixed_ready, stored, before_landed, vec_done = (
            sem("mixed_ready"), sem("stored"), sem("before_landed"), sem("vec_done"))
        block = ctx.enter_context(nc.Block())

        @block.sync
        def _(sp):
            for i in range(KT // PIECE):
                if i >= 2:
                    sp.wait_ge(y_low_ready, i - 1)
                sp.dma_start(y_raw[:, i % 2], y_src[i * PIECE:(i + 1) * PIECE].rearrange("k p t -> p k t")
                             ).then_inc(y_landed[i % 2], 16)

            def rest(n, load):
                if load:
                    for s in range(2):
                        load_tile(sp, ring, s, one(w[ds(2 * n + 2 + s, 1)]), 2 * n + 2 + s)
                if prior is not None:
                    sp.dma_start(before[:], one(prior[ds(n, 1)])).then_inc(before_landed, 16)
                sp.wait_ge(mixed_ready, n + 1)
                sp.dma_start(one(dst[ds(n, 1)]), mixed[:]).then_inc(stored, 16)

            with sp.Fori(0, KT - 1) as n:
                rest(n, True)
            load_ahead(sp, ring, 2 * KT, following)
            rest(KT - 1, False)
            sp.wait_ge(stored, 16 * KT)

        @block.gpsimd
        def _(pool):
            split_low_all(nc, pool, ring, 2 * KT)

        @block.scalar
        def _(act):
            for i in range(KT // PIECE):
                act.wait_ge(y_landed[i % 2], 16 * (i // 2) + 16)
                nc.scalar.activation(y_high[:, i * PIECE:(i + 1) * PIECE], y_raw[:, i % 2],
                                     ACT.Copy).then_inc(y_high_ready, 1)

            with act.Fori(0, KT) as n:
                split_high(nc, act, ring, 1, 2 * n + 1, n)
                act.wait_ge(ring.used, ring.base + 2 * n + 3)
                act.wait_ge(gate_ready, n + 1)
                nc.scalar.activation(expo[:], acc[0][:], ACT.Exp, scale=-1.0).then_inc(gate_exp, 1)
                split_high(nc, act, ring, 0, 2 * n + 2, n + 1)

        @block.tensor
        def _(pe):

            def body(n, first):
                pe.wait_ge(ring.low_ready, ring.base + 2 * n + 1)
                if not first:
                    pe.wait_ge(gate_exp, n)
                product(nc, acc[0][:], ring.high[:, 0], ring.low[:, 0], h[0], h[1]).then_inc(ring.used, 1)
                pe.wait_ge(ring.low_ready, ring.base + 2 * n + 2)
                if first:
                    pe.wait_ge(y_low_ready, KT // PIECE)
                else:
                    pe.wait_ge(mixed_ready, n)
                product(nc, acc[1][:], ring.high[:, 1], ring.low[:, 1], y_high, y_low).then_inc(ring.used, 1)

            body(0, True)
            with pe.Fori(1, KT) as n:
                body(n, False)

        @block.vector
        def _(dve):
            chain = Chain(dve, vec_done)
            nc.vector.nop().then_inc(gate_ready, 1)
            for i in range(KT // PIECE):
                dve.wait_ge(y_high_ready, i + 1)
                piece = slice(i * PIECE, (i + 1) * PIECE)
                nc.vector.tensor_tensor(y_low[:, piece], y_raw[:, i % 2], y_high[:, piece].bitcast(F32),
                                        ALU.subtract).then_inc(y_low_ready, 1)

            def body(n, first):
                dve.wait_ge(gate_exp, n + 1)
                if not first:
                    dve.wait_ge(mixed_ready, n)
                nc.vector.tensor_scalar(gate[:], expo[:], 1.0, None, ALU.add).then_inc(gate_ready, 1)
                dve.wait_ge(gate_ready, n + 2)
                chain.after(nc.vector.reciprocal(gate[:], gate[:]))
                dve.wait_ge(ring.used, ring.base + 2 * n + 4)
                if not first:
                    dve.wait_ge(stored, 16 * n)
                product_done = nc.vector.tensor_tensor(mixed[:], acc[1][:], gate[:], ALU.mult)
                if prior is None:
                    product_done.then_inc(mixed_ready, 1)
                else:
                    chain.after(product_done)
                    dve.wait_ge(before_landed, 16 * n + 16)
                    nc.vector.tensor_tensor(mixed[:], mixed[:], before[:], ALU.add).then_inc(mixed_ready, 1)

            body(0, True)
            with dve.Fori(1, KT) as n:
                chain.enter(n - 1, 1 if prior is None else 2)
                body(n, False)
    ring.base += 2 * KT



def out_stage(nc, dram, ring, m, mix, x_mid, following):
    with ExitStack() as ctx:
        sb = lambda n, s, dt=F32: ctx.enter_context(nc.sbuf_tensor(f"sb_out_{n}", s, dt))
        sem = ctx.enter_context(semaphores(nc, "out"))
        PIECE = 4
        raw = sb("raw_mix", [P, 2, PIECE, T])
        m_high, m_low = m
        acc = [ctx.enter_context(nc.psum_tensor(f"out_acc{i}", [P, T], F32)) for i in range(2)]
        landed = [sem("mix_landed0"), sem("mix_landed1")]
        x_landed, m_high_ready, m_low_ready, added = (sem("x_landed"), sem("m_high_ready"),
                                                      sem("m_low_ready"), sem("added"))
        w = dram["w_out"]
        block = ctx.enter_context(nc.Block())

        @block.sync
        def _(sp):
            for i in range(KT // PIECE):
                if i >= 2:
                    sp.wait_ge(m_low_ready, i - 1)
                sp.dma_start(raw[:, i % 2], mix[i * PIECE:(i + 1) * PIECE].rearrange("k p t -> p k t")
                             ).then_inc(landed[i % 2], 16)
            sp.dma_start(x_mid[:], dram["x_t"]).then_inc(x_landed, 16)
            with sp.Fori(1, KT // 2) as i:
                for s in range(2):
                    load_tile(sp, ring, s, one(w[ds(2 * i + s, 1)]), 2 * i + s)
            load_ahead(sp, ring, KT, following)

        @block.gpsimd
        def _(pool):
            split_low_all(nc, pool, ring, KT)

        @block.scalar
        def _(act):
            for i in range(KT // PIECE):
                act.wait_ge(landed[i % 2], 16 * (i // 2) + 16)
                nc.scalar.activation(m_high[:, i * PIECE:(i + 1) * PIECE], raw[:, i % 2],
                                     ACT.Copy).then_inc(m_high_ready, 1)
            with act.Fori(0, KT // 2) as i:
                for n in (1, 2):
                    split_high(nc, act, ring, n % 2, 2 * i + n, i + n // 2)

        @block.tensor
        def _(pe):
            pe.wait_ge(m_low_ready, KT // PIECE)
            with pe.Fori(0, KT // 2) as i:
                for s in range(2):
                    pe.wait_ge(ring.low_ready, ring.base + 2 * i + (s + 1))
                    pe.wait_ge(added, 2 * i + (s + 1))
                    product(nc, acc[s][:], ring.high[:, s], ring.low[:, s], m_high, m_low).then_inc(ring.used, 1)

        @block.vector
        def _(dve):
            nc.vector.nop().then_inc(added, 2)
            for i in range(KT // PIECE):
                dve.wait_ge(m_high_ready, i + 1)
                piece = slice(i * PIECE, (i + 1) * PIECE)
                nc.vector.tensor_tensor(m_low[:, piece], raw[:, i % 2], m_high[:, piece].bitcast(F32),
                                        ALU.subtract).then_inc(m_low_ready, 1)
            dve.wait_ge(x_landed, 16)
            with dve.Fori(0, KT // 2) as i:
                for s in range(2):
                    dve.wait_ge(ring.used, ring.base + 2 * i + (s + 3))
                    x = x_mid[:, ds(2 * i + s, 1)].rearrange("p a t -> p (a t)")
                    nc.vector.tensor_tensor(x, x, acc[s][:], ALU.add).then_inc(added, 1)
    ring.base += KT



def route_stage(nc, dram, ring, h, const, scratch):
    with ExitStack() as ctx:
        sb = lambda n, s, dt=F32: ctx.enter_context(nc.sbuf_tensor(f"sb_rt_{n}", s, dt))
        ps = lambda n, s: ctx.enter_context(nc.psum_tensor(f"rt_{n}", s, F32))
        sem = ctx.enter_context(semaphores(nc, "rt"))
        QUERY = KT
        PAIRS = KEYS // 2
        GROUP = 4
        BANKS = 4
        BLOCK_TURNS = GT // GROUP // BANKS
        GATE_PAIRS = T // GROUP // BANKS
        FREE_PAIRS = 12

        table = sb("table", [P, 2, KEYS, GT])
        hot1 = sb("hot1", [P, BANKS, GROUP, KEYS])
        hot2 = sb("hot2", [P, BANKS, GROUP, KEYS])
        place = sb("place", [P, 2, T])
        gate_t = sb("gate_t", [P, T])
        gelu = sb("gelu", [P, 2, T])
        count = sb("count", [P, P])
        spare = table[:, 1].rearrange("p j t -> p (j t)")
        at = [0]

        def carve(*shape):
            n = int(np.prod(shape))
            at[0] += n
            assert at[0] <= KEYS * GT
            names = "abcde"[:len(shape)]
            return spare[:, at[0] - n:at[0]].rearrange(
                f"p ({' '.join(names)}) -> p {' '.join(names)}", **dict(zip(names, shape)))

        keys = carve(KT, KEYS)
        query = carve(2, T)
        score = carve(2, NC, KEYS)
        top = carve(2, NC, TOPK)
        top_at = carve(2, NC, TOPK).bitcast(U32)
        top_key = carve(2, NC, TOPK)
        pair = carve(NC, TOPK, TOPK)
        best_at = carve(NC, TOPK).bitcast(U32)
        half_at = carve(NC, TOPK).bitcast(U32)
        half_pos = carve(NC, TOPK)
        hit = pair
        best = carve(NC, PEER_HEADS, TOPK)
        total = carve(NC, PEER_HEADS)
        chosen = carve(2, NC, PEER_HEADS, TOPK)

        acc = [ps(f"acc{i}", [P, T]) for i in range(2)]
        ps_score = [ps(f"score{i}", [P, NC, KEYS]) for i in range(2)]
        ps_gate = [ps(f"gate{i}", [P, T]) for i in range(BANKS)]

        acc_read = sem("acc_read")
        score_done = sem("score_done")
        score_read = sem("score_read")
        gelu_stored = [sem("gelu_stored0"), sem("gelu_stored1")]
        exp_in, exp_done, gates_ready, turned, vec_done = (
            sem(n) for n in ("exp_in", "exp_done", "gates_ready", "turned", "vec_done"))
        hot_ready = sem("hot_ready")
        made = sem("made")
        taken = sem("taken")
        table_stored = sem("table_stored")
        block = ctx.enter_context(nc.Block())

        @block.sync
        def _(sp):
            for half in range(2):
                a, b = slice(half * KT // 2, (half + 1) * KT // 2), slice(half * P // 2, (half + 1) * P // 2)
                sp.dma_start(keys[:, a], dram["sub_keys"][:, a]).then_inc(table_stored, 16)
                sp.dma_start(count[:, b], dram["count"][:, b]).then_inc(gelu_stored[half], 16)
            with sp.Fori(1, QUERY // 2) as i:
                for s in range(2):
                    load_tile(sp, ring, s, one(dram["w_query"][ds(2 * i + s, 1)]), 2 * i + s)
            for n in range(3):
                load_tile(sp, ring, n % 2, dram["u_tiles"][n], QUERY + n)

            def turn(i, loads=2):
                for s in range(2):
                    if s < loads:
                        load_tile(sp, ring, 1 - s, one(dram["u_tiles"][ds(2 * i + 3 + s, 1)]),
                                  2 * i + (QUERY + 3 + s))
                    sp.wait_ge(acc_read, 2 * i + (QUERY + s + 3))
                    sp.dma_start(one(scratch["gelu"][ds(2 * i + s, 1)]), gelu[:, s]).then_inc(gelu_stored[s], 16)

            with sp.Fori(0, FREE_PAIRS) as i:
                turn(i)
            with sp.Fori(0, T // GT // 2) as b2:
                for buf in range(2):
                    blk = 2 * b2 + buf
                    with sp.Fori(0, BLOCK_TURNS) as j:
                        turn(blk * BLOCK_TURNS + j + FREE_PAIRS)
                    sp.wait_ge(taken, blk * (GT // GROUP) + (GT // GROUP + BANKS))
                    sp.dma_start(scratch["gates"][ds(blk, 1)].rearrange("b i j t -> (b i) j t"),
                                 table[:, buf]).then_inc(table_stored, 16)
            with sp.Fori(FREE_PAIRS + GATE_PAIRS, PAIRS - 2) as i:
                turn(i)
            turn(PAIRS - 2, 1)
            turn(PAIRS - 1, 0)
            sp.wait_ge(table_stored, 16 * (T // GT + 2))
            for s in range(2):
                sp.wait_ge(gelu_stored[s], 16 * (PAIRS + 1))

        @block.gpsimd
        def _(pool):
            split_low_all(nc, pool, ring, QUERY + KEYS - 2)
            split_low(nc, pool, ring, 1, QUERY + KEYS - 1)

        @block.scalar
        def _(act):
            with act.Fori(0, QUERY // 2) as i:
                for s in range(2):
                    split_high(nc, act, ring, 1 - s, 2 * i + (s + 1), i + s)
                    act.wait_ge(ring.used, ring.base + 2 * i + (s + 3))
                    act.wait_ge(score_done, 2 * i + (s + 1))
                    nc.scalar.activation(query[:, s], acc[s][:], ACT.Copy).then_inc(acc_read, 1)

            def activate(i, s, ahead=True):
                n = 2 * i + (QUERY + s)
                if ahead:
                    split_high(nc, act, ring, 1 - s, n + 1, i + (QUERY // 2 + s))
                act.wait_ge(ring.used, ring.base + n + 3)
                act.wait_ge(gelu_stored[s], 16 * i + 16)
                nc.scalar.activation(gelu[:, s], acc[s][:], ACT.Gelu).then_inc(acc_read, 1)

            with act.Fori(0, FREE_PAIRS - 2) as i:
                for s in range(2):
                    activate(i, s)
            act.wait_ge(exp_in, 1)
            nc.scalar.activation(best, best, ACT.Exp).then_inc(exp_done, 1)
            with act.Fori(FREE_PAIRS - 2, FREE_PAIRS) as i:
                for s in range(2):
                    activate(i, s)
            with act.Fori(0, T // GT // 2) as b2:
                for buf in range(2):
                    blk = 2 * b2 + buf
                    act.wait_ge(table_stored, 16 * blk + 16)
                    with act.Fori(0, BLOCK_TURNS) as j:
                        i = blk * BLOCK_TURNS + j
                        for s in range(2):
                            activate(i + FREE_PAIRS, s)
                            for b in range(s * BANKS // 2, (s + 1) * BANKS // 2):
                                act.wait_ge(made, BANKS * i + (b + 1 + BANKS))
                                nc.scalar.activation(
                                    table[:, buf, :, ds((j * BANKS + b) * GROUP, GROUP)].rearrange("p j t -> p t j"),
                                    ps_gate[b][:].rearrange("p (t j) -> p t j", t=GROUP), ACT.Copy).then_inc(taken, 1)
            with act.Fori(FREE_PAIRS + GATE_PAIRS, PAIRS - 1) as i:
                for s in range(2):
                    activate(i, s)
            activate(PAIRS - 1, 0)
            activate(PAIRS - 1, 1, ahead=False)

        @block.tensor
        def _(pe):
            nc.tensor.nop().then_inc(score_done, 2)
            pe.wait_ge(table_stored, 32)

            def project(n, s):
                pe.wait_ge(ring.low_ready, ring.base + n + 1)
                pe.wait_ge(acc_read, n + 1)
                product(nc, acc[s][:], ring.high[:, s], ring.low[:, s], h[0], h[1]).then_inc(ring.used, 1)

            def match(n, s):
                pe.wait_ge(acc_read, n + 3)
                pe.wait_ge(score_read, n + 1)
                for c in range(NC):
                    last = nc.tensor.matmul(ps_score[s][:, c],
                                            query[:, s, c * P:(c + 1) * P],
                                            keys[:, ds(n, 1)].rearrange("p a k -> p (a k)"), start=True, stop=True)
                last.then_inc(score_done, 1)

            with pe.Fori(0, QUERY // 2) as i:
                project(2 * i, 0)
                project(2 * i + 1, 1)
                match(2 * i, 0)
                match(2 * i + 1, 1)
            with pe.Fori(0, FREE_PAIRS) as i:
                for s in range(2):
                    project(2 * i + (QUERY + s), s)
            pe.wait_ge(gates_ready, 1)
            for a, src in enumerate((chosen[:, 0], chosen[:, 1], best)):
                for c in range(NC):
                    last = nc.tensor.transpose(ps_gate[a][:, c * P:(c + 1) * P],
                                               src[:, c].rearrange("p h k -> p (h k)"), const["ident"])
            last.then_inc(turned, 1)
            with pe.Fori(0, GATE_PAIRS) as i:
                for s in range(2):
                    project(2 * i + (QUERY + 2 * FREE_PAIRS + s), s)
                    for b in range(s * BANKS // 2, (s + 1) * BANKS // 2):
                        pe.wait_ge(hot_ready, BANKS * i + (b + 1))
                        pe.wait_ge(taken, BANKS * i + (b + 1))
                        for g in range(GROUP):
                            last = nc.tensor.matmul(ps_gate[b][:, g * KEYS:(g + 1) * KEYS], hot1[:, b, g],
                                                    hot2[:, b, g], start=True, stop=True)
                        last.then_inc(made, 1)
            with pe.Fori(FREE_PAIRS + GATE_PAIRS, PAIRS) as i:
                for s in range(2):
                    project(2 * i + (QUERY + s), s)

        @block.vector
        def _(dve):
            vec = nc.vector
            chain = Chain(dve, vec_done)
            vec.nop().then_inc(acc_read, 2)
            vec.nop().then_inc(score_read, 2)
            vec.nop().then_inc(made, BANKS)
            vec.nop().then_inc(taken, BANKS)
            for s in range(2):
                dve.wait_ge(gelu_stored[s], 16)

            def top_of(dst, dst_at, src):
                for j in range(0, TOPK, 8):
                    for c in range(NC):
                        ins = vec.max(dst(c)[:, j:j + 8], src(c))
                    chain.after(ins)
                    for c in range(NC):
                        ins = vec.max_index(dst_at(c)[:, j:j + 8], dst(c)[:, j:j + 8], src(c))
                    chain.after(ins)
                    if j + 8 < TOPK:
                        for c in range(NC):
                            ins = vec.match_replace(src(c), dst(c)[:, j:j + 8], src(c), NEG)
                        chain.after(ins)

            for head in range(PEER_HEADS):
                for s in range(2):
                    dve.wait_ge(score_done, 2 * head + s + 3)
                    vec.tensor_copy(score[:, s], ps_score[s][:]).then_inc(score_read, 1)
                    dve.wait_ge(score_read, 2 * head + s + 3)
                    top_of(lambda c: top[:, s, c], lambda c: top_at[:, s, c], lambda c: score[:, s, c])
                chain.after(vec.tensor_copy(top_key, top_at))
                full = [P, NC, TOPK, TOPK]
                chain.after(vec.tensor_tensor(pair, top[:, 0].unsqueeze(3).to_broadcast(full),
                                              top[:, 1].unsqueeze(2).to_broadcast(full), ALU.add))
                top_of(lambda c: best[:, c, head], lambda c: best_at[:, c],
                       lambda c: pair[:, c].rearrange("p a b -> p (a b)"))
                for half, (op, by) in enumerate(((ALU.logical_shift_right, 4), (ALU.bitwise_and, TOPK - 1))):
                    chain.after(vec.tensor_scalar(half_at, best_at, by, None, op))
                    chain.after(vec.tensor_copy(half_pos, half_at))
                    chain.after(vec.tensor_tensor(
                        hit, half_pos.unsqueeze(3).to_broadcast(full),
                        count[:, 0:TOPK].unsqueeze(1).unsqueeze(1).to_broadcast(full), ALU.is_equal))
                    chain.after(vec.tensor_tensor(hit, hit, top_key[:, half].unsqueeze(2).to_broadcast(full),
                                                  ALU.mult))
                    chain.after(vec.tensor_reduce(chosen[:, half, :, head], hit, AX_X, ALU.add))
            flat = best.rearrange("p c h k -> p (c h) k")
            rows = total.rearrange("p c h -> p (c h)").unsqueeze(2).to_broadcast([P, NC * PEER_HEADS, TOPK])
            chain.after(vec.tensor_copy(total, best[:, :, :, 0]))
            vec.tensor_tensor(flat, flat, rows, ALU.subtract).then_inc(exp_in, 1)
            dve.wait_ge(exp_done, 1)
            chain.after(vec.tensor_reduce(total, best, AX_X, ALU.add))
            chain.after(vec.reciprocal(total, total))
            vec.tensor_tensor(flat, flat, rows, ALU.mult).then_inc(gates_ready, 1)
            dve.wait_ge(turned, 1)
            vec.tensor_copy(place[:, 0], ps_gate[0][:])
            vec.tensor_copy(place[:, 1], ps_gate[1][:])
            chain.after(vec.tensor_copy(gate_t[:], ps_gate[2][:]))
            with dve.Fori(0, GATE_PAIRS) as i:
                for b in range(BANKS):
                    dve.wait_ge(made, BANKS * i + (b + 1))
                    for g in range(GROUP):
                        t = (i * BANKS + b) * GROUP + g
                        vec.tensor_scalar(hot1[:, b, g], count[:], place[:, 0, ds(t, 1)],
                                          gate_t[:, ds(t, 1)], ALU.is_equal, ALU.mult)
                        ins = vec.tensor_scalar(hot2[:, b, g], count[:], place[:, 1, ds(t, 1)], None,
                                                ALU.is_equal)
                    ins.then_inc(hot_ready, 1)



def output_stage(nc, dram, x_mid, scratch):
    with ExitStack() as ctx:
        sb = lambda n, s, dt=F32: ctx.enter_context(nc.sbuf_tensor(f"sb_op_{n}", s, dt))
        sem = ctx.enter_context(semaphores(nc, "op"))
        N = KEYS // 2
        OUTS = 8
        raw = sb("raw", [P, 2, D])
        v_high, v_low = sb("v_high", [P, 4, D], F32R), sb("v_low", [P, 4, D], F32R)
        gelu, gate = sb("gelu", [P, 2, T]), sb("gate", [P, T // GT, 2, GT])
        w = sb("w", [P, 2, T])
        w_high, w_low = sb("w_high", [P, 4, T], F32R), sb("w_low", [P, 4, T], F32R)
        ps_out = [ctx.enter_context(nc.psum_tensor(f"op_out{i}", [P, T], F32)) for i in range(OUTS)]
        landed = [sem("landed0"), sem("landed1")]
        high_ready, low_ready = sem("high_ready"), sem("low_ready")
        x_landed, in_landed = sem("x_landed"), sem("in_landed")
        weighted = sem("weighted")
        w_split = sem("w_split")
        w_ready = sem("w_ready")
        pair_done = sem("pair_done")
        out_done = sem("out_done")
        out_added = sem("out_added")
        block = ctx.enter_context(nc.Block())

        @block.sync
        def _(sp):
            def inputs(g):
                sp.dma_start(gelu[:], scratch["gelu"][ds(2 * g, 2)].rearrange("a p t -> p a t")
                             ).then_inc(in_landed, 16)
                sp.dma_start(gate[:], scratch["gates"][:, :, ds(2 * g, 2)].rearrange("b i j t -> i b j t")
                             ).then_inc(in_landed, 16)

            for s in range(2):
                sp.dma_start(raw[:, s], dram["v_tiles"][s]).then_inc(landed[s], 16)
            inputs(0)
            sp.dma_start(x_mid[:], scratch["x_mid"]).then_inc(x_landed, 16)
            with sp.Fori(1, N) as g:
                for s in range(2):
                    sp.wait_ge(low_ready, 2 * g + s - 1)
                    sp.dma_start(raw[:, s], one(dram["v_tiles"][ds(2 * g + s, 1)])).then_inc(landed[s], 16)
                sp.wait_ge(weighted, g)
                inputs(g)

        @block.gpsimd
        def _(pool):
            with pool.Fori(0, N // 2) as g2:
                for s in range(4):
                    pool.wait_ge(high_ready, 4 * g2 + (s + 1))
                    nc.gpsimd.tensor_tensor(v_low[:, s], raw[:, s % 2], v_high[:, s].bitcast(F32),
                                            ALU.subtract).then_inc(low_ready, 1)

        @block.scalar
        def _(act):
            with act.Fori(0, N // 2) as g2:
                for s in range(4):
                    act.wait_ge(landed[s % 2], 32 * g2 + (16 * (s // 2) + 16))
                    if s % 2 == 0:
                        act.wait_ge(pair_done, 2 * g2 + (s // 2 + 1))
                    nc.scalar.activation(v_high[:, s], raw[:, s % 2], ACT.Copy).then_inc(high_ready, 1)

        @block.tensor
        def _(pe):
            nc.tensor.nop().then_inc(pair_done, 2)
            with pe.Fori(0, N // 2) as g2:
                for q in range(2):
                    pe.wait_ge(low_ready, 4 * g2 + (2 * q + 2))
                    pe.wait_ge(w_ready, 2 * g2 + (q + 1))
                    for d in range(KT):
                        pe.wait_ge(out_added, 2 * KT * g2 + (KT * q + d + 1))
                        o, m = ps_out[d % OUTS][:], slice(d * P, (d + 1) * P)
                        for s in (2 * q, 2 * q + 1):
                            nc.tensor.matmul(o, v_high[:, s, m], w_high[:, s], start=(s == 2 * q), stop=False)
                            nc.tensor.matmul(o, v_high[:, s, m], w_low[:, s], start=False, stop=False)
                            last = nc.tensor.matmul(o, v_low[:, s, m], w_high[:, s], start=False,
                                                    stop=(s == 2 * q + 1))
                        last.then_inc(out_done if d < KT - 1 else pair_done, 1)

        @block.vector
        def _(dve):
            vec = nc.vector
            vec.nop().then_inc(out_added, OUTS)

            def weights(g2, q):
                g = 2 * g2 + q
                two = slice(2 * q, 2 * q + 2)
                dve.wait_ge(in_landed, 32 * g + 32)
                vec.tensor_tensor(*(a[:].rearrange("p j (b t) -> p j b t", t=GT) for a in (w, gelu)),
                                  gate[:].rearrange("p b j t -> p j b t"), ALU.mult).then_inc(weighted, 1)
                dve.wait_ge(weighted, g + 1)
                vec.tensor_copy(w_high[:, two], w[:]).then_inc(w_split, 1)
                dve.wait_ge(w_split, g + 1)
                vec.tensor_tensor(w_low[:, two], w[:], w_high[:, two].bitcast(F32), ALU.subtract).then_inc(w_ready, 1)
                dve.wait_ge(w_ready, g + 1)

            def add_outputs(g):
                for d in range(KT):
                    if d < KT - 1:
                        dve.wait_ge(out_done, (KT - 1) * g + (d + 1))
                    else:
                        dve.wait_ge(pair_done, g + 3)
                    vec.tensor_tensor(x_mid[:, d], x_mid[:, d], ps_out[d % OUTS][:], ALU.add).then_inc(out_added, 1)

            weights(0, 0)
            weights(0, 1)
            dve.wait_ge(x_landed, 16)
            with dve.Fori(0, N // 2 - 1) as g2:
                for q in range(2):
                    add_outputs(2 * g2 + q)
                    weights(g2 + 1, q)
            for q in range(2):
                add_outputs(N - 2 + q)


def peer_front(nc, dram, ring, h, const, vecs, mix, scratch):
    with ExitStack() as tmp:
        x_mid = tmp.enter_context(nc.sbuf_tensor("x_mid_front", [P, KT, T], F32))
        out_stage(nc, dram, ring, h, mix, x_mid, dram["w_query"])
        work = tmp.enter_context(nc.sbuf_tensor("ffn_work", [P, KT, T], F32))
        norm_stage(nc, "ffn", x_mid, vecs["norm_ffn_w"], work, const["ones"], const["eps"], split=h,
                   keep=scratch["x_mid"])
    route_stage(nc, dram, ring, h, const, scratch)


def peer_back(nc, dram, const, vecs, scratch, out):
    with ExitStack() as ctx:
        x_mid = ctx.enter_context(nc.sbuf_tensor("x_mid_back", [P, KT, T], F32))
        output_stage(nc, dram, x_mid, scratch)
        work = ctx.enter_context(nc.sbuf_tensor("final_work", [P, KT, T], F32))
        norm_stage(nc, "final", x_mid, vecs["final_norm_w"], work, const["ones"], const["eps"], store=out)



SHAPES = {
    "x_t": [P, KT, T], "norm_mix_w": [P, KT], "norm_ffn_w": [P, KT], "final_norm_w": [P, KT],
    "w_ssd": [SSD_GROUPS * SSD_TILES, P, D], "w_dt": [P, KT, SSD_HEADS],
    "w_hg": [HG_HEADS * HG_TILES, P, D],
    "w_mix_s": [2 * KT, P, D], "w_mix_h": [2 * KT, P, D], "w_out": [KT, P, D], "w_query": [KT, P, D],
    "u_tiles": [KEYS, P, D], "v_tiles": [KEYS, P, D],
    "conv_w": [P, SSD_GROUPS * 4 * (CONV + 1)], "dt_bias": [P, SSD_HEADS], "a_log": [P, SSD_HEADS],
    "ssd_d": [P, KT], "ssd_norm_w": [P, KT], "hg_lb": [P, 2, KT], "hg_norm_w": [P, 1],
    "sub_keys": [P, KT, KEYS],
    "ident": [P, P], "ones": [P, P], "later": [P, P], "upto": [P, P], "level_mask": [P, LEVELS + 1, P],
    "count": [P, P],
}


def program(nc):
    dram = {n: nc.dram_tensor(n, s, F32, kind="ExternalInput").ap() for n, s in SHAPES.items()}
    out = nc.dram_tensor("out_t", [P, KT, T], F32, kind="ExternalOutput").ap()
    y_ssd = nc.dram_tensor("y_ssd", [KT, P, T], F32).ap()
    y_hg = nc.dram_tensor("y_hg", [KT, P, T], F32).ap()
    mix_s = nc.dram_tensor("mix_s", [KT, P, T], F32).ap()
    mix = nc.dram_tensor("mix", [KT, P, T], F32).ap()
    scratch = {n: nc.dram_tensor(n, s, F32).ap() for n, s in (
        ("gates", [T // GT, P, KEYS, GT]), ("gelu", [KEYS, P, T]), ("x_mid", [P, KT, T]))}
    with ExitStack() as ctx:
        sb = lambda n, s, dt=F32: ctx.enter_context(nc.sbuf_tensor(n, s, dt))
        const, eps, vecs = load_constants(nc, ctx, dram)
        with ExitStack() as rings:
            ring = Ring(nc, rings)
            h = [rings.enter_context(nc.sbuf_tensor(f"h_{n}", [P, KT, T], F32R)) for n in ("high", "low")]
            with ExitStack() as tmp:
                x = tmp.enter_context(nc.sbuf_tensor("x", [P, KT, T], F32))
                work = tmp.enter_context(nc.sbuf_tensor("x_work", [P, KT, T], F32))
                norm_stage(nc, "in", x, vecs["norm_mix_w"], work, const["ones"], const["eps"],
                           load=dram["x_t"], split=h, ring=ring, first_tiles=dram["w_ssd"])
            ssd_stage(nc, dram, ring, h, const, y_ssd, dram["w_hg"])
            hg_stage(nc, dram, ring, h, const, y_hg, dram["w_mix_s"])
            mix_stage(nc, "mix_s", dram["w_mix_s"], ring, h, y_ssd, None, mix_s, dram["w_mix_h"])
            mix_stage(nc, "mix_h", dram["w_mix_h"], ring, h, y_hg, mix_s, mix, dram["w_out"])
            peer_front(nc, dram, ring, h, const, vecs, mix, scratch)
        peer_back(nc, dram, const, vecs, scratch, out)


def load_constants(nc, ctx, dram):
    sb = lambda n, s: ctx.enter_context(nc.sbuf_tensor(n, s, F32))
    shared = {n: sb(f"c_{n}", SHAPES[n]) for n in ("ident", "ones", "later", "upto", "norm_mix_w",
                                                   "norm_ffn_w", "final_norm_w")}
    eps = sb("c_eps", [P, 1])
    landed = ctx.enter_context(nc.semaphore("c_landed"))
    with nc.Block() as block:
        @block.sync
        def _(sp):
            for n, t in shared.items():
                sp.dma_start(t[:], dram[n]).then_inc(landed, 16)
            sp.wait_ge(landed, 16 * len(shared))

        @block.vector
        def _(dve):
            nc.vector.memset(eps[:], EPS)
    const = {n: shared[n][:] for n in ("ident", "ones", "later", "upto")}
    const["eps"] = eps[:]
    return const, eps, {n: shared[n] for n in ("norm_mix_w", "norm_ffn_w", "final_norm_w")}


def tiles_of(w):
    n = w.shape[1] // P
    return w.reshape(KT, P, n, P).transpose(2, 1, 0, 3).reshape(n, P, D)


def columns(v):
    return v.reshape(KT, P).T


def laid_out(inp):
    a = {k: np.asarray(v) for k, v in inp.items()}
    r = {}
    r["x_t"] = a["x"][0].T.reshape(KT, P, T).transpose(1, 0, 2)
    for n in ("norm_mix_w", "norm_ffn_w", "ssd_norm_w"):
        r[n] = columns(a[n][0])
    r["final_norm_w"] = columns(a["final_norm_w"])
    w = a["w_in"][0]
    sizes = (D, D + 2 * SSD_GROUPS * P, SSD_HEADS, D, D, D, D, D, D)
    z, xbc, wdt, hq, hf, hi, hg, gs, gh = np.split(w, np.cumsum(sizes)[:-1], axis=1)
    z, xbc, hq, hf, hi, hg, gs, gh = (tiles_of(m) for m in (z, xbc, hq, hf, hi, hg, gs, gh))
    order = [i for g in range(SSD_GROUPS) for i in (2 * g, 2 * g + 1, KT + g, KT + SSD_GROUPS + g)]
    per_group = xbc[order].reshape(SSD_GROUPS, 4, P, D)
    r["w_ssd"] = np.concatenate([per_group, z.reshape(SSD_GROUPS, 2, P, D)], 1).reshape(-1, P, D)
    r["w_dt"] = wdt.reshape(KT, P, SSD_HEADS).transpose(1, 0, 2)
    r["w_hg"] = np.stack([hf, hq, hi, hg], 1).reshape(-1, P, D)
    r["w_mix_s"] = np.stack([gs, tiles_of(a["w_ssd_br"][0])], 1).reshape(-1, P, D)
    r["w_mix_h"] = np.stack([gh, tiles_of(a["w_hg_br"][0])], 1).reshape(-1, P, D)
    r["w_out"] = tiles_of(a["w_out"][0])
    r["w_query"] = tiles_of(a["peer_w_q"][0])
    r["u_tiles"] = a["peer_u"][0].reshape(KEYS, KEYS, KT, P).transpose(1, 3, 2, 0).reshape(KEYS, P, D)
    r["v_tiles"] = a["peer_v"][0].reshape(KEYS, KEYS, D).transpose(1, 0, 2)
    cw = np.concatenate([a["ssd_conv_w"][0], a["ssd_conv_b"][0][None]], 0)
    r["conv_w"] = cw.reshape(CONV + 1, -1, P)[:, order].transpose(2, 1, 0).reshape(P, -1)
    r["dt_bias"] = np.broadcast_to(a["ssd_dt_bias"][0], (P, SSD_HEADS))
    r["a_log"] = np.broadcast_to(a["ssd_a_log"][0], (P, SSD_HEADS))
    r["ssd_d"] = columns(np.repeat(a["ssd_d"][0], HD))
    r["hg_lb"] = a["hg_lb"].reshape(2, KT, P).transpose(2, 0, 1)
    r["hg_norm_w"] = a["hg_norm_w"][0][:, None]
    r["sub_keys"] = a["peer_sub_keys"][0].reshape(KT, KEYS, P).transpose(2, 0, 1)
    i = np.arange(P)
    r["ident"] = np.eye(P, dtype=np.float32)
    r["ones"] = np.ones((P, P), np.float32)
    r["later"] = (i[:, None] > i[None]).astype(np.float32)
    r["upto"] = (i[:, None] <= i[None]).astype(np.float32)
    s, t = i[:, None], i[None]
    levels = [(s // (2 * w) == t // (2 * w)) & (s // w % 2 == 0) & (t // w % 2 == 1) for w in HALVES]
    r["level_mask"] = np.stack(levels + [s == t], 1).astype(np.float32)
    r["count"] = np.broadcast_to(i.astype(np.float32), (P, P))
    return {n: np.ascontiguousarray(r[n]) for n in SHAPES}


def kernel(**inputs):
    import concourse.bacc as bacc
    from concourse.bass_utils import run_bass_kernel_spmd

    nc = bacc.Bacc("TRN2", target_bir_lowering=False, num_devices=1)
    program(nc)
    got = run_bass_kernel_spmd(nc, [laid_out(inputs)], core_ids=[0]).results[0]["out_t"]
    return np.ascontiguousarray(got.transpose(1, 0, 2).reshape(D, T).T)[None]
```

```python
from contextlib import ExitStack, contextmanager

import numpy as np

import concourse.bass as bass
from concourse import mybir

F32 = mybir.dt.float32
F32R = mybir.dt.float32r
U32 = mybir.dt.uint32
ALU = mybir.AluOpType
ACT = mybir.ActivationFunctionType
AX_X = mybir.AxisListType.X
EXP_LN_SET = "natural_log_exp_and_others"

P = 128
T = 512
D = 2048
KT = D // P
CH = 128
NC = T // CH
EPS = 1e-6

SSD_GROUPS = 8
SSD_HEADS = 32
HPG = SSD_HEADS // SSD_GROUPS
HD = 64
SSD_TILES = 6
CONV = 4

HG_HEADS = 16
HG_TILES = 4
LEVELS = 7
HALVES = [CH >> (l + 1) for l in range(LEVELS)]

PEER_HEADS = 8
KEYS = 128
TOPK = 16
GT = 32
HK = PEER_HEADS * TOPK
PIECE = 4
OWN = 96
REST = T - OWN
NEG = -3.0e38

ts = bass.ts
ds = bass.ds


def one(ap):
    return ap.rearrange("a p n -> (a p) n")


class Chain:

    def __init__(self, engine, done):
        self.engine, self.done = engine, done
        self.start, self.at, self.per, self.turn = 0, 0, 0, 0

    def after(self, ins):
        self.at += 1
        ins.then_inc(self.done, 1)
        self.engine.wait_ge(self.done, self.turn * self.per + (self.start + self.at))

    def enter(self, turn, per):
        self.start, self.at, self.per, self.turn = self.start + self.at, 0, per, turn

    def leave(self, turns):
        assert self.at == self.per, (self.at, self.per)
        self.start, self.at, self.per, self.turn = self.start + turns * self.per, 0, 0, 0


@contextmanager
def semaphores(nc, stage):
    with ExitStack() as ctx:
        made = []

        def sem(name):
            made.append(ctx.enter_context(nc.semaphore(f"{stage}_{name}")))
            return made[-1]

        yield sem
        with nc.Block() as block:
            @block.sync
            def _(sp):
                for s in made:
                    sp.sem_clear(s)


class Ring:

    def __init__(self, nc, ctx):
        sb = lambda n, dt: ctx.enter_context(nc.sbuf_tensor(f"ring_{n}", [P, 2, D], dt))
        sem = lambda n: ctx.enter_context(nc.semaphore(f"ring_{n}"))
        self.raw, self.high, self.low = sb("raw", F32), sb("high", F32R), sb("low", F32R)
        self.landed = [sem("landed0"), sem("landed1")]
        self.high_ready, self.low_ready, self.used = sem("high_ready"), sem("low_ready"), sem("used")
        self.base = 0


def load_tile(sp, ring, slot, tile, n):
    sp.wait_ge(ring.low_ready, ring.base + n - 1)
    sp.dma_start(ring.raw[:, slot], tile).then_inc(ring.landed[slot], 16)


def load_ahead(sp, ring, tiles, following):
    if following is not None:
        for s in range(2):
            load_tile(sp, ring, s, following[s], tiles + s)


def split_high(nc, act, ring, slot, n, pair):
    act.wait_ge(ring.landed[slot], 16 * pair + (8 * ring.base + 16))
    act.wait_ge(ring.used, ring.base + n + 1)
    nc.scalar.activation(ring.high[:, slot], ring.raw[:, slot], ACT.Copy).then_inc(ring.high_ready, 1)


def split_low(nc, pool, ring, slot, n):
    pool.wait_ge(ring.high_ready, ring.base + n + 1)
    nc.gpsimd.tensor_tensor(ring.low[:, slot], ring.raw[:, slot], ring.high[:, slot].bitcast(F32),
                            ALU.subtract).then_inc(ring.low_ready, 1)


def split_low_all(nc, pool, ring, tiles):
    with pool.Fori(0, tiles // 2) as i:
        for n in (1, 2):
            split_low(nc, pool, ring, n % 2, 2 * i + n)


def product(nc, out, high, low, x_high, x_low, steps=range(KT), tokens=slice(0, T),
            wait_piece=None):
    for k in steps:
        if wait_piece is not None and k % PIECE == 0:
            wait_piece(k // PIECE + 1)
        m = slice(k * P, (k + 1) * P)
        nc.tensor.matmul(out, high[:, m], x_high[:, k, tokens], start=(k == 0), stop=False, skip_group_check=True)
        nc.tensor.matmul(out, high[:, m], x_low[:, k, tokens], start=False, stop=False, skip_group_check=True)
        last = nc.tensor.matmul(out, low[:, m], x_high[:, k, tokens], start=False, stop=(k == KT - 1),
                                skip_group_check=True)
    return last



def norm_stage(nc, name, src, weight, work, ones, eps, load=None, split=None, store=None, ring=None,
               first_tiles=None, keep=None, mean=None):
    with ExitStack() as ctx:
        sem = ctx.enter_context(semaphores(nc, name))
        scaled_in = src if mean is None else work
        summed_before = mean is not None
        if mean is None:
            mean = ctx.enter_context(nc.psum_tensor(f"{name}_mean", [P, T], F32))
        rstd = ctx.enter_context(nc.sbuf_tensor(f"{name}_rstd", [P, T], F32))
        landed = [sem(f"landed{q}") for q in range(4)]
        squared, summed, rooted, scaled, high_done, stored, act_done = (
            sem(n) for n in ("squared", "summed", "rooted", "scaled", "high_done", "stored", "act_done"))
        normed_dve, normed_pool = sem("normed_dve"), sem("normed_pool")
        QUARTER = KT // 4
        on_pool = lambda k: k % 3 == 2
        low_on_pool = lambda k: k % 9 > 4
        block = ctx.enter_context(nc.Block())

        def wait_normed(engine, k):
            done = sum(on_pool(i) == on_pool(k) for i in range(k + 1))
            engine.wait_ge(normed_pool if on_pool(k) else normed_dve, done)

        def multiply_and_split(ops, engine, is_pool, normed):
            engine.wait_ge(rooted, 1)
            for k in range(KT):
                if on_pool(k) == is_pool:
                    ops.tensor_tensor(work[:, k], scaled_in[:, k], rstd[:], ALU.mult).then_inc(normed, 1)
            if split is not None:
                for k in range(KT):
                    if low_on_pool(k) == is_pool:
                        engine.wait_ge(high_done, k + 1)
                        ops.tensor_tensor(split[1][:, k], work[:, k], split[0][:, k].bitcast(F32), ALU.subtract)

        @block.sync
        def _(sp):
            if load is not None:
                for q in range(4):
                    sl = slice(q * QUARTER, (q + 1) * QUARTER)
                    sp.dma_start(src[:, sl], load[:, sl]).then_inc(landed[q], 16)
            if ring is not None:
                for s in range(2):
                    sp.dma_start(ring.raw[:, s], first_tiles[s]).then_inc(ring.landed[s], 16)
            if keep is not None:
                sp.dma_start(keep, src[:]).then_inc(stored, 16)
                sp.wait_ge(stored, 16)
            if store is not None:
                for k in range(KT):
                    wait_normed(sp, k)
                    sp.dma_start(store[:, k], work[:, k]).then_inc(stored, 16)
                sp.wait_ge(stored, 16 * KT)

        @block.scalar
        def _(act):
            nc.scalar.preload_act_table_set(EXP_LN_SET)
            if not summed_before:
                for q in range(4):
                    if load is not None:
                        act.wait_ge(landed[q], 16)
                    sl = slice(q * QUARTER, (q + 1) * QUARTER)
                    nc.scalar.activation(work[:, sl], src[:, sl], ACT.Square).then_inc(squared, 1)
                act.wait_ge(summed, 1)
            nc.scalar.activation(rstd[:], mean[:], ACT.Ln, bias=eps, scale=1.0 / D).then_inc(act_done, 1)
            act.wait_ge(act_done, 1)
            act.wait_ge(scaled, 1)
            nc.scalar.activation(rstd[:], rstd[:], ACT.Exp, scale=-0.5).then_inc(rooted, 1)
            if split is not None:
                for k in range(KT):
                    wait_normed(act, k)
                    nc.scalar.activation(split[0][:, k], work[:, k], ACT.Copy).then_inc(high_done, 1)
            if ring is not None:
                split_high(nc, act, ring, 0, 0, 0)

        @block.tensor
        def _(pe):
            if ring is not None:
                nc.tensor.nop().then_inc(ring.used, 2)
            if not summed_before:
                for k in range(KT):
                    pe.wait_ge(squared, k // QUARTER + 1)
                    last = nc.tensor.matmul(mean[:], ones, work[:, k], start=(k == 0), stop=(k == KT - 1))
                last.then_inc(summed, 1)

        @block.vector
        def _(dve):
            for k in range(KT):
                if not summed_before:
                    dve.wait_ge(squared, k // QUARTER + 1)
                ins = nc.vector.tensor_scalar(scaled_in[:, k], src[:, k], weight[:, k:k + 1], None, ALU.mult)
            ins.then_inc(scaled, 1)
            multiply_and_split(nc.vector, dve, False, normed_dve)

        @block.gpsimd
        def _(pool):
            multiply_and_split(nc.gpsimd, pool, True, normed_pool)
            if ring is not None:
                split_low(nc, pool, ring, 0, 0)



def ssd_stage(nc, dram, ring, h, const, y_out, following):
    G = SSD_GROUPS
    with ExitStack() as ctx:
        sb = lambda n, s, dt=F32: ctx.enter_context(nc.sbuf_tensor(f"sb_ssd_{n}", s, dt))
        ps = lambda n, s: ctx.enter_context(nc.psum_tensor(f"ssd_{n}", s, F32))
        sem = ctx.enter_context(semaphores(nc, "ssd"))
        W4 = HPG * CH
        conv = sb("conv", [P, SSD_TILES, T])
        sig = sb("sig", [P, SSD_TILES, T])
        act_in = sb("act_in", [P, SSD_TILES, T])
        half_tanh = sb("half_tanh", [P, 2, T])
        xdt = sb("xdt", [P, NC, HPG * HD])
        b_tok = sb("b_tok", [P, NC, P])
        steps_high = sb("steps_high", [P, HPG, CH], F32R)
        steps_low = sb("steps_low", [P, HPG, CH], F32R)
        later = sb("later", [P, P], F32R)
        ones = sb("ones", [P, P], F32R)
        decay = sb("decay", [P, HPG, CH])
        decay0 = sb("decay0", [P, HPG, CH])
        scores = sb("scores", [P, CH])
        mixed = sb("mixed", [P, HPG, CH])
        c_dec = sb("c_dec", [P, HPG, CH])
        x_dec = sb("x_dec", [P, HPG, HD])
        chunk_dec = sb("chunk_dec", [P, HPG])
        state = sb("state", [P, HPG, HD])
        y = sb("y", [P, 2, T])
        y_sq = sb("y_sq", [P, 2, T])
        rstd = sb("rstd", [P, T])
        y_norm = sb("y_norm", [P, 2, T])
        wdt = sb("wdt", [P, KT, SSD_HEADS])
        wdt_high = sb("wdt_high", [P, KT, SSD_HEADS], F32R)
        wdt_low = sb("wdt_low", [P, KT, SSD_HEADS], F32R)
        dt_bias = sb("dt_bias", [P, SSD_HEADS])
        a_log = sb("a_log", [P, SSD_HEADS])
        dt = sb("dt", [P, NC, SSD_HEADS])
        adt = sb("adt", [P, NC, SSD_HEADS])
        adt_high = sb("adt_high", [P, NC, SSD_HEADS], F32R)
        dtx = sb("dtx", [P, NC, SSD_HEADS])
        dte = sb("dte", [P, NC, SSD_HEADS])
        dtw = sb("dtw", [P, NC, SSD_HEADS])
        dtl = sb("dtl", [P, NC, SSD_HEADS])
        conv_w = sb("conv_w", [P, G * 4 * (CONV + 1)])
        d_col = sb("d_col", [P, KT])
        norm_w = sb("norm_w", [P, KT])

        acc = [ps(f"acc{i}", [P, T]) for i in range(2)]
        ps_decay = ps("ps_decay", [P, W4])
        ps_decay0 = ps("ps_decay0", [P, W4])
        ps_turn = ps("ps_turn", [P, T])
        ps_state = ps("ps_state", [P, HPG * HD])
        ps_y = [ps(f"ps_y{i}", [P, T]) for i in range(2)]

        consts = sem("consts")
        dt_split, dt_low, dt_sum, dt_exp, dt_ln = (sem(n) for n in ("dt_split", "dt_low", "dt_sum", "dt_exp", "dt_ln"))
        acc_read = sem("acc_read")
        tanh_done = sem("tanh_done")
        sig_done = sem("sig_done")
        in_ready = sem("in_ready")
        turned = sem("turned")
        turned_read = sem("turned_read")
        steps_ready = sem("steps_ready")
        a_done = sem("a_done")
        decayed = sem("decayed")
        mixed_ready = sem("mixed_ready")
        b_done = sem("b_done")
        state_ready = sem("state_ready")
        y_read = sem("y_read")
        gated = sem("gated")
        squared = sem("squared")
        summed = sem("summed")
        rooted = sem("rooted")
        y_ready = sem("y_ready")
        y_stored = sem("y_stored")
        act_done = sem("act_done")
        vec_done = sem("vec_done")
        block = ctx.enter_context(nc.Block())

        @block.sync
        def _(sp):
            for dst, src in ((wdt, dram["w_dt"]), (dt_bias, dram["dt_bias"]), (a_log, dram["a_log"]),
                             (conv_w, dram["conv_w"])):
                sp.dma_start(dst[:], src).then_inc(consts, 16)
            for dst, src in ((d_col, dram["ssd_d"]), (norm_w, dram["ssd_norm_w"])):
                sp.dma_start(dst[:], src).then_inc(y_stored, 16)

            def store(f):
                sp.wait_ge(y_ready, f + 1)
                for t in range(2):
                    sp.dma_start(one(y_out[ds(2 * f + t, 1)]), y_norm[:, t]).then_inc(y_stored, 16)

            for s in range(2, SSD_TILES):
                load_tile(sp, ring, s % 2, dram["w_ssd"][s], s)
            for s in range(SSD_TILES):
                load_tile(sp, ring, s % 2, dram["w_ssd"][SSD_TILES + s], SSD_TILES + s)
            with sp.Fori(2, G) as u:
                for s in range(SSD_TILES):
                    n = SSD_TILES * u + s
                    load_tile(sp, ring, s % 2, one(dram["w_ssd"][ds(n, 1)]), n)
                store(u - 2)
            load_ahead(sp, ring, G * SSD_TILES, following)
            store(G - 2)
            store(G - 1)
            sp.wait_ge(y_stored, 32 + 32 * G)

        @block.gpsimd
        def _(pool):
            split_low_all(nc, pool, ring, G * SSD_TILES)

        @block.scalar
        def _(act):
            chain = Chain(act, act_done)
            act.wait_ge(consts, 64)
            nc.scalar.activation(later[:], const["later"], ACT.Copy)
            nc.scalar.activation(ones[:], const["ones"], ACT.Copy)
            nc.scalar.activation(wdt_high[:], wdt[:], ACT.Copy).then_inc(dt_split, 1)
            chain.after(nc.scalar.activation(a_log[:], a_log[:], ACT.Exp))
            act.wait_ge(dt_sum, 1)
            nc.scalar.activation(dte[:], dte[:], ACT.Exp, scale=-1.0).then_inc(dt_exp, 1)
            act.wait_ge(dt_ln, 1)
            nc.scalar.activation(dtl[:], dtw[:], ACT.Ln).then_inc(dt_exp, 1)

            def body(u, proj, comp, fin):
                p, f = u - 1, u - 2
                for s in range(SSD_TILES):
                    if proj:
                        split_high(nc, act, ring, (s + 1) % 2, SSD_TILES * u + s + 1, 3 * u + (s + 1) // 2)
                    if s == 0 and fin:
                        act.wait_ge(gated, f + 1)
                        nc.scalar.activation(y_sq[:], y[:], ACT.Square).then_inc(squared, 1)
                    if proj:
                        if s < 4:
                            act.wait_ge(acc_read, SSD_TILES * u + s + 3)
                        else:
                            act.wait_ge(ring.used, ring.base + SSD_TILES * u + s + 3)
                        act.wait_ge(sig_done, SSD_TILES * u + s + 1)
                        nc.scalar.activation(half_tanh[:, s % 2], conv[:, s] if s < 4 else acc[s % 2][:],
                                             ACT.Tanh, scale=0.5).then_inc(tanh_done, 1)
                    if s == 1 and fin:
                        act.wait_ge(summed, f + 1)
                        chain.after(nc.scalar.activation(rstd[:], ps_decay[:], ACT.Ln, bias=const["eps"],
                                                         scale=1.0 / (2 * P)))
                        nc.scalar.activation(rstd[:], rstd[:], ACT.Exp, scale=-0.5).then_inc(rooted, 1)
                    if s >= 2 and comp:
                        act.wait_ge(a_done, NC * p + s - 1)
                        nc.scalar.activation(decay[:].rearrange("p h l -> p (h l)"), ps_decay[:], ACT.Exp)
                        nc.scalar.activation(decay0[:].rearrange("p h l -> p (h l)"), ps_decay0[:],
                                             ACT.Exp).then_inc(decayed, 1)

            body(0, True, False, False)
            body(1, True, True, False)
            with act.Fori(2, G) as u:
                chain.enter(u - 2, 1)
                body(u, True, True, True)
            chain.leave(G - 2)
            body(G, False, True, True)
            body(G + 1, False, False, True)

        @block.tensor
        def _(pe):
            pe.wait_ge(dt_low, 1)
            for c in range(NC):
                for k in range(KT):
                    tok = slice(c * CH, (c + 1) * CH)
                    o = ps_turn[:, c * SSD_HEADS:(c + 1) * SSD_HEADS]
                    nc.tensor.matmul(o, h[0][:, k, tok], wdt_high[:, k], start=(k == 0), stop=False,
                                     skip_group_check=True)
                    nc.tensor.matmul(o, h[1][:, k, tok], wdt_high[:, k], start=False, stop=False,
                                     skip_group_check=True)
                    last = nc.tensor.matmul(o, h[0][:, k, tok], wdt_low[:, k], start=False,
                                            stop=(k == KT - 1), skip_group_check=True)
            last.then_inc(dt_low, 1)

            def turn(dst, src, done):
                for c in range(NC):
                    last = nc.tensor.transpose(dst[:, c * P:(c + 1) * P], src[:, c * CH:(c + 1) * CH],
                                               const["ident"])
                last.then_inc(done, 1)

            def part_a(p, c):
                pe.wait_ge(steps_ready, NC * p + c + 1)
                pe.wait_ge(decayed, NC * p + c + 1)
                high, low = (x[:].rearrange("p h l -> p (h l)") for x in (steps_high, steps_low))
                for o, lhs in ((ps_decay, later), (ps_decay0, ones)):
                    nc.tensor.matmul(o[:], lhs[:], high, start=True, stop=False)
                    nc.tensor.matmul(o[:], lhs[:], low, start=False, stop=True)
                tok = slice(c * CH, (c + 1) * CH)
                nc.tensor.matmul(ps_turn[:, 0:CH], act_in[:, 2, tok], act_in[:, 3, tok],
                                 start=True, stop=True).then_inc(a_done, 1)

            def part_b(p, c):
                pe.wait_ge(mixed_ready, NC * p + c + 1)
                if c == 0:
                    pe.wait_ge(y_read, p + 1)
                else:
                    pe.wait_ge(state_ready, (NC - 1) * p + c)
                for head in range(HPG):
                    part = slice(HD * (head % 2), HD * (head % 2) + HD)
                    o = ps_y[head // 2][part, c * CH:(c + 1) * CH]
                    last = nc.tensor.matmul(o, xdt[:, c, head * HD:(head + 1) * HD], mixed[:, head],
                                            start=True, stop=(c == 0), skip_group_check=True)
                    if c > 0:
                        last = nc.tensor.matmul(o, state[:, head], c_dec[:, head], start=False, stop=True,
                                                skip_group_check=True)
                if c < NC - 1:
                    last = nc.tensor.matmul(ps_state[:], b_tok[:, c], x_dec[:].rearrange("p h d -> p (h d)"),
                                            start=True, stop=True)
                last.then_inc(b_done, 1)

            def body(u, proj, comp, fin):
                p, f = u - 1, u - 2
                for s in range(SSD_TILES):
                    n = SSD_TILES * u + s

                    def half(i):
                        return product(nc, acc[s % 2][:], ring.high[:, s % 2], ring.low[:, s % 2], h[0], h[1],
                                       range(i * KT // 2, (i + 1) * KT // 2))

                    if proj:
                        pe.wait_ge(ring.low_ready, ring.base + n + 1)
                        pe.wait_ge(acc_read, n + 1)
                        half(0)
                    if s == 0 and fin:
                        part_b(f, NC - 1)
                    if proj:
                        half(1).then_inc(ring.used, 1)
                    if s == 0:
                        if comp:
                            pe.wait_ge(in_ready, p + 1)
                            turn(ps_turn, act_in[:, 0], turned)
                    if s == 1:
                        if fin:
                            pe.wait_ge(squared, f + 1)
                            pe.wait_ge(decayed, NC * f + NC + 1)
                            for t in range(2):
                                last = nc.tensor.matmul(ps_decay[:], const["ones"], y_sq[:, t],
                                                        start=(t == 0), stop=(t == 1))
                            last.then_inc(summed, 1)
                        if comp:
                            pe.wait_ge(turned_read, 3 * p + 1)
                            turn(ps_turn, act_in[:, 1], turned)
                    if comp:
                        if s == 2:
                            pe.wait_ge(turned_read, 3 * p + 2)
                            turn(ps_turn, act_in[:, 2], turned)
                            pe.wait_ge(turned_read, 3 * p + 3)
                            pe.wait_ge(rooted, p + 1)
                            part_a(p, 0)
                        if s > 2:
                            part_b(p, s - 3)
                            part_a(p, s - 2)

            body(0, True, False, False)
            body(1, True, True, False)
            with pe.Fori(2, G) as u:
                body(u, True, True, True)
            body(G, False, True, True)
            body(G + 1, False, False, True)

        @block.vector
        def _(dve):
            chain = Chain(dve, vec_done)
            v = nc.vector
            v.nop().then_inc(acc_read, 2)
            v.nop().then_inc(sig_done, 2)
            v.nop().then_inc(decayed, 1)
            v.nop().then_inc(y_read, 1)
            v.nop().then_inc(rooted, 1)
            dve.wait_ge(dt_split, 1)
            v.tensor_tensor(wdt_low[:], wdt[:], wdt_high[:].bitcast(F32), ALU.subtract).then_inc(dt_low, 1)
            dve.wait_ge(dt_low, 2)
            dve.wait_ge(consts, 64)
            chain.after(v.tensor_tensor(dtx[:], ps_turn[:, 0:NC * SSD_HEADS].rearrange("p (c h) -> p c h", c=NC),
                                        dt_bias[:].unsqueeze(1).to_broadcast([P, NC, SSD_HEADS]), ALU.add))
            chain.after(v.tensor_scalar(dte[:], dtx[:], -1.0, None, ALU.mult))
            v.tensor_tensor(dte[:], dte[:], dtx[:], ALU.max).then_inc(dt_sum, 1)
            dve.wait_ge(dt_exp, 1)
            v.tensor_scalar(dtw[:], dte[:], 1.0, None, ALU.add).then_inc(dt_ln, 1)
            dve.wait_ge(dt_ln, 1)
            chain.after(v.tensor_scalar(dt[:], dtw[:], -1.0, None, ALU.add))
            chain.after(v.tensor_tensor(dte[:], dte[:], dt[:], ALU.subtract))
            dve.wait_ge(dt_exp, 2)
            chain.after(v.reciprocal(dtw[:], dtw[:]))
            chain.after(v.tensor_tensor(dte[:], dte[:], dtw[:], ALU.mult))
            chain.after(v.tensor_tensor(dtl[:], dtl[:], dte[:], ALU.add))
            chain.after(v.scalar_tensor_tensor(dt[:], dtx[:], 0.0, dtl[:], ALU.max, ALU.add))
            chain.after(v.scalar_tensor_tensor(adt[:], dt[:], -1.0,
                                               a_log[:].unsqueeze(1).to_broadcast([P, NC, SSD_HEADS]),
                                               ALU.mult, ALU.mult))
            chain.after(v.tensor_copy(adt_high[:], adt[:]))
            chain.after(v.tensor_tensor(adt[:], adt[:], adt_high[:].bitcast(F32), ALU.subtract))
            dve.wait_ge(y_stored, 32)

            def convolve(u, s):
                src, dst = acc[s % 2], conv[:, s]
                w = lambda j: conv_w[:, ds(u * 4 * (CONV + 1) + s * (CONV + 1) + j, 1)]
                dve.wait_ge(ring.used, ring.base + SSD_TILES * u + s + 3)
                chain.after(v.tensor_scalar(dst, src[:], w(CONV - 1), w(CONV), ALU.mult, ALU.add))
                for back in range(1, CONV):
                    ins = v.scalar_tensor_tensor(dst[:, back:], src[:, :T - back], w(CONV - 1 - back),
                                                 dst[:, back:], ALU.mult, ALU.add)
                    if back < CONV - 1:
                        chain.after(ins)
                ins.then_inc(acc_read, 1)

            def sigmoid(u, s):
                dve.wait_ge(tanh_done, SSD_TILES * u + s + 1)
                v.tensor_scalar(sig[:, s], half_tanh[:, s % 2], 1.0, 0.5, ALU.add, ALU.mult).then_inc(sig_done, 1)

            def take_z(u, s):
                dve.wait_ge(tanh_done, SSD_TILES * u + s + 1)
                v.tensor_copy(conv[:, s], acc[s % 2][:]).then_inc(acc_read, 1)

            def take_x(p, t):
                dve.wait_ge(turned, 3 * p + t + 1)
                v.tensor_tensor(xdt[:, :, t * P:(t + 1) * P].rearrange("p c (h d) -> p c h d", h=2),
                                ps_turn[:].rearrange("p (c h d) -> p c h d", c=NC, h=2),
                                dt[:, :, ds(HPG * p + 2 * t, 2)].unsqueeze(3).to_broadcast([P, NC, 2, HD]),
                                ALU.mult).then_inc(turned_read, 1)

            def make_steps(p, c):
                for steps, part in ((steps_high, adt_high[:].bitcast(F32)), (steps_low, adt[:])):
                    ins = v.tensor_tensor(steps[:], const["upto"].unsqueeze(1).to_broadcast([P, HPG, CH]),
                                          part[:, c, ds(HPG * p, HPG)].unsqueeze(2).to_broadcast([P, HPG, CH]),
                                          ALU.mult)
                ins.then_inc(steps_ready, 1)

            def next_state(p, c):
                dve.wait_ge(b_done, NC * p + c + 1)
                new = ps_state[:].rearrange("p (h d) -> p h d", h=HPG)
                if c == 0:
                    v.tensor_copy(state[:], new).then_inc(state_ready, 1)
                else:
                    chain.after(v.tensor_tensor(state[:], state[:],
                                                chunk_dec[:].unsqueeze(2).to_broadcast([P, HPG, HD]), ALU.mult))
                    v.tensor_tensor(state[:], state[:], new, ALU.add).then_inc(state_ready, 1)

            def mix(p, c):
                dve.wait_ge(decayed, NC * p + c + 2)
                if c > 0:
                    dve.wait_ge(mixed_ready, NC * p + c)
                chain.after(v.tensor_tensor(scores[:], ps_turn[:, 0:CH], const["upto"], ALU.mult))
                v.tensor_tensor(mixed[:], decay[:], scores[:].unsqueeze(1).to_broadcast([P, HPG, CH]), ALU.mult)
                if c < NC - 1:
                    v.tensor_tensor(x_dec[:], xdt[:, c].rearrange("p (h d) -> p h d", h=HPG),
                                    decay[:, :, CH - 1:CH].to_broadcast([P, HPG, HD]), ALU.mult)
                    v.tensor_copy(chunk_dec[:], decay0[:, :, CH - 1])
                v.tensor_tensor(c_dec[:], decay0[:],
                                act_in[:, 3, c * CH:(c + 1) * CH].unsqueeze(1).to_broadcast([P, HPG, CH]),
                                ALU.mult).then_inc(mixed_ready, 1)

            def body(u, proj, comp, fin):
                p, f = u - 1, u - 2
                for s in range(SSD_TILES):
                    if s == 0:
                        if fin:
                            dve.wait_ge(b_done, NC * f + NC)
                            for t in range(2):
                                ins = v.scalar_tensor_tensor(y[:, t], act_in[:, t], d_col[:, ds(2 * f + t, 1)],
                                                             ps_y[t][:], ALU.mult, ALU.add)
                            ins.then_inc(y_read, 1)
                            dve.wait_ge(y_read, f + 2)
                            v.tensor_tensor(y[:], y[:], act_in[:, 4:6], ALU.mult).then_inc(gated, 1)
                        if comp:
                            dve.wait_ge(sig_done, SSD_TILES * p + SSD_TILES + 2)
                            if fin:
                                dve.wait_ge(gated, f + 1)
                            v.tensor_tensor(act_in[:, 0:4], conv[:, 0:4], sig[:, 0:4], ALU.mult).then_inc(in_ready, 1)
                            dve.wait_ge(in_ready, p + 1)
                            chain.after(v.tensor_tensor(act_in[:, 4:6], conv[:, 4:6], sig[:, 4:6], ALU.mult))
                        if proj:
                            convolve(u, 0)
                        if comp:
                            take_x(p, 0)
                            make_steps(p, 0)
                    if s == 1:
                        if proj:
                            convolve(u, 1)
                            sigmoid(u, 0)
                        if comp:
                            take_x(p, 1)
                        if fin:
                            dve.wait_ge(rooted, f + 2)
                            dve.wait_ge(y_stored, 32 * f + 32)
                            for t in range(2):
                                ins = v.scalar_tensor_tensor(y_norm[:, t], y[:, t], norm_w[:, ds(2 * f + t, 1)],
                                                             rstd[:], ALU.mult, ALU.mult)
                            ins.then_inc(y_ready, 1)
                    if s == 2:
                        if comp:
                            dve.wait_ge(turned, 3 * p + 3)
                            v.tensor_copy(b_tok[:].rearrange("p c n -> p (c n)"), ps_turn[:]).then_inc(turned_read, 1)
                        if proj:
                            convolve(u, 2)
                            sigmoid(u, 1)
                        if comp:
                            mix(p, 0)
                            make_steps(p, 1)
                    if s >= 3:
                        if proj:
                            sigmoid(u, s - 1)
                            if s == 3:
                                convolve(u, s)
                            else:
                                take_z(u, s)
                        if comp:
                            next_state(p, s - 3)
                            mix(p, s - 2)
                            if s < SSD_TILES - 1:
                                make_steps(p, s - 1)
                if proj:
                    sigmoid(u, SSD_TILES - 1)

            body(0, True, False, False)
            body(1, True, True, False)
            with dve.Fori(2, G) as u:
                chain.enter(u - 2, 4 * 3 + 4 + 2 + 1)
                body(u, True, True, True)
            chain.leave(G - 2)
            body(G, False, True, True)
            body(G + 1, False, False, True)
    ring.base += G * SSD_TILES



def hg_stage(nc, dram, ring, h, const, y_out, following):
    H = HG_HEADS
    L7, L8, LK, LQ = LEVELS, LEVELS + 1, LEVELS + 2, LEVELS + 3
    with ExitStack() as ctx:
        sb = lambda n, s, dt=F32: ctx.enter_context(nc.sbuf_tensor(f"sb_hg_{n}", s, dt))
        ps = lambda n, s: ctx.enter_context(nc.psum_tensor(f"hg_{n}", s, F32))
        sem = ctx.enter_context(semaphores(nc, "hg"))
        mask = sb("mask", [P, LEVELS + 1, CH])
        lb = sb("lb", [P, 2, KT])
        lb_in = sb("lb_in", [P, 2, KT])
        lb_max = sb("lb_max", [P, KT])
        norm_w = sb("norm_w", [P, 1])
        f = sb("f", [P, T])
        k = sb("k", [P, T])
        q = sb("q", [P, T])
        v = sb("v", [P, T])
        og = sb("og", [P, T])
        sg = sb("sg", [P, T])
        b = sb("b", [P, T])
        lev = sb("lev", [P, LEVELS + 4, T])
        qe = sb("qe", [P, T])
        k_end = sb("k_end", [P, NC])
        v_tok = sb("v_tok", [P, NC, P])
        k_tok = sb("k_tok", [P, NC, P])
        masked = sb("masked", [P, LEVELS + 1, CH])
        probs = sb("probs", [P, 2, CH])
        state = sb("state", [P, P])
        o_sq = sb("o_sq", [P, T])
        rstd = sb("rstd", [P, T])
        o_norm = sb("o_norm", [P, T])

        acc = [ps(f"acc{i}", [P, T]) for i in range(2)]
        ps_lev = ps("ps_lev", [P, LEVELS + 1, CH])
        ps_o = ps("ps_o", [P, T])
        ps_state = ps("ps_state", [P, P])
        ps_v = ps("ps_v", [P, T])
        ps_k = ps("ps_k", [P, T])

        consts = sem("consts")
        lb_step = sem("lb_step")
        acc_read = sem("acc_read")
        f_exp, q_exp, g_exp, f_ready, f_log, b_ready = (
            sem(n) for n in ("f_exp", "q_exp", "g_exp", "f_ready", "f_log", "b_ready"))
        turned = sem("turned")
        turned_read = sem("turned_read")
        lev_diff = sem("lev_diff")
        lev_exp = sem("lev_exp")
        lev_ready = sem("lev_ready")
        a_done = sem("a_done")
        a_read = sem("a_read")
        probs_ready = sem("probs_ready")
        b_done = sem("b_done")
        state_ready = sem("state_ready")
        squared, summed, rooted = sem("squared"), sem("summed"), sem("rooted")
        o_ready = sem("o_ready")
        o_stored = sem("o_stored")
        act_done, vec_done = sem("act_done"), sem("vec_done")
        block = ctx.enter_context(nc.Block())

        @block.sync
        def _(sp):
            sp.dma_start(mask[:], dram["level_mask"]).then_inc(consts, 16)
            sp.dma_start(lb_in[:], dram["hg_lb"]).then_inc(consts, 16)
            sp.dma_start(norm_w[:], dram["hg_norm_w"]).then_inc(o_stored, 16)
            for s in range(2, HG_TILES):
                load_tile(sp, ring, s % 2, dram["w_hg"][s], s)

            def store(p):
                sp.wait_ge(o_ready, p + 2)
                sp.dma_start(one(y_out[ds(p, 1)]), o_norm[:]).then_inc(o_stored, 16)

            for s in range(HG_TILES):
                load_tile(sp, ring, s % 2, dram["w_hg"][HG_TILES + s], HG_TILES + s)
            with sp.Fori(2, H) as u:
                for s in range(HG_TILES):
                    n = HG_TILES * u + s
                    load_tile(sp, ring, s % 2, one(dram["w_hg"][ds(n, 1)]), n)
                store(u - 2)
            load_ahead(sp, ring, H * HG_TILES, following)
            store(H - 2)
            store(H - 1)
            sp.wait_ge(o_stored, 16 + 16 * H)

        @block.gpsimd
        def _(pool):
            split_low_all(nc, pool, ring, H * HG_TILES)

        @block.scalar
        def _(act):
            chain = Chain(act, act_done)
            nc.scalar.preload_act_table_set(EXP_LN_SET)
            act.wait_ge(lb_step, 1)
            nc.scalar.activation(lb_in[:], lb_in[:], ACT.Exp).then_inc(lb_step, 1)

            def body(u, proj, comp):
                p = u - 1
                for s in range(HG_TILES):
                    n = HG_TILES * u + s
                    if proj:
                        split_high(nc, act, ring, (s + 1) % 2, n + 1, 2 * u + (s + 1) // 2)
                    if s == 0 and proj:
                        act.wait_ge(ring.used, ring.base + n + 3)
                        act.wait_ge(lev_ready, u + 1)
                        nc.scalar.activation(f[:], acc[0][:], ACT.Exp, scale=-1.0).then_inc(f_exp, 1)
                        act.wait_ge(f_ready, u + 1)
                        nc.scalar.activation(b[:], f[:], ACT.Ln).then_inc(f_log, 1)
                    if s == 1 and proj:
                        act.wait_ge(ring.used, ring.base + n + 3)
                        nc.scalar.activation(sg[:], acc[1][:], ACT.Exp, scale=-1.0).then_inc(q_exp, 1)
                    if s == 2:
                        if proj:
                            act.wait_ge(lev_diff, u + 1)
                            nc.scalar.activation(lev[:, 0:LK], lev[:, 0:LK], ACT.Exp).then_inc(lev_exp, 1)
                        if comp:
                            act.wait_ge(b_done, NC * p + NC)
                            nc.scalar.activation(o_sq[:], ps_o[:], ACT.Square).then_inc(squared, 1)
                    if s == 3:
                        if comp:
                            act.wait_ge(summed, p + 1)
                            chain.after(nc.scalar.activation(rstd[:], ps_k[:], ACT.Ln, bias=const["eps"],
                                                             scale=1.0 / P))
                            nc.scalar.activation(rstd[:], rstd[:], ACT.Exp, scale=-0.5).then_inc(rooted, 1)
                        if proj:
                            act.wait_ge(ring.used, ring.base + n + 3)
                            act.wait_ge(acc_read, HG_TILES * u + 4)
                            nc.scalar.activation(sg[:], acc[1][:], ACT.Exp, scale=-1.0).then_inc(g_exp, 1)

            body(0, True, False)
            with act.Fori(1, H) as u:
                chain.enter(u - 1, 1)
                body(u, True, True)
            chain.leave(H - 1)
            body(H, False, True)

        @block.tensor
        def _(pe):

            def turn(dst, src):
                for c in range(NC):
                    last = nc.tensor.transpose(dst[:, c * P:(c + 1) * P], src[:, c * CH:(c + 1) * CH],
                                               const["ident"])
                last.then_inc(turned, 1)

            def part_a(p, c):
                pe.wait_ge(a_read, NC * p + c + 1)
                tok = slice(c * CH, (c + 1) * CH)
                for l in range(LEVELS):
                    nc.tensor.matmul(ps_lev[:, l], lev[:, l, tok], lev[:, l, tok], start=True, stop=True)
                nc.tensor.matmul(ps_lev[:, LEVELS], lev[:, LK, tok], lev[:, LQ, tok],
                                 start=True, stop=True).then_inc(a_done, 1)

            def part_b(p, c):
                tok = slice(c * CH, (c + 1) * CH)
                pe.wait_ge(probs_ready, NC * p + c + 1)
                if c == 0:
                    pe.wait_ge(o_ready, p + 1)
                    pe.wait_ge(turned_read, 2 * p + 2)
                last = nc.tensor.matmul(ps_o[:, tok], v_tok[:, c], probs[:, c % 2], start=True, stop=(c == 0))
                if c > 0:
                    pe.wait_ge(state_ready, (NC - 1) * p + c)
                    last = nc.tensor.matmul(ps_o[:, tok], state[:], qe[:, tok], start=False, stop=True)
                if c < NC - 1:
                    last = nc.tensor.matmul(ps_state[:], k_tok[:, c], v_tok[:, c], start=True, stop=True)
                last.then_inc(b_done, 1)

            def body(u, proj, comp):
                p = u - 1
                for s in range(HG_TILES):
                    n = HG_TILES * u + s

                    def half(i):
                        if not proj:
                            return
                        if i == 0:
                            pe.wait_ge(ring.low_ready, ring.base + n + 1)
                            pe.wait_ge(acc_read, n + 1)
                        last = product(nc, acc[s % 2][:], ring.high[:, s % 2], ring.low[:, s % 2], h[0], h[1],
                                       range(i * KT // 2, (i + 1) * KT // 2))
                        if i == 1:
                            last.then_inc(ring.used, 1)

                    half(0)
                    if comp:
                        if s == 0:
                            pe.wait_ge(lev_ready, p + 2)
                            turn(ps_v, v)
                            pe.wait_ge(rooted, p + 1)
                            turn(ps_k, lev[:, L8])
                            part_a(p, 0)
                        if s == 1:
                            part_b(p, 0)
                            part_a(p, 2)
                        if s == 2:
                            part_b(p, 2)
                        if s == 3:
                            pe.wait_ge(squared, p + 1)
                            nc.tensor.matmul(ps_k[:], const["ones"], o_sq[:], start=True, stop=True).then_inc(summed, 1)
                    half(1)
                    if comp:
                        if s == 0:
                            part_a(p, 1)
                        if s == 1:
                            part_b(p, 1)
                            part_a(p, 3)
                        if s == 2:
                            part_b(p, 3)

            body(0, True, False)
            with pe.Fori(1, H) as u:
                body(u, True, True)
            body(H, False, True)

        @block.vector
        def _(dve):
            chain = Chain(dve, vec_done)
            vec = nc.vector
            vec.nop().then_inc(acc_read, 2)
            vec.nop().then_inc(a_read, 1)
            vec.nop().then_inc(o_ready, 1)
            vec.nop().then_inc(rooted, 1)
            vec.nop().then_inc(lev_ready, 1)
            dve.wait_ge(consts, 32)
            dve.wait_ge(o_stored, 16)
            chain.after(vec.tensor_tensor(lb_max[:], lb_in[:, 0], lb_in[:, 1], ALU.max))
            vec.tensor_tensor(lb_in[:], lb_in[:], lb_max[:].unsqueeze(1).to_broadcast([P, 2, KT]),
                              ALU.subtract).then_inc(lb_step, 1)
            dve.wait_ge(lb_step, 2)
            chain.after(vec.tensor_tensor(lb_max[:], lb_in[:, 0], lb_in[:, 1], ALU.add))
            chain.after(vec.reciprocal(lb_max[:], lb_max[:]))
            chain.after(vec.tensor_tensor(lb[:, 0], lb_in[:, 0], lb_max[:], ALU.mult))
            chain.after(vec.tensor_scalar(lb[:, 1], lb[:, 0], -1.0, 1.0, ALU.mult, ALU.add))

            def take_f(u):
                dve.wait_ge(f_exp, u + 1)
                ins = vec.tensor_scalar(sg[:], f[:], 1.0, None, ALU.add)
                ins.then_inc(acc_read, 1)
                dve.wait_ge(acc_read, HG_TILES * u + 3)
                chain.after(vec.reciprocal(sg[:], sg[:]))
                vec.tensor_scalar(f[:], sg[:], lb[:, 1, ds(u, 1)], lb[:, 0, ds(u, 1)],
                                  ALU.mult, ALU.add).then_inc(f_ready, 1)
                dve.wait_ge(f_ready, u + 1)
                chain.after(vec.tensor_scalar(k[:], f[:], -1.0, 1.0, ALU.mult, ALU.add))
                dve.wait_ge(f_log, u + 1)
                for c in range(NC):
                    tok = slice(c * CH, (c + 1) * CH)
                    ins = vec.tensor_tensor_scan(b[:, tok], const["ones"][:, 0:CH], b[:, tok], 0.0,
                                                 ALU.mult, ALU.add)
                ins.then_inc(b_ready, 1)

            def swish(dst, src, exp_done, value, taken):
                dve.wait_ge(exp_done, value)
                chain.after(vec.tensor_scalar(sg[:], sg[:], 1.0, None, ALU.add))
                chain.after(vec.reciprocal(sg[:], sg[:]))
                vec.tensor_tensor(dst[:], src[:], sg[:], ALU.mult).then_inc(acc_read, 1)
                dve.wait_ge(acc_read, taken)

            def take_probs(p, c):
                dve.wait_ge(a_done, NC * p + c + 1)
                if c > 0:
                    dve.wait_ge(probs_ready, NC * p + c)
                vec.tensor_tensor(masked[:], ps_lev[:], mask[:], ALU.mult).then_inc(a_read, 1)
                dve.wait_ge(a_read, NC * p + c + 2)
                vec.tensor_reduce(probs[:, c % 2], masked[:].rearrange("p l t -> p t l"), AX_X,
                                  ALU.add).then_inc(probs_ready, 1)

            def next_state(p, c):
                dve.wait_ge(b_done, NC * p + c + 1)
                if c == 0:
                    vec.tensor_copy(state[:], ps_state[:]).then_inc(state_ready, 1)
                else:
                    vec.scalar_tensor_tensor(state[:], state[:], k_end[:, c:c + 1], ps_state[:],
                                             ALU.mult, ALU.add).then_inc(state_ready, 1)

            def exponents(u, p, comp):
                dve.wait_ge(b_ready, u + 1)
                for l, w in enumerate(HALVES):
                    if l == 3 and comp:
                        next_state(p, 2)
                    halves = lambda x: x.rearrange("p (n a w) -> p n a w", a=2, w=w)
                    src, dst = halves(b[:]), halves(lev[:, l])
                    n = T // (2 * w)
                    ref = src[:, :, 0, w - 1:w].to_broadcast([P, n, w])
                    vec.tensor_tensor(dst[:, :, 1, :], src[:, :, 1, :], ref, ALU.subtract)
                    vec.tensor_tensor(dst[:, :, 0, :], ref, src[:, :, 0, :], ALU.subtract)
                vec.tensor_copy(lev[:, L7], b[:])
                chunks = lambda x: x.rearrange("p (c t) -> p c t", c=NC)
                vec.tensor_tensor(chunks(lev[:, L8]), chunks(b[:])[:, :, CH - 1:CH].to_broadcast([P, NC, CH]),
                                  chunks(b[:]), ALU.subtract).then_inc(lev_diff, 1)

            def weigh(u, p, comp):
                dve.wait_ge(lev_exp, u + 1)
                for l, w in enumerate(HALVES):
                    halves = lambda x: x.rearrange("p (n a w) -> p n a w", a=2, w=w)
                    dst = halves(lev[:, l])
                    vec.tensor_tensor(dst[:, :, 1, :], dst[:, :, 1, :], halves(q[:])[:, :, 1, :], ALU.mult)
                    vec.tensor_tensor(dst[:, :, 0, :], dst[:, :, 0, :], halves(k[:])[:, :, 0, :], ALU.mult)
                vec.tensor_copy(lev[:, LK], k[:])
                vec.tensor_copy(lev[:, LQ], q[:])
                if comp:
                    dve.wait_ge(b_done, NC * p + NC)
                vec.tensor_tensor(qe[:], lev[:, L7], q[:], ALU.mult)
                vec.tensor_copy(k_end[:], lev[:, L7].rearrange("p (c t) -> p c t", c=NC)[:, :, CH - 1])
                vec.tensor_tensor(lev[:, L8], lev[:, L8], k[:], ALU.mult).then_inc(lev_ready, 1)
                dve.wait_ge(lev_ready, u + 2)

            def body(u, proj, comp):
                p = u - 1
                n = HG_TILES * u
                if comp:
                    dve.wait_ge(turned, 2 * p + 1)
                    vec.tensor_copy(v_tok[:].rearrange("p c v -> p (c v)"), ps_v[:]).then_inc(turned_read, 1)
                    dve.wait_ge(turned, 2 * p + 2)
                    vec.tensor_copy(k_tok[:].rearrange("p c v -> p (c v)"), ps_k[:]).then_inc(turned_read, 1)
                    take_probs(p, 0)
                    take_probs(p, 1)
                if proj:
                    take_f(u)
                if comp:
                    next_state(p, 0)
                    take_probs(p, 2)
                    next_state(p, 1)
                    take_probs(p, 3)
                if proj:
                    swish(q, acc[1], q_exp, u + 1, n + 4)
                    exponents(u, p, comp)
                    dve.wait_ge(ring.used, ring.base + n + 5)
                    vec.tensor_copy(v[:], acc[0][:]).then_inc(acc_read, 1)
                if comp and not proj:
                    next_state(p, 2)
                if proj:
                    weigh(u, p, comp)
                if comp:
                    dve.wait_ge(rooted, p + 2)
                    dve.wait_ge(o_stored, 16 * p + 16)
                    chain.after(vec.scalar_tensor_tensor(o_norm[:], ps_o[:], norm_w[:, 0:1], rstd[:],
                                                         ALU.mult, ALU.mult))
                    vec.tensor_tensor(o_norm[:], o_norm[:], og[:], ALU.mult).then_inc(o_ready, 1)
                    dve.wait_ge(o_ready, p + 2)
                if proj:
                    swish(og, acc[1], g_exp, u + 1, n + 6)

            body(0, True, False)
            with dve.Fori(1, H) as u:
                chain.enter(u - 1, 2 + 2 + 1 + 2)
                body(u, True, True)
            chain.leave(H - 1)
            body(H, False, True)
    ring.base += H * HG_TILES



def mix_stage(nc, name, w, ring, h, y_src, prior, dst, following):
    with ExitStack() as ctx:
        sb = lambda n, s, dt=F32: ctx.enter_context(nc.sbuf_tensor(f"sb_{name}_{n}", s, dt))
        ps = lambda n, s: ctx.enter_context(nc.psum_tensor(f"{name}_{n}", s, F32))
        sem = ctx.enter_context(semaphores(nc, name))
        y_raw = sb("y_raw", [P, 2, PIECE, T])
        y_high = sb("y_high", [P, KT, T], F32R)
        y_low = sb("y_low", [P, KT, T], F32R)
        half_tanh = sb("half_tanh", [P, T])
        gate = sb("gate", [P, T])
        mixed = sb("mixed", [P, T])
        before = sb("before", [P, T])
        acc = [ps(f"acc{i}", [P, T]) for i in range(2)]
        y_landed = [sem("y_landed0"), sem("y_landed1")]
        y_high_ready, y_low_ready = sem("y_high_ready"), sem("y_low_ready")
        gate_tanh, gate_ready = sem("gate_tanh"), sem("gate_ready")
        mixed_ready, stored, before_landed, vec_done = (
            sem("mixed_ready"), sem("stored"), sem("before_landed"), sem("vec_done"))
        block = ctx.enter_context(nc.Block())

        @block.sync
        def _(sp):
            for i in range(KT // PIECE):
                if i >= 2:
                    sp.wait_ge(y_low_ready, i - 1)
                sp.dma_start(y_raw[:, i % 2], y_src[i * PIECE:(i + 1) * PIECE].rearrange("k p t -> p k t")
                             ).then_inc(y_landed[i % 2], 16)

            def rest(n, load):
                if load:
                    for s in range(2):
                        load_tile(sp, ring, s, one(w[ds(2 * n + 2 + s, 1)]), 2 * n + 2 + s)
                if prior is not None:
                    sp.dma_start(before[:], one(prior[ds(n, 1)])).then_inc(before_landed, 16)
                sp.wait_ge(mixed_ready, n + 1)
                sp.dma_start(one(dst[ds(n, 1)]), mixed[:]).then_inc(stored, 16)

            with sp.Fori(0, KT - 1) as n:
                rest(n, True)
            load_ahead(sp, ring, 2 * KT, following)
            rest(KT - 1, False)
            sp.wait_ge(stored, 16 * KT)

        @block.gpsimd
        def _(pool):
            split_low_all(nc, pool, ring, 2 * KT)

        @block.scalar
        def _(act):
            split_high(nc, act, ring, 1, 1, 0)
            for i in range(KT // PIECE):
                act.wait_ge(y_landed[i % 2], 16 * (i // 2) + 16)
                nc.scalar.activation(y_high[:, i * PIECE:(i + 1) * PIECE], y_raw[:, i % 2],
                                     ACT.Copy).then_inc(y_high_ready, 1)

            def body(n):
                act.wait_ge(ring.used, ring.base + 2 * n + 3)
                act.wait_ge(gate_ready, n + 1)
                nc.scalar.activation(half_tanh[:], acc[0][:], ACT.Tanh, scale=0.5).then_inc(gate_tanh, 1)
                split_high(nc, act, ring, 0, 2 * n + 2, n + 1)

            with act.Fori(0, KT - 1) as n:
                body(n)
                split_high(nc, act, ring, 1, 2 * n + 3, n + 1)
            body(KT - 1)

        @block.tensor
        def _(pe):

            def body(n, first):
                pe.wait_ge(ring.low_ready, ring.base + 2 * n + 1)
                if not first:
                    pe.wait_ge(gate_tanh, n)
                product(nc, acc[0][:], ring.high[:, 0], ring.low[:, 0], h[0], h[1]).then_inc(ring.used, 1)
                pe.wait_ge(ring.low_ready, ring.base + 2 * n + 2)
                if not first:
                    pe.wait_ge(mixed_ready, n)
                product(nc, acc[1][:], ring.high[:, 1], ring.low[:, 1], y_high, y_low,
                        wait_piece=(lambda i: pe.wait_ge(y_low_ready, i)) if first else None).then_inc(ring.used, 1)

            body(0, True)
            with pe.Fori(1, KT) as n:
                body(n, False)

        @block.vector
        def _(dve):
            chain = Chain(dve, vec_done)
            nc.vector.nop().then_inc(gate_ready, 1)
            for i in range(KT // PIECE):
                dve.wait_ge(y_high_ready, i + 1)
                piece = slice(i * PIECE, (i + 1) * PIECE)
                nc.vector.tensor_tensor(y_low[:, piece], y_raw[:, i % 2], y_high[:, piece].bitcast(F32),
                                        ALU.subtract).then_inc(y_low_ready, 1)

            def body(n, first):
                dve.wait_ge(gate_tanh, n + 1)
                if not first:
                    dve.wait_ge(mixed_ready, n)
                nc.vector.tensor_scalar(gate[:], half_tanh[:], 1.0, 0.5, ALU.add, ALU.mult).then_inc(gate_ready, 1)
                dve.wait_ge(gate_ready, n + 2)
                dve.wait_ge(ring.used, ring.base + 2 * n + 4)
                if not first:
                    dve.wait_ge(stored, 16 * n)
                product_done = nc.vector.tensor_tensor(mixed[:], acc[1][:], gate[:], ALU.mult)
                if prior is None:
                    product_done.then_inc(mixed_ready, 1)
                else:
                    chain.after(product_done)
                    dve.wait_ge(before_landed, 16 * n + 16)
                    nc.vector.tensor_tensor(mixed[:], mixed[:], before[:], ALU.add).then_inc(mixed_ready, 1)

            body(0, True)
            with dve.Fori(1, KT) as n:
                chain.enter(n - 1, 0 if prior is None else 1)
                body(n, False)
    ring.base += 2 * KT



def out_stage(nc, dram, ring, m, mix, x_mid, mean, ones, following):
    with ExitStack() as ctx:
        sb = lambda n, s, dt=F32: ctx.enter_context(nc.sbuf_tensor(f"sb_out_{n}", s, dt))
        sem = ctx.enter_context(semaphores(nc, "out"))
        raw = sb("raw_mix", [P, 2, PIECE, T])
        m_high, m_low = m
        acc = [ctx.enter_context(nc.psum_tensor(f"out_acc{i}", [P, T], F32)) for i in range(2)]
        landed = [sem("mix_landed0"), sem("mix_landed1")]
        x_landed, m_high_ready, m_low_ready, added = (sem("x_landed"), sem("m_high_ready"),
                                                      sem("m_low_ready"), sem("added"))
        square = sb("square", [P, 2, T])
        squared = sem("squared")
        summed = sem("summed")
        w = dram["w_out"]
        block = ctx.enter_context(nc.Block())

        @block.sync
        def _(sp):
            for i in range(KT // PIECE):
                if i >= 2:
                    sp.wait_ge(m_low_ready, i - 1)
                sp.dma_start(raw[:, i % 2], mix[i * PIECE:(i + 1) * PIECE].rearrange("k p t -> p k t")
                             ).then_inc(landed[i % 2], 16)
            sp.dma_start(x_mid[:], dram["x_t"]).then_inc(x_landed, 16)
            with sp.Fori(1, KT // 2) as i:
                for s in range(2):
                    load_tile(sp, ring, s, one(w[ds(2 * i + s, 1)]), 2 * i + s)
            load_ahead(sp, ring, KT, following)

        @block.gpsimd
        def _(pool):
            split_low_all(nc, pool, ring, KT)

        @block.scalar
        def _(act):
            split_high(nc, act, ring, 1, 1, 0)
            for i in range(KT // PIECE):
                act.wait_ge(landed[i % 2], 16 * (i // 2) + 16)
                nc.scalar.activation(m_high[:, i * PIECE:(i + 1) * PIECE], raw[:, i % 2],
                                     ACT.Copy).then_inc(m_high_ready, 1)

            def square_of(n, slot):
                act.wait_ge(added, n + 3)
                act.wait_ge(summed, n + 1)
                nc.scalar.activation(square[:, slot], x_mid[:, ds(n, 1)].rearrange("p a t -> p (a t)"),
                                     ACT.Square).then_inc(squared, 1)

            split_high(nc, act, ring, 0, 2, 1)
            square_of(0, 0)
            with act.Fori(1, KT // 2) as i:
                for s in range(2):
                    split_high(nc, act, ring, 1 - s, 2 * i + (s + 1), i + s)
                    square_of(2 * i + (s - 1), 1 - s)
            square_of(KT - 1, 1)

        @block.tensor
        def _(pe):
            nc.tensor.nop().then_inc(summed, 2)

            def project(n, slot):
                pe.wait_ge(ring.low_ready, ring.base + n + 1)
                pe.wait_ge(added, n + 1)
                product(nc, acc[slot][:], ring.high[:, slot], ring.low[:, slot], m_high, m_low,
                        wait_piece=lambda j: pe.wait_ge(m_low_ready, j)).then_inc(ring.used, 1)

            def sum_squares(n, slot, start=False, stop=False):
                pe.wait_ge(squared, n + 1)
                nc.tensor.matmul(mean[:], ones, square[:, slot], start=start, stop=stop,
                                 skip_group_check=True).then_inc(summed, 1)

            project(0, 0)
            project(1, 1)
            sum_squares(0, 0, start=True)
            with pe.Fori(1, KT // 2) as i:
                for s in range(2):
                    project(2 * i + s, s)
                    sum_squares(2 * i + (s - 1), 1 - s)
            sum_squares(KT - 1, 1, stop=True)

        @block.vector
        def _(dve):
            nc.vector.nop().then_inc(added, 2)
            for i in range(KT // PIECE):
                dve.wait_ge(m_high_ready, i + 1)
                piece = slice(i * PIECE, (i + 1) * PIECE)
                nc.vector.tensor_tensor(m_low[:, piece], raw[:, i % 2], m_high[:, piece].bitcast(F32),
                                        ALU.subtract).then_inc(m_low_ready, 1)
            dve.wait_ge(x_landed, 16)
            with dve.Fori(0, KT // 2) as i:
                for s in range(2):
                    dve.wait_ge(ring.used, ring.base + 2 * i + (s + 3))
                    x = x_mid[:, ds(2 * i + s, 1)].rearrange("p a t -> p (a t)")
                    nc.vector.tensor_tensor(x, x, acc[s][:], ALU.add).then_inc(added, 1)
    ring.base += KT



class Staged:

    def __init__(self, ap, seen, done):
        self.ap, self.seen, self.done = ap, seen, done


def gather(nc, pool, rows, table, row_of, k, slot, staged):
    nc.gpsimd.tensor_copy(staged.ap[0:OWN, slot:slot + 1], row_of[0:OWN, ds(k, 1)]).then_inc(staged.done, 1)
    pool.wait_ge(staged.done, k + 1)
    nc.gpsimd.tensor_copy(staged.seen[0:OWN, ds(k, 1)], staged.ap[0:OWN, slot:slot + 1])
    return pool.indirect_dma_start(rows[0:OWN, slot], None, table,
                                   bass.IndirectOffsetOnAxis(ap=staged.ap[0:OWN, slot:slot + 1], axis=0))



def route_stage(nc, dram, ring, h, const, scratch, row_of, weight, following):
    with ExitStack() as ctx:
        sb = lambda n, s, dt=F32: ctx.enter_context(nc.sbuf_tensor(f"sb_rt_{n}", s, dt))
        ps = lambda n, s: ctx.enter_context(nc.psum_tensor(f"rt_{n}", s, F32))
        sem = ctx.enter_context(semaphores(nc, "rt"))
        QUERY = KT
        PAIRS = KEYS // 2
        GROUP = 4
        BANKS = 4
        BLOCK_TURNS = GT // GROUP // BANKS
        GATE_PAIRS = REST // GROUP // BANKS
        BLOCKS = REST // GT
        FREE_PAIRS = 16
        SLOTS = 3
        THREES = 32
        TWOS = PAIRS - FREE_PAIRS - THREES
        assert 3 * THREES + 2 * TWOS == HK and THREES >= GATE_PAIRS

        table = sb("table", [P, 2, KEYS, GT])
        hot1_high = sb("hot1_high", [P, 2, GROUP, KEYS], F32R)
        hot1_low = sb("hot1_low", [P, 2, GROUP, KEYS], F32R)
        hot2 = sb("hot2", [P, 2, GROUP, KEYS], F32R)
        place = sb("place", [P, 2, T])
        gate_high = sb("gate_high", [P, T], F32R)
        gate_low = sb("gate_low", [P, T])
        gelu = sb("gelu", [P, 2, REST])
        count = sb("count", [P, P])
        ident = sb("ident", [P, P], F32R)
        h_tok = sb("h_tok", [P, D])
        rows = sb("rows", [P, SLOTS, D])
        dot = sb("dot", [P, SLOTS])
        dots = sb("dots", [P, HK])
        staged = Staged(sb("staged", [P, SLOTS], U32), sb("seen", [P, HK], U32), sem("staged"))
        spare = table[:].rearrange("p b j t -> p (b j t)")
        at = [0]

        def carve(*shape):
            n = int(np.prod(shape))
            at[0] += n
            assert at[0] <= 2 * KEYS * GT
            names = "abcde"[:len(shape)]
            return spare[:, at[0] - n:at[0]].rearrange(
                f"p ({' '.join(names)}) -> p {' '.join(names)}", **dict(zip(names, shape)))

        keys = carve(KT, KEYS)
        query = carve(2, T)
        score = carve(2, NC, KEYS)
        top = carve(2, NC, TOPK)
        top_at = carve(2, NC, TOPK).bitcast(U32)
        top_key = carve(2, NC, TOPK)
        pair = carve(NC, TOPK, TOPK)
        best_at = carve(NC, TOPK).bitcast(U32)
        half_at = carve(NC, TOPK).bitcast(U32)
        half_pos = carve(NC, TOPK)
        hit = pair
        best = carve(NC, PEER_HEADS, TOPK)
        total = carve(NC, PEER_HEADS)
        chosen = carve(2, NC, PEER_HEADS, TOPK)

        acc = [ps(f"acc{i}", [P, T]) for i in range(2)]
        ps_score = [ps(f"score{i}", [P, NC, KEYS]) for i in range(2)]
        ps_gate = [ps(f"gate{i}", [P, T]) for i in range(BANKS)]

        acc_read = sem("acc_read")
        score_done = sem("score_done")
        score_read = sem("score_read")
        gelu_stored = [sem("gelu_stored0"), sem("gelu_stored1")]
        exp_in, exp_done, gates_ready, turned, vec_done = (
            sem(n) for n in ("exp_in", "exp_done", "gates_ready", "turned", "vec_done"))
        hot_ready = sem("hot_ready")
        made = sem("made")
        taken = sem("taken")
        table_stored = sem("table_stored")
        ident_ready, h_turned, h_taken = sem("ident_ready"), sem("h_turned"), sem("h_taken")
        own_ready = sem("own_ready")
        gathered = [sem(f"gathered{i}") for i in range(SLOTS)]
        dotted = sem("dotted")
        dot_kept = sem("dot_kept")
        own_gelu = sem("own_gelu")
        block = ctx.enter_context(nc.Block())

        @block.sync
        def _(sp):
            for half in range(2):
                a, b = slice(half * KT // 2, (half + 1) * KT // 2), slice(half * P // 2, (half + 1) * P // 2)
                sp.dma_start(keys[:, a], dram["sub_keys"][:, a]).then_inc(table_stored, 16)
                sp.dma_start(count[:, b], dram["count"][:, b]).then_inc(gelu_stored[half], 16)
            with sp.Fori(1, QUERY // 2) as i:
                for s in range(2):
                    load_tile(sp, ring, s, one(dram["w_query"][ds(2 * i + s, 1)]), 2 * i + s)
            for n in range(3):
                load_tile(sp, ring, n % 2, dram["u_tiles"][n], QUERY + n)

            def turn(i, loads=2):
                for s in range(2):
                    if s < loads:
                        load_tile(sp, ring, 1 - s, one(dram["u_tiles"][ds(2 * i + 3 + s, 1)]),
                                  2 * i + (QUERY + 3 + s))
                    sp.wait_ge(acc_read, 2 * i + (QUERY + s + 3))
                    sp.dma_start(one(scratch["gelu"][ds(2 * i + s, 1)]), gelu[:, s]).then_inc(gelu_stored[s], 16)

            with sp.Fori(0, FREE_PAIRS) as i:
                turn(i)

            def gate_block(blk, buf):
                with sp.Fori(0, BLOCK_TURNS) as j:
                    turn(blk * BLOCK_TURNS + j + FREE_PAIRS)
                sp.wait_ge(taken, blk * (GT // GROUP) + (GT // GROUP + BANKS))
                sp.dma_start(scratch["gates"][ds(blk, 1)].rearrange("b i j t -> (b i) j t"),
                             table[:, buf]).then_inc(table_stored, 16)

            with sp.Fori(0, BLOCKS // 2) as b2:
                for buf in range(2):
                    gate_block(2 * b2 + buf, buf)
            gate_block(BLOCKS - 1, 0)
            with sp.Fori(FREE_PAIRS + GATE_PAIRS, PAIRS - 2) as i:
                turn(i)
            turn(PAIRS - 2, 1)
            load_ahead(sp, ring, QUERY + KEYS, following)
            turn(PAIRS - 1, 0)
            sp.wait_ge(table_stored, 16 * (BLOCKS + 2))
            for s in range(2):
                sp.wait_ge(gelu_stored[s], 16 * (PAIRS + 1))

        @block.gpsimd
        def _(pool):
            def fetch(k, slot, back):
                pool.wait_ge(dotted, k + (1 + SLOTS - back))
                gather(nc, pool, rows, dram["u_rows"], row_of, k, slot, staged).then_inc(gathered[slot], 16)

            first = QUERY + 2 * FREE_PAIRS
            split_low_all(nc, pool, ring, first)
            pool.wait_ge(own_ready, 1)
            with pool.Fori(0, THREES) as i:
                split_low(nc, pool, ring, 1, 2 * i + (first + 1))
                fetch(3 * i, 0, 3)
                fetch(3 * i + 1, 1, 3)
                split_low(nc, pool, ring, 0, 2 * i + (first + 2))
                fetch(3 * i + 2, 2, 3)
            with pool.Fori(0, TWOS) as i:
                for s in range(2):
                    split_low(nc, pool, ring, 1 - s, 2 * i + (first + 2 * THREES + 1 + s))
                    fetch(2 * i + (3 * THREES + s), s, 2)

        @block.scalar
        def _(act):
            nc.scalar.activation(ident[:], const["ident"], ACT.Copy).then_inc(ident_ready, 1)
            with act.Fori(0, QUERY // 2) as i:
                for s in range(2):
                    split_high(nc, act, ring, 1 - s, 2 * i + (s + 1), i + s)
                    act.wait_ge(ring.used, ring.base + 2 * i + (s + 3))
                    act.wait_ge(score_done, 2 * i + (s + 1))
                    nc.scalar.activation(query[:, s], acc[s][:], ACT.Copy).then_inc(acc_read, 1)

            def activate(i, s):
                n = 2 * i + (QUERY + s)
                split_high(nc, act, ring, 1 - s, n + 1, i + (QUERY // 2 + s))
                act.wait_ge(ring.used, ring.base + n + 3)
                act.wait_ge(gelu_stored[s], 16 * i + 16)
                nc.scalar.activation(gelu[:, s], acc[s][:, 0:REST], ACT.Gelu).then_inc(acc_read, 1)

            with act.Fori(0, FREE_PAIRS - 2) as i:
                for s in range(2):
                    activate(i, s)
            act.wait_ge(exp_in, 1)
            nc.scalar.activation(best, best, ACT.Exp).then_inc(exp_done, 1)
            with act.Fori(FREE_PAIRS - 2, FREE_PAIRS) as i:
                for s in range(2):
                    activate(i, s)

            def gate_block(blk, buf):
                act.wait_ge(table_stored, 16 * blk + 16)
                with act.Fori(0, BLOCK_TURNS) as j:
                    i = blk * BLOCK_TURNS + j
                    for s in range(2):
                        activate(i + FREE_PAIRS, s)
                        for b in range(s * BANKS // 2, (s + 1) * BANKS // 2):
                            act.wait_ge(made, BANKS * i + (b + 1 + BANKS))
                            nc.scalar.activation(
                                table[:, buf, :, ds((j * BANKS + b) * GROUP, GROUP)].rearrange("p j t -> p t j"),
                                ps_gate[b][:].rearrange("p (t j) -> p t j", t=GROUP), ACT.Copy).then_inc(taken, 1)

            with act.Fori(0, BLOCKS // 2) as b2:
                for buf in range(2):
                    gate_block(2 * b2 + buf, buf)
            gate_block(BLOCKS - 1, 0)
            with act.Fori(FREE_PAIRS + GATE_PAIRS, PAIRS) as i:
                for s in range(2):
                    activate(i, s)
            act.wait_ge(dot_kept, HK + SLOTS)
            nc.scalar.activation(dots[0:OWN], dots[0:OWN], ACT.Gelu).then_inc(own_gelu, 1)

        @block.tensor
        def _(pe):
            nc.tensor.nop().then_inc(score_done, 2)
            pe.wait_ge(table_stored, 32)
            pe.wait_ge(ident_ready, 1)
            for k in range(KT):
                o = ps_gate[k // 4][0:OWN, k % 4 * P:(k % 4 + 1) * P]
                nc.tensor.matmul(o, h[0][:, k, 0:OWN], ident[:], start=True, stop=False)
                last = nc.tensor.matmul(o, h[1][:, k, 0:OWN], ident[:], start=False, stop=True)
            last.then_inc(h_turned, 1)

            def project(n, s, tokens=slice(OWN, T)):
                pe.wait_ge(ring.low_ready, ring.base + n + 1)
                pe.wait_ge(acc_read, n + 1)
                product(nc, acc[s][:, 0:tokens.stop - tokens.start], ring.high[:, s], ring.low[:, s], h[0], h[1],
                        tokens=tokens).then_inc(ring.used, 1)

            def match(n, s):
                pe.wait_ge(acc_read, n + 3)
                pe.wait_ge(score_read, n + 1)
                for c in range(NC):
                    last = nc.tensor.matmul(ps_score[s][:, c],
                                            query[:, s, c * P:(c + 1) * P],
                                            keys[:, ds(n, 1)].rearrange("p a k -> p (a k)"), start=True, stop=True)
                last.then_inc(score_done, 1)

            with pe.Fori(0, QUERY // 2) as i:
                project(2 * i, 0, slice(0, T))
                project(2 * i + 1, 1, slice(0, T))
                match(2 * i, 0)
                match(2 * i + 1, 1)
            with pe.Fori(0, FREE_PAIRS) as i:
                for s in range(2):
                    project(2 * i + (QUERY + s), s)
            pe.wait_ge(gates_ready, 1)
            for a, src in enumerate((chosen[:, 0], chosen[:, 1], best)):
                for c in range(NC):
                    last = nc.tensor.transpose(ps_gate[a][:, c * P:(c + 1) * P],
                                               src[:, c].rearrange("p h k -> p (h k)"), const["ident"])
            last.then_inc(turned, 1)
            with pe.Fori(0, GATE_PAIRS) as i:
                for s in range(2):
                    project(2 * i + (QUERY + 2 * FREE_PAIRS + s), s)
                    for b in range(s * BANKS // 2, (s + 1) * BANKS // 2):
                        pe.wait_ge(hot_ready, BANKS * i + (b + 1))
                        pe.wait_ge(taken, BANKS * i + (b + 1))
                        for g in range(GROUP):
                            o = ps_gate[b][:, g * KEYS:(g + 1) * KEYS]
                            nc.tensor.matmul(o, hot1_high[:, b % 2, g], hot2[:, b % 2, g], start=True, stop=False)
                            last = nc.tensor.matmul(o, hot1_low[:, b % 2, g], hot2[:, b % 2, g],
                                                    start=False, stop=True)
                        last.then_inc(made, 1)
            with pe.Fori(FREE_PAIRS + GATE_PAIRS, PAIRS) as i:
                for s in range(2):
                    project(2 * i + (QUERY + s), s)

        @block.vector
        def _(dve):
            vec = nc.vector
            chain = Chain(dve, vec_done)
            vec.nop().then_inc(acc_read, 2)
            vec.nop().then_inc(score_read, 2)
            vec.nop().then_inc(made, BANKS)
            vec.nop().then_inc(taken, BANKS)
            vec.nop().then_inc(dotted, SLOTS)
            vec.nop().then_inc(dot_kept, SLOTS)
            for s in range(2):
                dve.wait_ge(gelu_stored[s], 16)
            dve.wait_ge(h_turned, 1)
            for a in range(KT // 4):
                ins = vec.tensor_copy(h_tok[0:OWN, a * 4 * P:(a + 1) * 4 * P], ps_gate[a][0:OWN])
            ins.then_inc(h_taken, 1)

            def top_of(dst, dst_at, src):
                for j in range(0, TOPK, 8):
                    for c in range(NC):
                        ins = vec.max(dst(c)[:, j:j + 8], src(c))
                    chain.after(ins)
                    for c in range(NC):
                        ins = vec.max_index(dst_at(c)[:, j:j + 8], dst(c)[:, j:j + 8], src(c))
                    chain.after(ins)
                    if j + 8 < TOPK:
                        for c in range(NC):
                            ins = vec.match_replace(src(c), dst(c)[:, j:j + 8], src(c), NEG)
                        chain.after(ins)

            for head in range(PEER_HEADS):
                for s in range(2):
                    dve.wait_ge(score_done, 2 * head + s + 3)
                    vec.tensor_copy(score[:, s], ps_score[s][:]).then_inc(score_read, 1)
                    dve.wait_ge(score_read, 2 * head + s + 3)
                    top_of(lambda c: top[:, s, c], lambda c: top_at[:, s, c], lambda c: score[:, s, c])
                chain.after(vec.tensor_copy(top_key, top_at))
                full = [P, NC, TOPK, TOPK]
                chain.after(vec.tensor_tensor(pair, top[:, 0].unsqueeze(3).to_broadcast(full),
                                              top[:, 1].unsqueeze(2).to_broadcast(full), ALU.add))
                top_of(lambda c: best[:, c, head], lambda c: best_at[:, c],
                       lambda c: pair[:, c].rearrange("p a b -> p (a b)"))
                for half, (op, by) in enumerate(((ALU.logical_shift_right, 4), (ALU.bitwise_and, TOPK - 1))):
                    chain.after(vec.tensor_scalar(half_at, best_at, by, None, op))
                    chain.after(vec.tensor_copy(half_pos, half_at))
                    chain.after(vec.tensor_tensor(
                        hit, half_pos.unsqueeze(3).to_broadcast(full),
                        count[:, 0:TOPK].unsqueeze(1).unsqueeze(1).to_broadcast(full), ALU.is_equal))
                    chain.after(vec.tensor_tensor(hit, hit, top_key[:, half].unsqueeze(2).to_broadcast(full),
                                                  ALU.mult))
                    chain.after(vec.tensor_reduce(chosen[:, half, :, head], hit, AX_X, ALU.add))
            flat = best.rearrange("p c h k -> p (c h) k")
            of_rows = total.rearrange("p c h -> p (c h)").unsqueeze(2).to_broadcast([P, NC * PEER_HEADS, TOPK])
            chain.after(vec.tensor_copy(total, best[:, :, :, 0]))
            vec.tensor_tensor(flat, flat, of_rows, ALU.subtract).then_inc(exp_in, 1)
            dve.wait_ge(exp_done, 1)
            chain.after(vec.tensor_reduce(total, best, AX_X, ALU.add))
            chain.after(vec.reciprocal(total, total))
            vec.tensor_tensor(flat, flat, of_rows, ALU.mult).then_inc(gates_ready, 1)
            first_at = [chosen[0:OWN, half, 0].rearrange("p h k -> p (h k)") for half in range(2)]
            chain.after(vec.scalar_tensor_tensor(dots[0:OWN], first_at[1], float(KEYS), first_at[0],
                                                 ALU.mult, ALU.add))
            vec.tensor_copy(row_of[0:OWN], dots[0:OWN]).then_inc(own_ready, 1)
            dve.wait_ge(gates_ready, 1)
            chain.after(vec.tensor_copy(weight[0:OWN], best[0:OWN, 0].rearrange("p h k -> p (h k)")))
            dve.wait_ge(turned, 1)
            vec.tensor_copy(place[:, 0], ps_gate[0][:])
            vec.tensor_copy(place[:, 1], ps_gate[1][:])
            chain.after(vec.tensor_copy(gate_high[:], ps_gate[2][:]))
            chain.after(vec.tensor_tensor(gate_low[:], ps_gate[2][:], gate_high[:].bitcast(F32), ALU.subtract))

            def take_dot(k, slot, turn):
                dve.wait_ge(gathered[slot], 16 * turn + 16)
                dve.wait_ge(dot_kept, k + 1)
                vec.tensor_tensor_reduce(rows[0:OWN, slot], rows[0:OWN, slot], h_tok[0:OWN], 1.0, 0.0,
                                         ALU.mult, ALU.add, dot[0:OWN, slot:slot + 1]).then_inc(dotted, 1)
                dve.wait_ge(dotted, k + (1 + SLOTS))
                vec.tensor_copy(dots[0:OWN, ds(k, 1)], dot[0:OWN, slot:slot + 1]).then_inc(dot_kept, 1)

            def hot_rows(i, b):
                dve.wait_ge(made, BANKS * i + (b + 3))
                for g in range(GROUP):
                    t = (i * BANKS + b) * GROUP + (OWN + g)
                    for hot1, gate in ((hot1_high, gate_high[:].bitcast(F32)), (hot1_low, gate_low[:])):
                        vec.tensor_scalar(hot1[:, b % 2, g], count[:], place[:, 0, ds(t, 1)],
                                          gate[:, ds(t, 1)], ALU.is_equal, ALU.mult)
                    ins = vec.tensor_scalar(hot2[:, b % 2, g], count[:], place[:, 1, ds(t, 1)], None,
                                            ALU.is_equal)
                ins.then_inc(hot_ready, 1)

            for b in range(BANKS):
                hot_rows(0, b)
            with dve.Fori(1, GATE_PAIRS) as i:
                hot_rows(i, 0)
                hot_rows(i, 1)
                take_dot(3 * i - 3, 0, i - 1)
                take_dot(3 * i - 2, 1, i - 1)
                hot_rows(i, 2)
                hot_rows(i, 3)
                take_dot(3 * i - 1, 2, i - 1)
            with dve.Fori(GATE_PAIRS - 1, THREES) as i:
                for slot in range(3):
                    take_dot(3 * i + slot, slot, i)
            with dve.Fori(0, TWOS) as i:
                for slot in range(2):
                    take_dot(2 * i + (3 * THREES + slot), slot, i + THREES)
            dve.wait_ge(own_gelu, 1)
            vec.tensor_tensor(weight[0:OWN], weight[0:OWN], dots[0:OWN], ALU.mult)
    ring.base += QUERY + KEYS



def output_stage(nc, dram, ring, x_mid, const, scratch, row_of, weight):
    with ExitStack() as ctx:
        sb = lambda n, s, dt=F32: ctx.enter_context(nc.sbuf_tensor(f"sb_op_{n}", s, dt))
        sem = ctx.enter_context(semaphores(nc, "op"))
        N = KEYS // 2
        OUTS = 8
        more_high, more_low = sb("more_high", [P, 2, D], F32R), sb("more_low", [P, 2, D], F32R)
        v_high = [ring.high[:, 0], ring.high[:, 1], more_high[:, 0], more_high[:, 1]]
        v_low = [ring.low[:, 0], ring.low[:, 1], more_low[:, 0], more_low[:, 1]]
        gelu, gate = sb("gelu", [P, 4, REST]), sb("gate", [P, REST // GT, 4, GT])
        w = sb("w", [P, 2, REST])
        w_high, w_low = sb("w_high", [P, 4, REST], F32R), sb("w_low", [P, 4, REST], F32R)
        rows = sb("rows", [P, 4, D])
        total = sb("total", [P, D])
        staged = Staged(sb("staged", [P, 4], U32), sb("seen", [P, HK], U32), sem("staged"))
        ps_out = [ctx.enter_context(nc.psum_tensor(f"op_out{i}", [P, T], F32)) for i in range(OUTS)]
        x_landed, in_landed = sem("x_landed"), sem("in_landed")
        weighted = sem("weighted")
        w_split = sem("w_split")
        w_ready = sem("w_ready")
        pair_done = sem("pair_done")
        out_done = sem("out_done")
        out_added = sem("out_added")
        gathered = [sem(f"gathered{i}") for i in range(4)]
        summed = sem("summed")
        total_turned = sem("total_turned")
        block = ctx.enter_context(nc.Block())

        @block.sync
        def _(sp):
            def inputs(g2):
                sp.dma_start(gelu[:], scratch["gelu"][ds(4 * g2, 4)].rearrange("a p t -> p a t")
                             ).then_inc(in_landed, 16)
                sp.dma_start(gate[:], scratch["gates"][:, :, ds(4 * g2, 4)].rearrange("b i j t -> i b j t")
                             ).then_inc(in_landed, 16)

            inputs(0)
            for s in range(2, 4):
                load_tile(sp, ring, s % 2, dram["v_tiles"][s], s)
            sp.dma_start(x_mid[:], scratch["x_mid"]).then_inc(x_landed, 16)
            with sp.Fori(1, N // 2) as g2:
                sp.wait_ge(weighted, 2 * g2)
                inputs(g2)
                for s in range(4):
                    load_tile(sp, ring, s % 2, one(dram["v_tiles"][ds(4 * g2 + s, 1)]), 4 * g2 + s)

        @block.gpsimd
        def _(pool):
            def low(n, slot):
                pool.wait_ge(ring.high_ready, ring.base + n + 1)
                nc.gpsimd.tensor_tensor(v_low[slot], ring.raw[:, slot % 2], v_high[slot].bitcast(F32),
                                        ALU.subtract).then_inc(ring.low_ready, 1)

            def fetch(g2, s):
                pool.wait_ge(summed, 4 * g2 + (s + 1))
                gather(nc, pool, rows, dram["v_rows"], row_of, 4 * g2 + s, s, staged).then_inc(gathered[s], 16)

            def body(g2, last):
                for s in range(4):
                    if s < 3 or not last:
                        low(4 * g2 + (s + 1), (s + 1) % 4)
                    fetch(g2, s)

            with pool.Fori(0, N // 2 - 1) as g2:
                body(g2, False)
            body(N // 2 - 1, True)

        @block.scalar
        def _(act):
            def high(g2, s):
                act.wait_ge(ring.landed[s % 2], 32 * g2 + (8 * ring.base + 16 * (s // 2) + 16))
                if s % 2 == 0:
                    act.wait_ge(pair_done, 2 * g2 + (s // 2 + 1))
                nc.scalar.activation(v_high[s], ring.raw[:, s % 2], ACT.Copy).then_inc(ring.high_ready, 1)

            with act.Fori(0, N // 2 - 1) as g2:
                for s in (1, 2, 3):
                    high(g2, s)
                high(g2 + 1, 0)
            for s in (1, 2, 3):
                high(N // 2 - 1, s)

        @block.tensor
        def _(pe):
            nc.tensor.nop().then_inc(pair_done, 2)
            with pe.Fori(0, N // 2) as g2:
                for q in range(2):
                    pe.wait_ge(ring.low_ready, ring.base + 4 * g2 + (2 * q + 2))
                    pe.wait_ge(w_ready, 2 * g2 + (q + 1))
                    for d in range(KT):
                        pe.wait_ge(out_added, 2 * KT * g2 + (KT * q + d + 1))
                        o, m = ps_out[d % OUTS][:, 0:REST], slice(d * P, (d + 1) * P)
                        for s in (2 * q, 2 * q + 1):
                            nc.tensor.matmul(o, v_high[s][:, m], w_high[:, s], start=(s == 2 * q), stop=False)
                            nc.tensor.matmul(o, v_high[s][:, m], w_low[:, s], start=False, stop=False)
                            last = nc.tensor.matmul(o, v_low[s][:, m], w_high[:, s], start=False,
                                                    stop=(s == 2 * q + 1))
                        last.then_inc(out_done if d < KT - 1 else pair_done, 1)
            pe.wait_ge(out_added, KT * N + OUTS)
            pe.wait_ge(summed, HK + 4)
            for d in range(KT):
                last = nc.tensor.transpose(ps_out[d // 4][:, d % 4 * OWN:(d % 4 + 1) * OWN],
                                           total[0:OWN, d * P:(d + 1) * P], const["ident"][0:OWN, 0:OWN])
            last.then_inc(total_turned, 1)

        @block.vector
        def _(dve):
            vec = nc.vector
            vec.nop().then_inc(out_added, OUTS)
            vec.memset(total[:], 0.0).then_inc(summed, 4)

            def add_rows(k, slot, turn):
                dve.wait_ge(gathered[slot], 16 * turn + 16)
                dve.wait_ge(summed, k + 4)
                vec.scalar_tensor_tensor(total[0:OWN], rows[0:OWN, slot], weight[0:OWN, ds(k, 1)], total[0:OWN],
                                         ALU.mult, ALU.add).then_inc(summed, 1)

            def weights(g2, q):
                g = 2 * g2 + q
                two = slice(2 * q, 2 * q + 2)
                dve.wait_ge(in_landed, 32 * g2 + 32)
                vec.tensor_tensor(*(a.rearrange("p j (b t) -> p j b t", t=GT) for a in (w[:], gelu[:, two])),
                                  gate[:, :, two].rearrange("p b j t -> p j b t"), ALU.mult).then_inc(weighted, 1)
                dve.wait_ge(weighted, g + 1)
                vec.tensor_copy(w_high[:, two], w[:]).then_inc(w_split, 1)
                dve.wait_ge(w_split, g + 1)
                vec.tensor_tensor(w_low[:, two], w[:], w_high[:, two].bitcast(F32), ALU.subtract).then_inc(w_ready, 1)
                dve.wait_ge(w_ready, g + 1)

            def add_outputs(g2, q):
                g = 2 * g2 + q
                for d in range(KT):
                    if d % 8 == 5:
                        add_rows(2 * g + d // 8, 2 * q + d // 8, g2)
                    if d < KT - 1:
                        dve.wait_ge(out_done, (KT - 1) * g + (d + 1))
                    else:
                        dve.wait_ge(pair_done, g + 3)
                    x = x_mid[:, d, OWN:T]
                    vec.tensor_tensor(x, x, ps_out[d % OUTS][:, 0:REST], ALU.add).then_inc(out_added, 1)

            weights(0, 0)
            weights(0, 1)
            dve.wait_ge(x_landed, 16)
            with dve.Fori(0, N // 2 - 1) as g2:
                for q in range(2):
                    add_outputs(g2, q)
                    weights(g2 + 1, q)
            for q in range(2):
                add_outputs(N // 2 - 1, q)
            dve.wait_ge(total_turned, 1)
            for a in range(KT // 4):
                x = x_mid[:, 4 * a:4 * a + 4, 0:OWN]
                vec.tensor_tensor(x, x, ps_out[a][:, 0:4 * OWN].rearrange("p (d t) -> p d t", d=4), ALU.add)


def peer_front(nc, dram, ring, h, const, vecs, mix, scratch, row_of, weight):
    with ExitStack() as tmp:
        x_mid = tmp.enter_context(nc.sbuf_tensor("x_mid_front", [P, KT, T], F32))
        mean = tmp.enter_context(nc.psum_tensor("mean_of_squares", [P, T], F32))
        out_stage(nc, dram, ring, h, mix, x_mid, mean, const["ones"], dram["w_query"])
        work = tmp.enter_context(nc.sbuf_tensor("ffn_work", [P, KT, T], F32))
        norm_stage(nc, "ffn", x_mid, vecs["norm_ffn_w"], work, const["ones"], const["eps"], split=h,
                   keep=scratch["x_mid"], mean=mean)
    route_stage(nc, dram, ring, h, const, scratch, row_of, weight, dram["v_tiles"])


def peer_back(nc, dram, ring, const, vecs, scratch, row_of, weight, out):
    with ExitStack() as ctx:
        x_mid = ctx.enter_context(nc.sbuf_tensor("x_mid_back", [P, KT, T], F32))
        output_stage(nc, dram, ring, x_mid, const, scratch, row_of, weight)
        work = ctx.enter_context(nc.sbuf_tensor("final_work", [P, KT, T], F32))
        norm_stage(nc, "final", x_mid, vecs["final_norm_w"], work, const["ones"], const["eps"], store=out)



SHAPES = {
    "x_t": [P, KT, T], "norm_mix_w": [P, KT], "norm_ffn_w": [P, KT], "final_norm_w": [P, KT],
    "w_ssd": [SSD_GROUPS * SSD_TILES, P, D], "w_dt": [P, KT, SSD_HEADS],
    "w_hg": [HG_HEADS * HG_TILES, P, D],
    "w_mix_s": [2 * KT, P, D], "w_mix_h": [2 * KT, P, D], "w_out": [KT, P, D], "w_query": [KT, P, D],
    "u_tiles": [KEYS, P, D], "v_tiles": [KEYS, P, D],
    "u_rows": [KEYS * KEYS, D],
    "conv_w": [P, SSD_GROUPS * 4 * (CONV + 1)], "dt_bias": [P, SSD_HEADS], "a_log": [P, SSD_HEADS],
    "ssd_d": [P, KT], "ssd_norm_w": [P, KT], "hg_lb": [P, 2, KT], "hg_norm_w": [P, 1],
    "sub_keys": [P, KT, KEYS],
    "ident": [P, P], "ones": [P, P], "later": [P, P], "upto": [P, P], "level_mask": [P, LEVELS + 1, P],
    "count": [P, P],
}


def program(nc):
    dram = {n: nc.dram_tensor(n, s, F32, kind="ExternalInput").ap() for n, s in SHAPES.items()}
    out = nc.dram_tensor("out_t", [P, KT, T], F32, kind="ExternalOutput").ap()
    y_ssd = nc.dram_tensor("y_ssd", [KT, P, T], F32).ap()
    y_hg = nc.dram_tensor("y_hg", [KT, P, T], F32).ap()
    mix_s = nc.dram_tensor("mix_s", [KT, P, T], F32).ap()
    mix = nc.dram_tensor("mix", [KT, P, T], F32).ap()
    scratch = {n: nc.dram_tensor(n, s, F32).ap() for n, s in (
        ("gates", [REST // GT, P, KEYS, GT]), ("gelu", [KEYS, P, REST]), ("x_mid", [P, KT, T]))}
    with ExitStack() as ctx:
        sb = lambda n, s, dt=F32: ctx.enter_context(nc.sbuf_tensor(n, s, dt))
        const, eps, vecs = load_constants(nc, ctx, dram)
        row_of, weight = sb("row_of", [P, HK], U32), sb("own_weight", [P, HK])
        dram["v_rows"] = dram["v_tiles"].rearrange("a p n -> (a p) n")
        with ExitStack() as rings:
            ring = Ring(nc, rings)
            with ExitStack() as products:
                h = [products.enter_context(nc.sbuf_tensor(f"h_{n}", [P, KT, T], F32R)) for n in ("high", "low")]
                with ExitStack() as tmp:
                    x = tmp.enter_context(nc.sbuf_tensor("x", [P, KT, T], F32))
                    work = tmp.enter_context(nc.sbuf_tensor("x_work", [P, KT, T], F32))
                    norm_stage(nc, "in", x, vecs["norm_mix_w"], work, const["ones"], const["eps"],
                               load=dram["x_t"], split=h, ring=ring, first_tiles=dram["w_ssd"])
                ssd_stage(nc, dram, ring, h, const, y_ssd, dram["w_hg"])
                hg_stage(nc, dram, ring, h, const, y_hg, dram["w_mix_s"])
                mix_stage(nc, "mix_s", dram["w_mix_s"], ring, h, y_ssd, None, mix_s, dram["w_mix_h"])
                mix_stage(nc, "mix_h", dram["w_mix_h"], ring, h, y_hg, mix_s, mix, dram["w_out"])
                peer_front(nc, dram, ring, h, const, vecs, mix, scratch, row_of[:], weight[:])
            peer_back(nc, dram, ring, const, vecs, scratch, row_of[:], weight[:], out)


def load_constants(nc, ctx, dram):
    sb = lambda n, s: ctx.enter_context(nc.sbuf_tensor(n, s, F32))
    shared = {n: sb(f"c_{n}", SHAPES[n]) for n in ("ident", "ones", "later", "upto", "norm_mix_w",
                                                   "norm_ffn_w", "final_norm_w")}
    eps = sb("c_eps", [P, 1])
    landed = ctx.enter_context(nc.semaphore("c_landed"))
    with nc.Block() as block:
        @block.sync
        def _(sp):
            for n, t in shared.items():
                sp.dma_start(t[:], dram[n]).then_inc(landed, 16)
            sp.wait_ge(landed, 16 * len(shared))

        @block.vector
        def _(dve):
            nc.vector.memset(eps[:], EPS)
    const = {n: shared[n][:] for n in ("ident", "ones", "later", "upto")}
    const["eps"] = eps[:]
    return const, eps, {n: shared[n] for n in ("norm_mix_w", "norm_ffn_w", "final_norm_w")}


def tiles_of(w):
    n = w.shape[1] // P
    return w.reshape(KT, P, n, P).transpose(2, 1, 0, 3).reshape(n, P, D)


def columns(v):
    return v.reshape(KT, P).T


def laid_out(inp):
    a = {k: np.asarray(v) for k, v in inp.items()}
    r = {}
    r["x_t"] = a["x"][0].T.reshape(KT, P, T).transpose(1, 0, 2)
    for n in ("norm_mix_w", "norm_ffn_w", "ssd_norm_w"):
        r[n] = columns(a[n][0])
    r["final_norm_w"] = columns(a["final_norm_w"])
    w = a["w_in"][0]
    sizes = (D, D + 2 * SSD_GROUPS * P, SSD_HEADS, D, D, D, D, D, D)
    z, xbc, wdt, hq, hf, hi, hg, gs, gh = np.split(w, np.cumsum(sizes)[:-1], axis=1)
    z, xbc, hq, hf, hi, hg, gs, gh = (tiles_of(m) for m in (z, xbc, hq, hf, hi, hg, gs, gh))
    order = [i for g in range(SSD_GROUPS) for i in (2 * g, 2 * g + 1, KT + g, KT + SSD_GROUPS + g)]
    per_group = xbc[order].reshape(SSD_GROUPS, 4, P, D)
    r["w_ssd"] = np.concatenate([per_group, z.reshape(SSD_GROUPS, 2, P, D)], 1).reshape(-1, P, D)
    r["w_dt"] = wdt.reshape(KT, P, SSD_HEADS).transpose(1, 0, 2)
    r["w_hg"] = np.stack([hf, hq, hi, hg], 1).reshape(-1, P, D)
    r["w_mix_s"] = np.stack([gs, tiles_of(a["w_ssd_br"][0])], 1).reshape(-1, P, D)
    r["w_mix_h"] = np.stack([gh, tiles_of(a["w_hg_br"][0])], 1).reshape(-1, P, D)
    r["w_out"] = tiles_of(a["w_out"][0])
    r["w_query"] = tiles_of(a["peer_w_q"][0])
    r["u_tiles"] = a["peer_u"][0].reshape(KEYS, KEYS, KT, P).transpose(1, 3, 2, 0).reshape(KEYS, P, D)
    r["u_rows"] = a["peer_u"][0].reshape(KEYS, KEYS, D).transpose(1, 0, 2).reshape(KEYS * KEYS, D)
    r["v_tiles"] = a["peer_v"][0].reshape(KEYS, KEYS, D).transpose(1, 0, 2)
    cw = np.concatenate([a["ssd_conv_w"][0], a["ssd_conv_b"][0][None]], 0)
    r["conv_w"] = cw.reshape(CONV + 1, -1, P)[:, order].transpose(2, 1, 0).reshape(P, -1)
    r["dt_bias"] = np.broadcast_to(a["ssd_dt_bias"][0], (P, SSD_HEADS))
    r["a_log"] = np.broadcast_to(a["ssd_a_log"][0], (P, SSD_HEADS))
    r["ssd_d"] = columns(np.repeat(a["ssd_d"][0], HD))
    r["hg_lb"] = a["hg_lb"].reshape(2, KT, P).transpose(2, 0, 1)
    r["hg_norm_w"] = a["hg_norm_w"][0][:, None]
    r["sub_keys"] = a["peer_sub_keys"][0].reshape(KT, KEYS, P).transpose(2, 0, 1)
    i = np.arange(P)
    r["ident"] = np.eye(P, dtype=np.float32)
    r["ones"] = np.ones((P, P), np.float32)
    r["later"] = (i[:, None] > i[None]).astype(np.float32)
    r["upto"] = (i[:, None] <= i[None]).astype(np.float32)
    s, t = i[:, None], i[None]
    levels = [(s // (2 * w) == t // (2 * w)) & (s // w % 2 == 0) & (t // w % 2 == 1) for w in HALVES]
    r["level_mask"] = np.stack(levels + [s == t], 1).astype(np.float32)
    r["count"] = np.broadcast_to(i.astype(np.float32), (P, P))
    return {n: np.ascontiguousarray(r[n]) for n in SHAPES}


def kernel(**inputs):
    import concourse.bacc as bacc
    from concourse.bass_utils import run_bass_kernel_spmd

    nc = bacc.Bacc("TRN2", target_bir_lowering=False, num_devices=1)
    program(nc)
    got = run_bass_kernel_spmd(nc, [laid_out(inputs)], core_ids=[0]).results[0]["out_t"]
    return np.ascontiguousarray(got.transpose(1, 0, 2).reshape(D, T).T)[None]
```
